# Optimizing a Trainium2 kernel written in Bass

```python
import math
import jax, jax.numpy as jnp
from jax import lax
import numpy as np

D_MODEL = 1024
BATCH = 1
SEQ = 256
DEPTH = 2

CHUNK = 64
N_A_LAYERS = DEPTH // 2
N_B_LAYERS = DEPTH - N_A_LAYERS
N_DENSE_FFN = (DEPTH + 1) // 2
N_MOE_FFN = DEPTH // 2
DEEPNORM_ALPHA = (2.0 * DEPTH) ** 0.25
DEEPNORM_BETA = (8.0 * DEPTH) ** -0.25
LN_EPS = 1e-5

RET_HEADS = 4
RET_QK_DIM = D_MODEL // RET_HEADS
RET_V_WIDTH = 2 * D_MODEL
RET_V_DIM = RET_V_WIDTH // RET_HEADS
RET_IN_WIDTH = 2 * D_MODEL + 2 * RET_V_WIDTH
ROPE_BASE = 10000.0

SB_HEADS = 16
SB_HEAD_DIM = D_MODEL // SB_HEADS
SB_QBLOCK = 128

D_FF = 2816
N_EXPERTS = 8
TOP_K = 2
D_EXPERT = 3584


def layer_norm(x, g, b):
    xf = x.astype(jnp.float32)
    mu = jnp.mean(xf, axis=-1, keepdims=True)
    var = jnp.mean(jnp.square(xf - mu), axis=-1, keepdims=True)
    y = (xf - mu) * lax.rsqrt(var + LN_EPS) * g.astype(jnp.float32) + b.astype(jnp.float32)
    return y.astype(x.dtype)

def rotary(x):
    s, d = x.shape[-2], x.shape[-1]
    inv_freq = 1.0 / (ROPE_BASE ** (jnp.arange(0, d, 2, dtype=jnp.float32) / d))
    ang = jnp.arange(s, dtype=jnp.float32)[:, None] * inv_freq[None, :]
    cos, sin = jnp.cos(ang).astype(x.dtype), jnp.sin(ang).astype(x.dtype)
    x1, x2 = x[..., : d // 2], x[..., d // 2:]
    return jnp.concatenate([x1 * cos - x2 * sin, x1 * sin + x2 * cos], axis=-1)

def retention_mixer(x, w_in, w_out):
    b, s, _ = x.shape
    nc = s // CHUNK
    dt = x.dtype
    proj = x @ w_in
    q, k, v, g = jnp.split(proj, [D_MODEL, 2 * D_MODEL, 2 * D_MODEL + RET_V_WIDTH], axis=-1)
    q = q.reshape(b, s, RET_HEADS, RET_QK_DIM).transpose(0, 2, 1, 3)
    k = k.reshape(b, s, RET_HEADS, RET_QK_DIM).transpose(0, 2, 1, 3) * (RET_QK_DIM ** -0.5)
    v = v.reshape(b, s, RET_HEADS, RET_V_DIM).transpose(0, 2, 1, 3)
    q, k = rotary(q), rotary(k)
    log_g = jnp.log(1.0 - 2.0 ** (-5.0 - jnp.arange(RET_HEADS, dtype=jnp.float32)))
    idx = jnp.arange(CHUNK, dtype=jnp.float32)
    intra_decay = jnp.exp(log_g[:, None, None] * jnp.abs(idx[:, None] - idx[None, :])).astype(dt)
    q_decay = jnp.exp(log_g[:, None] * (idx + 1.0))[..., None].astype(dt)
    k_decay = jnp.exp(log_g[:, None] * (CHUNK - 1.0 - idx))[..., None].astype(dt)
    chunk_decay = jnp.exp(log_g * CHUNK)[:, None, None].astype(dt)

    def to_chunks(t):
        return t.reshape(b, RET_HEADS, nc, CHUNK, t.shape[-1]).transpose(2, 0, 1, 3, 4)

    def step(state, inp):
        qi, ki, vi = inp
        scores = jnp.einsum('bhnd,bhmd->bhnm', qi, ki) * intra_decay
        out = (jnp.einsum('bhnm,bhme->bhne', scores, vi)
               + jnp.einsum('bhnd,bhde->bhne', qi * q_decay, state))
        state = state * chunk_decay + jnp.einsum('bhmd,bhme->bhde', ki * k_decay, vi)
        return state, out

    state0 = jnp.zeros((b, RET_HEADS, RET_QK_DIM, RET_V_DIM), dt)
    _, oc = lax.scan(step, state0, (to_chunks(q), to_chunks(k), to_chunks(v)))
    o = oc.transpose(1, 0, 3, 2, 4).reshape(b, s, RET_HEADS, RET_V_DIM)
    of = o.astype(jnp.float32)
    mu = jnp.mean(of, axis=-1, keepdims=True)
    var = jnp.mean(jnp.square(of - mu), axis=-1, keepdims=True)
    o = ((of - mu) * lax.rsqrt(var + LN_EPS)).astype(dt).reshape(b, s, RET_V_WIDTH)
    return (jax.nn.silu(g) * o) @ w_out

def shared_kv(x, w_kv):
    b, s, _ = x.shape
    kv = x @ w_kv
    k, v = jnp.split(kv, 2, axis=-1)
    k = k.reshape(b, s, SB_HEADS, SB_HEAD_DIM).transpose(0, 2, 1, 3)
    v = v.reshape(b, s, SB_HEADS, SB_HEAD_DIM).transpose(0, 2, 1, 3)
    return k, v

def stick_breaking_mixer(x, k, v, w_q, w_out):
    b, s, _ = x.shape
    scale = SB_HEAD_DIM ** -0.5
    q = (x @ w_q).reshape(b, s, SB_HEADS, SB_HEAD_DIM).transpose(0, 2, 1, 3)
    outs = []
    for start in range(0, s, SB_QBLOCK):
        end = start + SB_QBLOCK
        qb = q[:, :, start:end]
        kb, vb = k[:, :, :end], v[:, :, :end]
        z = jnp.einsum('bhtd,bhsd->bhts', qb, kb).astype(jnp.float32) * scale
        causal = jnp.arange(end)[None, :] < jnp.arange(start, end)[:, None]
        log_keep = jnp.where(causal, jax.nn.log_sigmoid(-z), 0.0)
        between = lax.cumsum(log_keep, axis=3, reverse=True) - log_keep
        w = jnp.where(causal, jnp.exp(jax.nn.log_sigmoid(z) + between), 0.0)
        outs.append(jnp.einsum('bhts,bhsd->bhtd', w.astype(vb.dtype), vb))
    o = jnp.concatenate(outs, axis=2).transpose(0, 2, 1, 3).reshape(b, s, D_MODEL)
    return o @ w_out

def swiglu(x, w_in, w_out):
    gate, up = jnp.split(x @ w_in, 2, axis=-1)
    return (jax.nn.silu(gate) * up) @ w_out

def moe_swiglu(x, w_router, w_in, w_out):
    b, s, d = x.shape
    xt = x.reshape(b * s, d)
    logits = (xt @ w_router).astype(jnp.float32)
    top_val, top_idx = lax.top_k(logits, TOP_K)
    top_w = jax.nn.softmax(top_val, axis=-1)
    gates = jnp.sum(jax.nn.one_hot(top_idx, N_EXPERTS, dtype=jnp.float32) * top_w[..., None], axis=1)
    gates = gates.astype(x.dtype)
    y = jnp.zeros_like(xt)
    for e in range(N_EXPERTS):
        y = y + gates[:, e:e + 1] * swiglu(xt, w_in[e], w_out[e])
    return y.reshape(b, s, d)

def first_inputs(seed: int = 0) -> dict:
    key = jax.random.key(seed)
    ks = jax.random.split(key, 20)
    f32 = jnp.float32
    beta = DEEPNORM_BETA

    def nrm(k, shape, fan_in, gain=1.0):
        return jax.random.normal(k, shape, f32) * (fan_in ** -0.5) * gain

    x = jax.random.normal(ks[0], (BATCH, SEQ, D_MODEL), f32)
    ret_w_in = jnp.concatenate([
        nrm(ks[1], (N_A_LAYERS, D_MODEL, 2 * D_MODEL), D_MODEL),
        nrm(ks[2], (N_A_LAYERS, D_MODEL, RET_V_WIDTH), D_MODEL, beta),
        nrm(ks[3], (N_A_LAYERS, D_MODEL, RET_V_WIDTH), D_MODEL),
    ], axis=-1)
    ret_w_out = nrm(ks[4], (N_A_LAYERS, RET_V_WIDTH, D_MODEL), RET_V_WIDTH, beta)
    sb_w_kv = jnp.concatenate([
        nrm(ks[5], (D_MODEL, D_MODEL), D_MODEL),
        nrm(ks[6], (D_MODEL, D_MODEL), D_MODEL, beta),
    ], axis=-1)
    sb_w_q = nrm(ks[7], (N_B_LAYERS, D_MODEL, D_MODEL), D_MODEL)
    sb_w_out = nrm(ks[8], (N_B_LAYERS, D_MODEL, D_MODEL), D_MODEL, beta)
    ln_mix_g = 1.0 + 0.02 * jax.random.normal(ks[9], (DEPTH, D_MODEL), f32)
    ln_mix_b = 0.02 * jax.random.normal(ks[10], (DEPTH, D_MODEL), f32)
    ln_ffn_g = 1.0 + 0.02 * jax.random.normal(ks[11], (DEPTH, D_MODEL), f32)
    ln_ffn_b = 0.02 * jax.random.normal(ks[12], (DEPTH, D_MODEL), f32)
    ffn_w_in = nrm(ks[13], (N_DENSE_FFN, D_MODEL, 2 * D_FF), D_MODEL, beta)
    ffn_w_out = nrm(ks[14], (N_DENSE_FFN, D_FF, D_MODEL), D_FF, beta)
    moe_w_router = nrm(ks[15], (N_MOE_FFN, D_MODEL, N_EXPERTS), D_MODEL)
    moe_w_in = nrm(ks[16], (N_MOE_FFN, N_EXPERTS, D_MODEL, 2 * D_EXPERT), D_MODEL, beta)
    moe_w_out = nrm(ks[17], (N_MOE_FFN, N_EXPERTS, D_EXPERT, D_MODEL), D_EXPERT, beta)
    return {"x": x, "ret_w_in": ret_w_in, "ret_w_out": ret_w_out, "sb_w_kv": sb_w_kv,
            "sb_w_q": sb_w_q, "sb_w_out": sb_w_out, "ln_mix_g": ln_mix_g, "ln_mix_b": ln_mix_b,
            "ln_ffn_g": ln_ffn_g, "ln_ffn_b": ln_ffn_b, "ffn_w_in": ffn_w_in, "ffn_w_out": ffn_w_out,
            "moe_w_router": moe_w_router, "moe_w_in": moe_w_in, "moe_w_out": moe_w_out}

def first_block(x, ret_w_in, ret_w_out, sb_w_kv, sb_w_q, sb_w_out, ln_mix_g, ln_mix_b,
              ln_ffn_g, ln_ffn_b, ffn_w_in, ffn_w_out, moe_w_router, moe_w_in, moe_w_out):
    shared_k = None
    shared_v = None
    for layer in range(DEPTH):
        if layer < N_A_LAYERS:
            mix = retention_mixer(x, ret_w_in[layer], ret_w_out[layer])
        else:
            j = layer - N_A_LAYERS
            mix = stick_breaking_mixer(x, shared_k, shared_v, sb_w_q[j], sb_w_out[j])
        x = layer_norm(DEEPNORM_ALPHA * x + mix, ln_mix_g[layer], ln_mix_b[layer])
        if layer % 2 == 0:
            f = swiglu(x, ffn_w_in[layer // 2], ffn_w_out[layer // 2])
        else:
            f = moe_swiglu(x, moe_w_router[layer // 2], moe_w_in[layer // 2], moe_w_out[layer // 2])
        x = layer_norm(DEEPNORM_ALPHA * x + f, ln_ffn_g[layer], ln_ffn_b[layer])
        if layer == N_A_LAYERS - 1:
            shared_k, shared_v = shared_kv(x, sb_w_kv)
    return x


D_MIX = D_MODEL
ATTN_WIDTH = D_MIX // 2
ATTN_HEAD_DIM = 64
ATTN_HEADS = ATTN_WIDTH // ATTN_HEAD_DIM
DILATED_PATTERNS = ((128, 1), (512, 4), (2048, 16))
ROPE_THETA = 10000.0
MLSTM_WIDTH = D_MIX - ATTN_WIDTH
MLSTM_HEADS = 4
MLSTM_HEAD_DIM = MLSTM_WIDTH // MLSTM_HEADS
MLSTM_CHUNK = 128
MLSTM_CONV = 5
PROJ_COLS = 3 * ATTN_WIDTH + 4 * MLSTM_WIDTH + 4 * MLSTM_HEADS
D_FF_2 = ((8 * D_MODEL // 3 + 255) // 256) * 256
FFN_CONV = 3
NORM_EPS = 1e-6
NEG_INF = -1e30


def rms_norm(x, g):
    xf = x.astype(jnp.float32)
    y = xf * lax.rsqrt(jnp.mean(xf * xf, axis=-1, keepdims=True) + NORM_EPS)
    return (y * g.astype(jnp.float32)).astype(x.dtype)

def depthwise_conv_centred(x, w, b):
    k = w.shape[0]
    pad = k // 2
    s = x.shape[1]
    xp = jnp.pad(x, ((0, 0), (pad, pad), (0, 0)))
    out = xp[:, 0:s] * w[0]
    for j in range(1, k):
        out = out + xp[:, j:j + s] * w[j]
    return out + b

def apply_rotary(t):
    s, dh = t.shape[2], t.shape[3]
    inv_freq = ROPE_THETA ** (-jnp.arange(0, dh, 2, dtype=jnp.float32) / dh)
    ang = jnp.arange(s, dtype=jnp.float32)[:, None] * inv_freq[None, :]
    cos, sin = jnp.cos(ang), jnp.sin(ang)
    t1, t2 = t[..., :dh // 2], t[..., dh // 2:]
    return jnp.concatenate([t1 * cos - t2 * sin, t2 * cos + t1 * sin], axis=-1)

def dilated_window_branch(q, k, v, window, dilation):
    b, h, s, dh = q.shape
    half = window // (2 * dilation)
    blk = half
    n_sub = s // dilation
    nb = -(-n_sub // blk)
    lp = nb * blk

    def to_sub(t):
        return jnp.swapaxes(t.reshape(b, h, n_sub, dilation, dh), 2, 3)

    qs = jnp.pad(to_sub(q), ((0, 0), (0, 0), (0, 0), (0, lp - n_sub), (0, 0)))
    kpad = ((0, 0), (0, 0), (0, 0), (blk, lp - n_sub + blk), (0, 0))
    ks = jnp.pad(to_sub(k), kpad)
    vs = jnp.pad(to_sub(v), kpad)

    def band(t):
        return jnp.concatenate(
            [t[:, :, :, i * blk:i * blk + lp].reshape(b, h, dilation, nb, blk, dh) for i in range(3)], axis=4)

    qb = qs.reshape(b, h, dilation, nb, blk, dh)
    kb, vb = band(ks), band(vs)
    scores = jnp.einsum('bhrnqe,bhrnke->bhrnqk', qb, kb) * (dh ** -0.5)
    qi = jnp.arange(nb)[:, None] * blk + jnp.arange(blk)[None, :]
    ki = jnp.arange(nb)[:, None] * blk - blk + jnp.arange(3 * blk)[None, :]
    off = ki[:, None, :] - qi[:, :, None]
    valid = (jnp.abs(off) <= half) & (ki[:, None, :] >= 0) & (ki[:, None, :] < n_sub)
    scores = jnp.where(valid, scores, NEG_INF)
    m = jnp.max(scores, axis=-1, keepdims=True)
    p = jnp.exp(scores - m)
    den = jnp.sum(p, axis=-1)
    out = jnp.einsum('bhrnqk,bhrnke->bhrnqe', p, vb) / den[..., None]
    lse = m[..., 0] + jnp.log(den)
    out = jnp.swapaxes(out.reshape(b, h, dilation, lp, dh)[:, :, :, :n_sub], 2, 3).reshape(b, h, s, dh)
    lse = jnp.swapaxes(lse.reshape(b, h, dilation, lp)[:, :, :, :n_sub], 2, 3).reshape(b, h, s)
    return out, lse

def dilated_attention(q, k, v):
    outs, lses = [], []
    for window, dilation in DILATED_PATTERNS:
        o, l = dilated_window_branch(q, k, v, window, dilation)
        outs.append(o)
        lses.append(l)
    wts = jax.nn.softmax(jnp.stack(lses, axis=0), axis=0)
    out = wts[0][..., None] * outs[0]
    for i in range(1, len(outs)):
        out = out + wts[i][..., None] * outs[i]
    return out

def mlstm_direction(q, k, v, log_i, log_f):
    b, h, s, dh = q.shape
    ch = MLSTM_CHUNK
    nc = s // ch
    k = k * (dh ** -0.5)

    def chunks(t):
        return jnp.moveaxis(t.reshape(b, h, nc, ch, *t.shape[3:]), 2, 0)

    causal = jnp.tril(jnp.ones((ch, ch), dtype=bool))

    def step(carry, xs):
        c_st, n_st, m_st = carry
        qc, kc, vc, lic, lfc = xs
        bcum = jnp.cumsum(lfc, axis=-1)
        dlog = bcum[..., :, None] - bcum[..., None, :] + lic[..., None, :]
        dlog = jnp.where(causal, dlog, NEG_INF)
        inter = bcum + m_st[..., None]
        m_t = jnp.maximum(inter, jnp.max(dlog, axis=-1))
        sc = jnp.einsum('bhte,bhse->bhts', qc, kc) * jnp.exp(dlog - m_t[..., None])
        g = jnp.exp(inter - m_t)
        num = jnp.einsum('bhts,bhsf->bhtf', sc, vc) + g[..., None] * jnp.einsum('bhte,bhef->bhtf', qc, c_st)
        den = jnp.sum(sc, axis=-1) + g * jnp.einsum('bhte,bhe->bht', qc, n_st)
        h_t = num / jnp.maximum(jnp.abs(den), jnp.exp(-m_t))[..., None]
        b_last = bcum[..., -1]
        wlog = b_last[..., None] - bcum + lic
        m_new = jnp.maximum(b_last + m_st, jnp.max(wlog, axis=-1))
        wexp = jnp.exp(wlog - m_new[..., None])
        decay = jnp.exp(b_last + m_st - m_new)
        c_new = decay[..., None, None] * c_st + jnp.einsum('bhs,bhse,bhsf->bhef', wexp, kc, vc)
        n_new = decay[..., None] * n_st + jnp.einsum('bhs,bhse->bhe', wexp, kc)
        return (c_new, n_new, m_new), h_t

    init = (jnp.zeros((b, h, dh, dh), jnp.float32), jnp.zeros((b, h, dh), jnp.float32),
            jnp.zeros((b, h), jnp.float32))
    _, hs = lax.scan(step, init, (chunks(q), chunks(k), chunks(v), chunks(log_i), chunks(log_f)))
    return jnp.moveaxis(hs, 0, 2).reshape(b, h, s, dh)

def hybrid_mixer(hn, w_in, mlstm_conv_w, mlstm_conv_b, mlstm_gate_b, mlstm_head_g, w_out):
    b, s, _ = hn.shape
    f32 = jnp.float32
    sizes = [ATTN_WIDTH] * 3 + [MLSTM_WIDTH] * 4 + [4 * MLSTM_HEADS]
    split_at = np.cumsum(sizes)[:-1].tolist()
    aq, ak, av, mq, mk, mv, mo, gates = jnp.split(hn @ w_in, split_at, axis=-1)

    def heads(t, n):
        return jnp.transpose(t.astype(f32).reshape(b, s, n, -1), (0, 2, 1, 3))

    q = apply_rotary(heads(aq, ATTN_HEADS))
    k = apply_rotary(heads(ak, ATTN_HEADS))
    v = heads(av, ATTN_HEADS)
    attn = dilated_attention(q, k, v)
    attn = jnp.transpose(attn, (0, 2, 1, 3)).reshape(b, s, ATTN_WIDTH).astype(hn.dtype)

    qk = jax.nn.silu(depthwise_conv_centred(jnp.concatenate([mq, mk], axis=-1), mlstm_conv_w, mlstm_conv_b))
    mq, mk = jnp.split(qk, 2, axis=-1)
    q = heads(mq, MLSTM_HEADS)
    k = heads(mk, MLSTM_HEADS)
    v = heads(mv, MLSTM_HEADS)
    g = (gates + mlstm_gate_b).astype(f32).reshape(b, s, 4, MLSTM_HEADS)
    g = jnp.transpose(g, (2, 0, 3, 1))
    h_fwd = mlstm_direction(q, k, v, g[0], jax.nn.log_sigmoid(g[1]))
    flip = lambda t: jnp.flip(t, axis=2)
    h_bwd = flip(mlstm_direction(flip(q), flip(k), flip(v), flip(g[2]), flip(jax.nn.log_sigmoid(g[3]))))
    hm = h_fwd + h_bwd
    hm = hm * lax.rsqrt(jnp.mean(hm * hm, axis=-1, keepdims=True) + NORM_EPS)
    hm = jnp.transpose(hm, (0, 2, 1, 3)).reshape(b, s, MLSTM_WIDTH)
    mlstm = (hm * mlstm_head_g.astype(f32) * jax.nn.sigmoid(mo.astype(f32))).astype(hn.dtype)

    return jnp.concatenate([attn, mlstm], axis=-1) @ w_out

def conv_ffn(hn, w_up, conv_w, conv_b, w_down):
    u = depthwise_conv_centred(hn @ w_up, conv_w, conv_b)
    gate, val = jnp.split(u, 2, axis=-1)
    return (jax.nn.gelu(gate, approximate=True) * val) @ w_down

def second_inputs(seed: int = 0) -> dict:
    key = jax.random.key(seed)
    ks = jax.random.split(key, 16)

    def nrm(k, shape, scale):
        return jax.random.normal(k, shape, jnp.float32) * scale

    base = jnp.stack([jnp.zeros((MLSTM_HEADS,), jnp.float32),
                      jnp.linspace(3.0, 6.0, MLSTM_HEADS, dtype=jnp.float32)], axis=0)
    gate_b = (nrm(ks[5], (DEPTH, 2, 2, MLSTM_HEADS), 0.1) + base[None, None]).reshape(DEPTH, 4 * MLSTM_HEADS)
    return {
        'x': nrm(ks[0], (BATCH, SEQ, D_MODEL), 1.0),
        'mix_pre_g': 1.0 + nrm(ks[1], (DEPTH, D_MODEL), 0.02),
        'w_in': nrm(ks[2], (DEPTH, D_MODEL, PROJ_COLS), D_MODEL ** -0.5),
        'mlstm_conv_w': nrm(ks[3], (DEPTH, MLSTM_CONV, 2 * MLSTM_WIDTH), MLSTM_CONV ** -0.5),
        'mlstm_conv_b': nrm(ks[4], (DEPTH, 2 * MLSTM_WIDTH), 0.02),
        'mlstm_gate_b': gate_b,
        'mlstm_head_g': 1.0 + nrm(ks[6], (DEPTH, MLSTM_WIDTH), 0.02),
        'w_out': nrm(ks[7], (DEPTH, D_MIX, D_MODEL), D_MIX ** -0.5),
        'mix_post_g': 1.0 + nrm(ks[8], (DEPTH, D_MODEL), 0.02),
        'ffn_pre_g': 1.0 + nrm(ks[9], (DEPTH, D_MODEL), 0.02),
        'w_up': nrm(ks[10], (DEPTH, D_MODEL, 2 * D_FF_2), D_MODEL ** -0.5),
        'ffn_conv_w': nrm(ks[11], (DEPTH, FFN_CONV, 2 * D_FF_2), FFN_CONV ** -0.5),
        'ffn_conv_b': nrm(ks[12], (DEPTH, 2 * D_FF_2), 0.02),
        'w_down': nrm(ks[13], (DEPTH, D_FF_2, D_MODEL), D_FF_2 ** -0.5),
        'ffn_post_g': 1.0 + nrm(ks[14], (DEPTH, D_MODEL), 0.02),
    }

def second_block(x, mix_pre_g, w_in, mlstm_conv_w, mlstm_conv_b, mlstm_gate_b, mlstm_head_g, w_out,
              mix_post_g, ffn_pre_g, w_up, ffn_conv_w, ffn_conv_b, w_down, ffn_post_g):
    for l in range(DEPTH):
        mixed = hybrid_mixer(rms_norm(x, mix_pre_g[l]), w_in[l], mlstm_conv_w[l], mlstm_conv_b[l],
                             mlstm_gate_b[l], mlstm_head_g[l], w_out[l])
        x = x + rms_norm(mixed, mix_post_g[l])
        ff = conv_ffn(rms_norm(x, ffn_pre_g[l]), w_up[l], ffn_conv_w[l], ffn_conv_b[l], w_down[l])
        x = x + rms_norm(ff, ffn_post_g[l])
    return x


def setup_inputs(seed=0):
    out = dict(first_inputs(seed))
    for name, value in second_inputs(seed + 1).items():
        if name != "x":
            out[name + "_2"] = value
    return out


def reference(
    x, ret_w_in, ret_w_out, sb_w_kv, sb_w_q, sb_w_out, ln_mix_g, ln_mix_b, ln_ffn_g, ln_ffn_b,
    ffn_w_in, ffn_w_out, moe_w_router, moe_w_in, moe_w_out, mix_pre_g_2, w_in_2, mlstm_conv_w_2,
    mlstm_conv_b_2, mlstm_gate_b_2, mlstm_head_g_2, w_out_2, mix_post_g_2, ffn_pre_g_2, w_up_2,
    ffn_conv_w_2, ffn_conv_b_2, w_down_2, ffn_post_g_2,
):
    x = first_block(
        x, ret_w_in, ret_w_out, sb_w_kv, sb_w_q, sb_w_out, ln_mix_g, ln_mix_b, ln_ffn_g,
        ln_ffn_b, ffn_w_in, ffn_w_out, moe_w_router, moe_w_in, moe_w_out,
    )
    return second_block(
        x, mix_pre_g_2, w_in_2, mlstm_conv_w_2, mlstm_conv_b_2, mlstm_gate_b_2, mlstm_head_g_2,
        w_out_2, mix_post_g_2, ffn_pre_g_2, w_up_2, ffn_conv_w_2, ffn_conv_b_2, w_down_2,
        ffn_post_g_2,
    )


_drawn_inputs = setup_inputs


def setup_inputs(seed=0):
    import zlib

    import numpy as np

    out = dict(_drawn_inputs(seed))
    spreads = {}
    factors = {'mlstm_conv_b_2': 2.986, 'mlstm_head_g_2': 2.669, 'ffn_post_g_2': 3.598}
    for name, (base, spread) in spreads.items():
        noise = np.random.default_rng([zlib.crc32(name.encode()), seed]).standard_normal(out[name].shape)
        drawn = base * np.exp(spread * noise) if base else spread * noise
        out[name] = __import__('jax').numpy.asarray(drawn.astype(out[name].dtype))
    for name, factor in factors.items():
        out[name] = (out[name] * factor).astype(out[name].dtype)
    return out
```

```python
from contextlib import ExitStack

import numpy as np

import concourse.bass as bass
from concourse import mybir

ACT_STEPS, VEC_STEPS = 5, 107

P = 128
D = 1024
S = 256
TB = S // P
KT = D // P
HALF = 512
F32 = mybir.dt.float32
ALU = mybir.AluOpType
ACT = mybir.ActivationFunctionType
AX = mybir.AxisListType

SLOTS = 6
SLOT = 2048

RET_H, RET_V = 4, 2048
SB_H = 16
FF = 2816
FT = FF // P
EXPERTS = 8
EF = 3584
ET = EF // P
ALPHA = 4.0 ** 0.25
LN_EPS = 1e-5
LAYERS = 2
AT_H, AT_D, AT_W = 8, 64, 512
ML_H, ML_D, ML_W = 4, 128, 512
ML_TAPS, FF_TAPS = 5, 3
PAD = ML_TAPS // 2
RMS_EPS = 1e-6
NEG = -1e30
CHUNK = 64

RET_ROWS = [2] * (RET_V // P // 2)
MIX_ROWS = [2] * (KT // 2)
FFN_ROWS = [2] * (FT // 2)
EXPERT_ROWS = [2] * (ET // 2)
LAYER_ROWS = [2] * (FT // 2)

PAR_MIX_G, PAR_FFN_G, PAR_TAP, PAR_TAP_B = 0, KT, 2 * KT, 2 * KT + 8 * ML_TAPS
PAR_FTAP = PAR_TAP_B + 8
PAR_FTAP_B = PAR_FTAP + 2 * FT * FF_TAPS
PARS = PAR_FTAP_B + 2 * FT
GAINS = 2 * D + ML_W
DECAY = RET_H * 3 * P

EXPERT_TURN = dict(chunk=ET + len(EXPERT_ROWS), tile=ET, sum=4)
LAYER_TURN = dict(chunk=9 + 4 + 4 + len(MIX_ROWS) + FT + len(LAYER_ROWS), tile=80, sum=24)
assert all(t["chunk"] % SLOTS == 0 and t["tile"] % 4 == 0 and t["sum"] % 4 == 0
           for t in (EXPERT_TURN, LAYER_TURN))


class Count:

    def __init__(self, group=1, unit=1):
        self.index, self.skew, self.group, self.unit = 0, 0, group, unit

    @property
    def value(self):
        return self.skew + self.unit * (self.index // self.group)

    def next(self):
        self.index += 1
        return self.value

    def more(self, count):
        self.index += count

    def enter(self, turn, per_turn):
        self.began, self.before, self.per_turn = self.index, self.skew, per_turn
        self.skew = turn * (per_turn * self.unit // self.group) + self.before

    def leave(self, turns):
        assert self.index - self.began == self.per_turn, (self.index - self.began, self.per_turn)
        self.skew = self.before + (turns - 1) * self.per_turn * self.unit // self.group


class Counts(dict):

    def __init__(self, *names, **made):
        for name in names:
            self[name] = Count()
        self.update(made)

    def enter(self, turn, **per_turn):
        self.inside = per_turn
        for name, events in per_turn.items():
            self[name].enter(turn, events)

    def leave(self, turns):
        for name in self.inside:
            self[name].leave(turns)


def program(nc, a, out):
    with ExitStack() as ctx:
        def sb(name, *shape):
            return ctx.enter_context(nc.sbuf_tensor(name, [P, *shape], F32))

        def sem(name):
            return ctx.enter_context(nc.semaphore(name))

        ring = sb("ring", SLOTS, SLOT)
        ident = sb("ident", P)
        suffix = sb("suffix", 2, P)
        earlier = sb("earlier", P)
        rope = sb("rope", TB, 2, AT_D // 2)
        reach = sb("reach", TB, S)
        windows = sb("windows", TB, S)
        ml_mask = sb("ml_mask", 2, TB, S)
        neg_row = sb("neg_row", ML_H, P)
        ones_row = sb("ones_row", S)
        x_tok = sb("x_tok", TB, D)
        y_tok = sb("y_tok", TB, D)
        xT = sb("xT", KT, S)
        headT = sb("headT", 2 * KT, S)
        v_tok = sb("v_tok", TB * RET_V)
        g_tok = sb("g_tok", TB, RET_V)
        hT = sb("hT", ET, S)
        gain = sb("gain", 2 * GAINS)
        par = sb("par", LAYERS, PARS)
        parL = sb("parL", PARS)
        gate_bias = sb("gate_bias", LAYERS, 4)
        gate_biasL = sb("gate_biasL", 4)
        router_w = sb("router_w", KT, EXPERTS)
        gates_w = sb("gates_w", LAYERS, KT * 16)
        gates_wL = sb("gates_wL", KT * 16)
        acted = sb("acted", 2, S)
        junk = sb("junk", D)
        stats = sb("stats", 4, 2, 6)
        mean_var = sb("mean_var", 4, 2)
        std = sb("std", 8)
        rstd = sb("rstd", 8)
        sq_sum = sb("sq_sum", TB, 2)
        sq_tot = sb("sq_tot", 8)
        eps = sb("eps", 2)
        logits = sb("logits", TB, EXPERTS)
        beaten = sb("beaten", TB, EXPERTS, EXPERTS)
        rank = sb("rank", TB, EXPERTS)
        top = sb("top", TB, 2)
        gate = sb("gate", TB, EXPERTS)
        gate_e = sb("gate_e", TB)

        hflat = hT[:].rearrange("p k t -> p (k t)")
        gflat = g_tok[:].rearrange("p b n -> p (b n)")
        yflat = y_tok[:].rearrange("p b n -> p (b n)")
        tflat = headT[:].rearrange("p k t -> p (k t)")

        ret_decay = hflat[:, 0:DECAY].rearrange("p (h n) -> p h n", h=RET_H)
        ret_rope = hflat[:, DECAY:DECAY + 2 * S].rearrange("p (i t) -> p i t", i=2)
        ret_p = hflat[:, 2048:2048 + DECAY].rearrange("p (h n) -> p h n", h=RET_H)
        ret_tmp = hflat[:, 4096:4096 + 4 * S].rearrange("p (i t) -> p i t", i=4)
        ret_v = v_tok[:].rearrange("p (b n) -> p b n", b=TB)
        sb_v = v_tok[:, 0:TB * D].rearrange("p (b n) -> p b n", b=TB)
        sb_w, sb_keep, sb_e, sb_size = [hflat[:, i * 1536:(i + 1) * 1536].rearrange("p (i n) -> p i n", i=4)
                                     for i in range(3)] + [gflat[:, 0:1536].rearrange("p (i n) -> p i n", i=4)]
        rot = gflat[:, 0:2 * TB * AT_W].rearrange("p (i b n) -> p i b n", i=2, b=TB)
        o_tok = gflat[:, 2 * TB * AT_W:4 * TB * AT_W].rearrange("p (b n) -> p b n", b=TB)
        rot_tmp = yflat[:, 0:2 * AT_W].rearrange("p (i h c n) -> p i h c n", i=2, h=AT_H, c=2)
        at_p = [tflat[:, 2048 + i * 512:2560 + i * 512].rearrange("p (b s) -> p b s", b=TB) for i in range(2)]
        at_pT = [tflat[:, 3072 + i * 512:3584 + i * 512].rearrange("p (b t) -> p b t", b=TB) for i in range(2)]
        VA = AT_D + 1
        at_v = v_tok[:, 0:TB * AT_H * VA].rearrange("p (b h d) -> p b h d", b=TB, h=AT_H)
        V0 = TB * AT_H * VA
        VM = ML_D + 1
        ml_v = v_tok[:, V0:V0 + TB * ML_H * VM].rearrange("p (b h d) -> p b h d", b=TB, h=ML_H)
        V1 = V0 + TB * ML_H * VM
        ml_o = v_tok[:, V1:V1 + TB * ML_W].rearrange("p (b n) -> p b n", b=TB)
        conv = hflat[:, 0:8 * (S + 2 * PAD)].rearrange("p (f t) -> p f t", f=8)
        ml_qk = hflat[:, 2080:2080 + 8 * S].rearrange("p (f t) -> p f t", f=8)
        ml_e = [hflat[:, 4128 + i * 1024:5152 + i * 1024].rearrange("p (d s t) -> p d s t", d=2, s=TB)
                for i in range(2)]
        row = sb("row", 5, 2, S)
        gate_tok = sb("gate_tok", TB, 16)
        ml_col = sb("ml_col", 2, 2, TB, ML_H)
        neg_max = sb("neg_max", 2, TB)
        den = sb("den", 4, TB)
        fconv = sb("fconv", 2, 2, S)

        banks = [ctx.enter_context(nc.psum_tensor(f"bank{i}", [P, HALF], F32)) for i in range(8)]
        sums, tiles = banks[:4], banks[4:]

        landed = [sem(f"landed{i}") for i in range(SLOTS)]
        w_used = sem("w_used")
        tile_ready = sem("tile_ready")
        tile_taken = sem("tile_taken")
        sum_ready = sem("sum_ready")
        sum_taken = sem("sum_taken")
        vec_step = sem("vec_step")
        act_step = sem("act_step")
        consts_in = sem("consts_in")
        x_in = sem("x_in")
        gain_in = [sem(f"gain_in{i}") for i in range(2)]
        gains_in = sem("gains_in")
        eps_set = sem("eps_set")
        var_ready = sem("var_ready")
        std_ready = sem("std_ready")
        square_ready = sem("square_ready")
        x_ready = sem("x_ready")
        tok_ready = sem("tok_ready")
        og_ready = sem("og_ready")
        acted_ready = sem("acted_ready")
        z_ready = sem("z_ready")
        abs_ready = sem("abs_ready")
        log_ready = sem("log_ready")
        keep_ready = sem("keep_ready")
        wexp_ready = sem("wexp_ready")
        w_ready = sem("w_ready")
        gexp_in = sem("gexp_in")
        gexp_ready = sem("gexp_ready")
        lay_ready = sem("lay_ready")
        rot_ready = sem("rot_ready")
        conv_ready = sem("conv_ready")
        mqk_ready = sem("mqk_ready")
        forget_in = sem("forget_in")
        forget_log = sem("forget_log")
        rows_ready = sem("rows_ready")
        floor_ready = sem("floor_ready")
        p_in = sem("p_in")
        p_exp = sem("p_exp")
        d_exp = sem("d_exp")
        mixed_ready = sem("mixed_ready")
        lin_ready = sem("lin_ready")
        gtap_ready = sem("gtap_ready")
        h_ready = sem("h_ready")
        out_done = sem("out_done")

        block = ctx.enter_context(nc.Block())

        @block.sync
        def _(sp):
            n = Counts("chunk")

            def load(src, kt=None, cols=SLOT, in_loop=False):
                i = n["chunk"].index
                if i >= SLOTS:
                    sp.wait_ge(w_used, n["chunk"].value - SLOTS + 1)
                    if in_loop:
                        sp.nop(nofuse=True)
                dst = ring[:, i % SLOTS, 0:cols]
                if kt:
                    dst = ring[:, i % SLOTS, 0:kt * D].rearrange("p (k n) -> p k n", k=kt)
                sp.dma_start(dst, src).then_inc(landed[i % SLOTS], 16)
                n["chunk"].next()

            def load_rows(w, kts, **kw):
                k = 0
                for kt in kts:
                    load(w[k * P:(k + kt) * P, :].rearrange("(k p) n -> p k n", p=P), kt=kt, **kw)
                    k += kt

            for b in range(TB):
                sp.dma_start(x_tok[:, b, :], a["x"][0, b * P:(b + 1) * P, :]).then_inc(x_in, 16)
            for h in range(2 * RET_H):
                load(a["ret_qk"][h])
            for g in range(2 * RET_V // HALF):
                for part in range(2):
                    load(a["ret_vg"][g, part])
            load_rows(a["ret_w_out"][0], RET_ROWS)
            for j in range(FT):
                load(a["ffn_up"][j])
            load_rows(a["ffn_w_out"][0], FFN_ROWS)
            for name in ("sb_k", "sb_q"):
                for j in range(4):
                    load(a[name][j])
            for g in range(2):
                for part in range(2):
                    load(a["sb_v"][g, part])
            load_rows(a["sb_w_out"][0], MIX_ROWS)

            with sp.Fori(0, EXPERTS) as e:
                n.enter(e, chunk=EXPERT_TURN["chunk"])
                for j in range(ET):
                    load(a["moe_up"][bass.ds(e, 1), j].rearrange("a p n -> (a p) n"), in_loop=True)
                load_rows(a["moe_w_out"][0, bass.ds(e, 1)].rearrange("a r n -> (a r) n"), EXPERT_ROWS, in_loop=True)
            n.leave(EXPERTS)

            with sp.Fori(0, LAYERS) as l:
                n.enter(l, chunk=LAYER_TURN["chunk"])
                for g in range(3):
                    w = a["w2_attn"][bass.ds(l, 1), g].rearrange("a c p n -> (a c) p n")
                    load(w[0, :, 0:SLOT // 2], cols=SLOT // 2, in_loop=True)
                    load(w[0, :, SLOT // 2:SLOT], cols=SLOT // 2, in_loop=True)
                    load(w[1], in_loop=True)
                for j in range(4):
                    load(a["w2_mqk"][bass.ds(l, 1), j].rearrange("a p n -> (a p) n"), in_loop=True)
                for g in range(2):
                    for part in range(2):
                        load(a["w2_mvo"][bass.ds(l, 1), g, part].rearrange("a p n -> (a p) n"), in_loop=True)
                load_rows(a["w_out_2"][bass.ds(l, 1)].rearrange("a r n -> (a r) n"), MIX_ROWS, in_loop=True)
                for j in range(FT):
                    load(a["w2_up"][bass.ds(l, 1), j].rearrange("a p n -> (a p) n"), in_loop=True)
                load_rows(a["w_down_2"][bass.ds(l, 1)].rearrange("a r n -> (a r) n"), LAYER_ROWS, in_loop=True)
            n.leave(LAYERS)
            for b in range(TB):
                sp.wait_ge(x_ready, 4 * TB + LAYERS * 2 * TB - TB + b + 1)
                sp.dma_start(out[0, b * P:(b + 1) * P, :], x_tok[:, b, :]).then_inc(out_done, 16)
            sp.wait_ge(out_done, 16 * TB)

        CONSTS = ((ident, "c_ident"), (suffix, "c_suffix"), (earlier, "c_earlier"), (rope, "c_rope"),
                  (reach, "c_reach"), (windows, "c_windows"), (ml_mask, "c_ml_mask"), (router_w, "router_w"),
                  (gates_w, "gates_w"), (ret_decay, "c_decay"), (ret_rope, "c_ret_rope"))
        PARAMS = ((PAR_MIX_G, PAR_FFN_G, "mix_pre_g"), (PAR_FFN_G, PAR_TAP, "ffn_pre_g"), (PAR_TAP, PAR_TAP_B, "taps"),
                  (PAR_TAP_B, PAR_FTAP, "taps_b"), (PAR_FTAP, PAR_FTAP_B, "ffn_taps"), (PAR_FTAP_B, PARS, "ffn_taps_b"))
        CONSTS_IN = 16 * (len(CONSTS) + len(PARAMS) + 2)

        @block.gpsimd
        def _(pool):
            nc.gpsimd.memset(eps[:, 0:1], LN_EPS)
            nc.gpsimd.memset(eps[:, 1:2], RMS_EPS).then_inc(eps_set, 1)
            nc.gpsimd.memset(ones_row[:], 1.0).then_inc(eps_set, 1)
            for dst, name in CONSTS:
                ap = dst[:] if not isinstance(dst, bass.AP) else dst
                if len(ap.shape) > 2:
                    free = "abc"[:len(ap.shape) - 1]
                    ap = ap.rearrange(f"p {' '.join(free)} -> p ({' '.join(free)})")
                pool.dma_start(ap, a[name]).then_inc(consts_in, 16)
            for c0, c1, name in PARAMS:
                pool.dma_start(par[:, :, c0:c1], a[name]).then_inc(consts_in, 16)
            pool.dma_start(neg_row[0:ML_H, :, :].rearrange("p a b -> p (a b)"), a["c_neg_row"]).then_inc(consts_in, 16)
            pool.dma_start(gate_bias[0:ML_H, :, :].rearrange("p a b -> p (a b)"), a["gate_bias"]).then_inc(consts_in, 16)
            for k, (g, b_) in enumerate((("ln_mix_g", "ln_mix_b"), ("ln_ffn_g", "ln_ffn_b")) * 2):
                if k >= 2:
                    pool.wait_ge(x_ready, TB * (k - 1))
                for i, name in enumerate((g, b_)):
                    at = (k % 2) * 2 * D + i * D
                    pool.dma_start(gain[:, at:at + D], a[name][k // 2].partition_broadcast(P))\
                        .then_inc(gain_in[k % 2], 16)
            pool.wait_ge(x_ready, TB * 4)
            for l in range(LAYERS):
                for at, name, w in ((0, "mix_post_g_2", D), (D, "ffn_post_g_2", D), (2 * D, "mlstm_head_g_2", ML_W)):
                    pool.dma_start(gain[:, l * GAINS + at:l * GAINS + at + w],
                                   a[name][l].partition_broadcast(P)).then_inc(gains_in, 16)

        @block.tensor
        def _(pe):
            n = Counts("tile", "sum", "chunk", "x", "tok", "og", "z", "keep", "w", "lay", "rot", "mqk",
                       "rows", "floor", "pexp", "mixed", "h", land=Count(SLOTS, 16))
            fresh = [False]

            def slot():
                i = n["chunk"].index
                pe.wait_ge(landed[i % SLOTS], n["land"].value + 16)
                fresh[0] = i > 0
                n["chunk"].next(), n["land"].next()
                return ring[:, i % SLOTS, :]

            def mm(*args, **kw):
                ins = nc.tensor.matmul(*args, **kw)
                if fresh[0]:
                    ins.then_inc(w_used, 1)
                    fresh[0] = False
                return ins

            def open_tile():
                return open_tiles(1)[0]

            def open_tiles(count):
                i = n["tile"].index
                n["tile"].more(count)
                if i + count > 4:
                    pe.wait_ge(tile_taken, n["tile"].value - 4)
                return [tiles[(i + k) % 4] for k in range(count)]

            def open_sum():
                return open_sums(1)[0]

            def open_sums(count):
                i = n["sum"].index
                n["sum"].more(count)
                if i + count > 4:
                    pe.wait_ge(sum_taken, n["sum"].value - 4)
                return [sums[(i + k) % 4] for k in range(count)]

            def all_taken():
                pe.wait_ge(tile_taken, n["tile"].value)

            def transposes(block_of, count):
                for j in range(count // 2):
                    bank = open_tile()
                    for i in range(2):
                        for b in range(TB):
                            last = nc.tensor.transpose(bank[:, i * S + b * P:i * S + (b + 1) * P],
                                                       block_of(b, 2 * j + i), ident[:])
                    last.then_inc(tile_ready, 1)

            def feature_tile():
                w = slot().rearrange("p (k n) -> p k n", k=KT)
                bank = open_tile()
                for i in range(2):
                    for k in range(KT):
                        last = mm(bank[:, i * S:(i + 1) * S], w[:, k, i * P:(i + 1) * P], xT[:, k, :],
                                  start=(k == 0), stop=(k == KT - 1))
                last.then_inc(tile_ready, 1)

            def token_tiles(kts=(4, 4)):
                pair = open_tiles(TB)
                k = 0
                for kt in kts:
                    w = slot()
                    for kk in range(kt):
                        for b in range(TB):
                            last = mm(pair[b][:], xT[:, k, b * P:(b + 1) * P], w[:, kk * HALF:(kk + 1) * HALF],
                                      start=(k == 0), stop=(k == KT - 1))
                            if k == KT - 1:
                                last.then_inc(tile_ready, 1)
                        k += 1

            def down(lhs, kts, ready=None):
                acc = open_sums(4)
                k, total = 0, sum(kts)
                for kt in kts:
                    w = slot()
                    for kk in range(kt):
                        if ready is not None:
                            ready(k)
                        for b in range(TB):
                            for h in range(2):
                                last = mm(acc[2 * b + h][:], lhs(k, b), w[:, kk * D + h * HALF:kk * D + (h + 1) * HALF],
                                          start=(k == 0), stop=(k == total - 1))
                                if k == total - 1:
                                    last.then_inc(sum_ready, 1)
                        k += 1

            def ffn(kts):
                first = n["tile"].value
                for _ in range(sum(kts)):
                    feature_tile()
                down(lambda k, b: hT[:, k, b * P:(b + 1) * P], kts,
                     lambda k: pe.wait_ge(tile_taken, first + k + 1))

            def x_transposes():
                n["x"].more(TB)
                pe.wait_ge(x_ready, n["x"].value)
                transposes(lambda b, d: x_tok[:, b, d * P:(d + 1) * P], KT)
                all_taken()

            pe.wait_ge(consts_in, CONSTS_IN)
            pe.wait_ge(x_in, 16 * TB)
            transposes(lambda b, d: x_tok[:, b, d * P:(d + 1) * P], KT)
            all_taken()
            for _ in range(2 * RET_H):
                feature_tile()
            for _ in range(2 * RET_V // HALF):
                token_tiles()
            all_taken()
            first = n["tile"].value
            for h in range(RET_H):
                q, k = headT[:, 2 * h:2 * h + 2, :], headT[:, KT + 2 * h:KT + 2 * h + 2, :]
                bank = open_tile()
                for c in range(2):
                    nc.tensor.matmul(bank[:, 0:S], k[:, c, 0:P], q[:, c, :], start=(c == 0), stop=(c == 1))
                for c in range(2):
                    last = nc.tensor.matmul(bank[:, S:S + P], k[:, c, P:S], q[:, c, P:S],
                                            start=(c == 0), stop=(c == 1))
                last.then_inc(tile_ready, 1)
            for h in range(RET_H):
                pe.wait_ge(tile_taken, first + h + 1)
                v = [ret_v[:, b, h * HALF:(h + 1) * HALF] for b in range(TB)]
                bank = open_tile()
                nc.tensor.matmul(bank[:], ret_p[:, h, 0:P], v[0], start=True, stop=True).then_inc(tile_ready, 1)
                bank = open_tile()
                nc.tensor.matmul(bank[:], ret_p[:, h, P:S], v[0], start=True, stop=False)
                nc.tensor.matmul(bank[:], ret_p[:, h, S:S + P], v[1], start=False, stop=True).then_inc(tile_ready, 1)
            n["og"].more(RET_H * TB)
            pe.wait_ge(og_ready, n["og"].value)
            transposes(lambda b, d: g_tok[:, b, d * P:(d + 1) * P], 2 * KT)
            all_taken()
            down(lambda k, b: headT[:, k, b * P:(b + 1) * P], RET_ROWS)
            x_transposes()
            ffn(FFN_ROWS)
            x_transposes()

            for _ in range(8):
                feature_tile()
            for _ in range(2):
                token_tiles()
            all_taken()
            opened = {}

            def sb_scores(h):
                po = (h % 2) * 64
                q, k = headT[po:po + 64, KT + h // 2, :], headT[po:po + 64, h // 2, :]
                opened[h] = bank = open_tile()
                nc.tensor.matmul(bank[:, 0:S], k[:, 0:P], q, start=True, stop=False, skip_group_check=True)
                nc.tensor.matmul(bank[:, S:S + P], k[:, P:S], q[:, P:S], start=False, stop=False,
                                 skip_group_check=True).then_inc(z_ready, 1)

            def sb_suffix(h):
                pe.wait_ge(keep_ready, n["keep"].next())
                bank, keep = opened[h], sb_keep[:, h % 4, :]
                nc.tensor.matmul(bank[:, 0:S], suffix[:, 0, :], keep[:, 0:S], start=False, stop=False,
                                 skip_group_check=True)
                nc.tensor.matmul(bank[:, P:S], suffix[:, 1, :], keep[:, S:S + P], start=False, stop=False,
                                 skip_group_check=True)
                nc.tensor.matmul(bank[:, S:S + P], suffix[:, 0, :], keep[:, S:S + P], start=False, stop=True,
                                 skip_group_check=True).then_inc(tile_ready, 1)

            def sb_out(m):
                bank = open_sum()
                for i in range(2):
                    h = 2 * m + i
                    pe.wait_ge(w_ready, n["w"].next())
                    o, w = bank[64 * i:64 * i + 64, 0:S], sb_w[:, h % 4, :]
                    nc.tensor.matmul(o, sb_v[:, 0, h * 64:(h + 1) * 64], w[:, 0:S], start=True, stop=False)
                    last = nc.tensor.matmul(o[:, P:S], sb_v[:, 1, h * 64:(h + 1) * 64], w[:, S:S + P],
                                            start=False, stop=True)
                last.then_inc(sum_ready, 1)

            for s in range(SB_H + 3):
                if s < SB_H:
                    sb_scores(s)
                if 1 <= s <= SB_H:
                    sb_suffix(s - 1)
                if s >= 4 and s % 2 == 0:
                    sb_out((s - 4) // 2)
            pe.wait_ge(sum_taken, n["sum"].value)
            down(lambda k, b: xT[:, k, b * P:(b + 1) * P], MIX_ROWS)
            x_transposes()

            bank = open_tile()
            for b in range(TB):
                for k in range(KT):
                    last = nc.tensor.matmul(bank[:, b * EXPERTS:(b + 1) * EXPERTS], xT[:, k, b * P:(b + 1) * P],
                                            router_w[:, k, :], start=(k == 0), stop=(k == KT - 1))
            last.then_inc(tile_ready, 1)
            with pe.Fori(0, EXPERTS) as e:
                n.enter(e, land=EXPERT_TURN["chunk"], **EXPERT_TURN)
                ffn(EXPERT_ROWS)
            n.leave(EXPERTS)

            with pe.Fori(0, LAYERS) as l:
                n.enter(l, land=LAYER_TURN["chunk"], tok=4, lay=1, rot=2, mqk=8, rows=1, floor=1, pexp=AT_H,
                        mixed=1, h=FT, **LAYER_TURN)
                pe.wait_ge(lay_ready, n["lay"].next())

                def y_transposes():
                    n["tok"].more(TB)
                    pe.wait_ge(tok_ready, n["tok"].value)
                    transposes(lambda b, d: y_tok[:, b, d * P:(d + 1) * P], KT)
                    all_taken()

                y_transposes()
                bank = open_tile()
                for b in range(TB):
                    for k in range(KT):
                        last = nc.tensor.matmul(bank[:, b * 16:(b + 1) * 16], xT[:, k, b * P:(b + 1) * P],
                                                gates_wL[:, k * 16:(k + 1) * 16], start=(k == 0), stop=(k == KT - 1))
                last.then_inc(tile_ready, 1)
                for _ in range(3):
                    token_tiles((2, 2, 4))
                for _ in range(4):
                    feature_tile()
                for _ in range(2):
                    token_tiles()
                for kind in range(2):
                    bank = open_tile()
                    pe.nop(nofuse=True)
                    for d in range(2):
                        for b in range(TB):
                            c = (2 * d + kind) * ML_H
                            last = nc.tensor.transpose(bank[0:ML_H, d * S + b * P:d * S + (b + 1) * P],
                                                       gate_tok[:, b, c:c + ML_H], ident[:])
                    last.then_inc(tile_ready, 1)
                for i in range(2):
                    pe.wait_ge(rot_ready, n["rot"].next())
                    transposes(lambda b, d: rot[:, i, b, d * P:(d + 1) * P], AT_W // P)
                all_taken()
                turned = {}

                def at_scores(h):
                    po = (h % 2) * 64
                    q, k = headT[po:po + 64, h // 2, :], headT[po:po + 64, 4 + h // 2, :]
                    bank = open_tile()
                    for b in range(TB):
                        last = nc.tensor.matmul(bank[:, b * S:(b + 1) * S], q[:, b * P:(b + 1) * P], k,
                                                start=True, stop=True)
                    last.then_inc(tile_ready, 1)

                def at_turn(h):
                    pe.wait_ge(p_exp, n["pexp"].next())
                    bank = open_tile()
                    for kb in range(TB):
                        for b in range(TB):
                            last = nc.tensor.transpose(bank[:, kb * S + b * P:kb * S + (b + 1) * P],
                                                       at_p[h % 2][:, b, kb * P:(kb + 1) * P], ident[:])
                    last.then_inc(tile_ready, 1)
                    turned[h] = n["tile"].value

                def at_out(h):
                    pe.wait_ge(tile_taken, turned[h])
                    bank = open_sum()
                    for b in range(TB):
                        for kb in range(TB):
                            last = nc.tensor.matmul(bank[:, b * VA:(b + 1) * VA], at_pT[h % 2][:, kb, b * P:(b + 1) * P],
                                                    at_v[:, kb, h, :], start=(kb == 0), stop=(kb == 1))
                    last.then_inc(sum_ready, 1)

                for s in range(AT_H + 2):
                    if s < AT_H:
                        at_scores(s)
                    if 1 <= s <= AT_H:
                        at_turn(s - 1)
                    if s >= 2:
                        at_out(s - 2)

                pe.wait_ge(rows_ready, n["rows"].next())
                pe.wait_ge(floor_ready, n["floor"].next())
                bank = open_tile()
                pe.nop(nofuse=True)
                for kind, r in enumerate((2, 4)):
                    for d in range(2):
                        for b in range(TB):
                            c = ((kind * 2 + d) * TB + b) * ML_H
                            last = nc.tensor.transpose(bank[:, c:c + ML_H], row[0:ML_H, r, d, b * P:(b + 1) * P],
                                                       ident[0:ML_H, 0:ML_H])
                last.then_inc(tile_ready, 1)
                n["mqk"].more(8)
                pe.wait_ge(mqk_ready, n["mqk"].value)
                decayed = {}

                def ml_scores(h):
                    bank = open_tile()
                    nc.tensor.matmul(bank[:], neg_row[0:ML_H, h, :], row[0:ML_H, 3, :, :].rearrange("p d t -> p (d t)"),
                                     start=True, stop=True).then_inc(tile_ready, 1)
                    bank = open_tile()
                    for kb in range(TB):
                        last = nc.tensor.matmul(bank[:, kb * S:(kb + 1) * S], ml_qk[:, ML_H + h, kb * P:(kb + 1) * P],
                                                ml_qk[:, h, :], start=True, stop=True)
                    last.then_inc(tile_ready, 1)
                    decayed[h] = n["tile"].value

                def ml_out(h):
                    pe.wait_ge(tile_taken, decayed[h])
                    for d in range(2):
                        bank = open_sum()
                        for b in range(TB):
                            seen = range(0, b + 1) if d == 0 else range(b, TB)
                            for i, kb in enumerate(seen):
                                last = nc.tensor.matmul(bank[:, b * VM:(b + 1) * VM], ml_e[h % 2][:, d, kb, b * P:(b + 1) * P],
                                                        ml_v[:, kb, h, :], start=(i == 0), stop=(i == len(seen) - 1))
                        last.then_inc(sum_ready, 1)

                for s in range(ML_H + 1):
                    if s < ML_H:
                        ml_scores(s)
                    if s >= 1:
                        ml_out(s - 1)
                pe.wait_ge(mixed_ready, n["mixed"].next())
                transposes(lambda b, d: o_tok[:, b, d * P:(d + 1) * P], KT)
                all_taken()
                down(lambda k, b: headT[:, k, b * P:(b + 1) * P], MIX_ROWS)
                y_transposes()
                for _ in range(FT):
                    feature_tile()
                down(lambda k, b: hT[:, k, b * P:(b + 1) * P], LAYER_ROWS,
                     lambda k: pe.wait_ge(h_ready, n["h"].next()))
            n.leave(LAYERS)

        @block.scalar
        def _(act):
            n = Counts("tile", "sum", "step", "var", "x", "tok", "abs", "gexp", "lay", "conv", "forget",
                       "rows", "pin", "gtap", "h")

            def step(ins):
                ins.then_inc(act_step, 1)
                act.wait_ge(act_step, n["step"].next())

            def arrived():
                i = n["tile"].index
                act.wait_ge(tile_ready, n["tile"].next())
                return tiles[i % 4]

            def hand_over():
                act.wait_ge(tile_taken, n["tile"].value)

            def copy_tiles(dst, count, func=ACT.Copy, scale=1.0):
                for j in range(count):
                    bank = arrived()
                    nc.scalar.activation(dst(j), bank[:], func, scale=scale).then_inc(tile_taken, 1)

            def pair(t):
                return lambda j: t[:, 2 * j:2 * j + 2, :].rearrange("p k t -> p (k t)")

            def layer_norm_roots():
                for b in range(TB):
                    act.wait_ge(var_ready, n["var"].next())
                    nc.scalar.activation(std[:, b:b + 1], mean_var[:, b, 1:2], ACT.Sqrt,
                                         bias=eps[:, 0:1]).then_inc(std_ready, 1)

            def silu_tiles(count):
                for j in range(count):
                    bank = arrived()
                    act.wait_ge(tile_taken, n["tile"].value - 2)
                    nc.scalar.activation(acted[:, j % 2, :], bank[:, 0:S], ACT.Silu).then_inc(acted_ready, 1)

            act.wait_ge(eps_set, 2)
            copy_tiles(pair(xT), 4)
            for _ in range(2 * RET_H):
                n["tile"].next()
            hand_over()
            copy_tiles(lambda j: ret_v[:, j % 2, (j // 2) * HALF:(j // 2 + 1) * HALF], 8)
            copy_tiles(lambda j: g_tok[:, j % 2, (j // 2) * HALF:(j // 2 + 1) * HALF], 8, ACT.Silu)
            for _ in range(RET_H):
                n["tile"].next()
            for g in range(RET_H * TB // 4):
                for i in range(4):
                    n["tile"].next()
                    act.wait_ge(var_ready, n["var"].next())
                    nc.scalar.activation(std[:, 4 + i:5 + i], mean_var[:, i, 1:2], ACT.Sqrt,
                                         bias=eps[:, 0:1]).then_inc(std_ready, 1)
            hand_over()
            copy_tiles(pair(headT), 8)
            n["sum"].next(), n["sum"].next(), n["sum"].next(), n["sum"].next()
            layer_norm_roots()
            copy_tiles(pair(xT), 4)
            silu_tiles(FT)
            for _ in range(4):
                n["sum"].next()
            layer_norm_roots()
            hand_over()
            copy_tiles(pair(xT), 4)

            copy_tiles(pair(headT), 4)
            copy_tiles(lambda j: headT[:, KT + 2 * j:KT + 2 * j + 2, :].rearrange("p k t -> p (k t)"), 4,
                       scale=64 ** -0.5)
            copy_tiles(lambda j: sb_v[:, j % 2, (j // 2) * HALF:(j // 2 + 1) * HALF], 4)

            def sb_log(h):
                act.wait_ge(abs_ready, n["abs"].next())
                e = sb_e[:, h % 4, :]
                step(nc.scalar.activation(e, sb_size[:, h % 4, :], ACT.Exp, scale=-1.0))
                nc.scalar.activation(e, e, ACT.Ln, bias=1.0).then_inc(log_ready, 1)

            def sb_exp(h):
                act.wait_ge(tile_taken, n["tile"].next())
                nc.scalar.activation(sb_w[:, h % 4, :], sb_w[:, h % 4, :], ACT.Exp).then_inc(wexp_ready, 1)

            def sb_take(m):
                i = n["sum"].index
                act.wait_ge(sum_ready, n["sum"].next())
                nc.scalar.activation(xT[:, m, :], sums[i % 4][:, 0:S], ACT.Copy).then_inc(sum_taken, 1)

            for s in range(SB_H + 2):
                if s < SB_H:
                    sb_log(s)
                if s >= 2:
                    sb_exp(s - 2)
                if s >= 5 and s % 2 == 1:
                    sb_take((s - 5) // 2)
            sb_take(SB_H // 2 - 1)
            for _ in range(4):
                n["sum"].next()
            layer_norm_roots()
            hand_over()
            copy_tiles(pair(xT), 4)

            n["tile"].next()
            act.wait_ge(gexp_in, n["gexp"].next())
            nc.scalar.activation(gate[:].rearrange("p b e -> p (b e)"), gate[:].rearrange("p b e -> p (b e)"),
                                 ACT.Exp).then_inc(gexp_ready, 1)
            with act.Fori(0, EXPERTS) as e:
                n.enter(e, tile=ET, sum=4)
                silu_tiles(ET)
                for _ in range(4):
                    n["sum"].next()
            n.leave(EXPERTS)
            layer_norm_roots()

            for _ in range(TB * 3):
                n["x"].next()
            with act.Fori(0, LAYERS) as l:
                n.enter(l, tile=LAYER_TURN["tile"], sum=LAYER_TURN["sum"], x=4, var=5, lay=1, conv=8, forget=1,
                        rows=1, pin=AT_H, gtap=FT, h=FT, step=ACT_STEPS)

                def pre_norm_root(b):
                    act.wait_ge(x_ready, n["x"].next())
                    step(nc.scalar.activation(junk[:], x_tok[:, b, :], ACT.Square, accum_out=sq_tot[:, b:b + 1]))
                    nc.scalar.activation(std[:, b:b + 1], sq_tot[:, b:b + 1], ACT.Sqrt, bias=eps[:, 1:2],
                                         scale=1.0 / D).then_inc(std_ready, 1)

                def gained(g0):
                    for j in range(4):
                        bank = arrived()
                        for i in range(2):
                            last = nc.scalar.activation(xT[:, 2 * j + i, :], bank[:, i * S:(i + 1) * S], ACT.Copy,
                                                        scale=parL[:, g0 + 2 * j + i:g0 + 2 * j + i + 1])
                        last.then_inc(tile_taken, 1)

                def post_norm_roots():
                    for b in range(TB):
                        for h in range(2):
                            i = n["sum"].index
                            act.wait_ge(sum_ready, n["sum"].next())
                            last = nc.scalar.activation(junk[:, h * HALF:(h + 1) * HALF], sums[i % 4][:], ACT.Square,
                                                        accum_out=sq_sum[:, b, h:h + 1])
                        last.then_inc(square_ready, 1)
                        act.wait_ge(var_ready, n["var"].next())
                        nc.scalar.activation(std[:, b:b + 1], sq_tot[:, b:b + 1], ACT.Sqrt, bias=eps[:, 1:2],
                                             scale=1.0 / D).then_inc(std_ready, 1)

                act.wait_ge(lay_ready, n["lay"].next())
                for b in range(TB):
                    pre_norm_root(b)
                hand_over()
                gained(PAR_MIX_G)
                for _ in range(5):
                    n["tile"].next()
                hand_over()
                for b in range(TB):
                    bank = arrived()
                    nc.scalar.activation(at_v[:, b, :, 0:AT_D], bank[:].rearrange("p (h d) -> p h d", h=AT_H),
                                         ACT.Copy).then_inc(tile_taken, 1)
                for j in range(4):
                    bank = arrived()
                    nc.scalar.activation(conv[:, 2 * j:2 * j + 2, PAD:PAD + S],
                                         bank[:].rearrange("p (f t) -> p f t", f=2), ACT.Copy).then_inc(tile_taken, 1)
                for b in range(TB):
                    bank = arrived()
                    nc.scalar.activation(ml_v[:, b, :, 0:ML_D], bank[:].rearrange("p (h d) -> p h d", h=ML_H),
                                         ACT.Copy).then_inc(tile_taken, 1)
                copy_tiles(lambda b: ml_o[:, b, :], TB, ACT.Sigmoid)
                n["tile"].next(), n["tile"].next()
                act.wait_ge(forget_in, n["forget"].next())
                r = row[0:ML_H, 4, :, :].rearrange("p d t -> p (d t)")
                step(nc.scalar.activation(r, r, ACT.Exp))
                nc.scalar.activation(r, r, ACT.Ln, bias=1.0).then_inc(forget_log, 1)
                act.wait_ge(rows_ready, n["rows"].next())
                nc.scalar.activation(r, r, ACT.Exp).then_inc(floor_ready, 1)
                for f in range(8):
                    act.wait_ge(conv_ready, n["conv"].next())
                    nc.scalar.activation(ml_qk[:, f, :], ml_qk[:, f, :], ACT.Silu,
                                         bias=parL[:, PAR_TAP_B + f:PAR_TAP_B + f + 1]).then_inc(mqk_ready, 1)
                hand_over()
                copy_tiles(pair(headT), 4)
                for h in range(AT_H):
                    n["tile"].next(), n["tile"].next(), n["sum"].next()
                    act.wait_ge(p_in, n["pin"].next())
                    for b in range(TB):
                        last = nc.scalar.activation(at_p[h % 2][:, b, :], at_p[h % 2][:, b, :], ACT.Exp,
                                                    bias=neg_max[:, h % 2, b:b + 1])
                    last.then_inc(p_exp, 1)
                n["tile"].next()
                for h in range(ML_H):
                    act.wait_ge(tile_taken, n["tile"].next())
                    e = ml_e[h % 2].rearrange("p d s t -> p (d s t)")
                    nc.scalar.activation(e, e, ACT.Exp).then_inc(d_exp, 1)
                    n["tile"].next(), n["sum"].next(), n["sum"].next()
                act.wait_ge(var_ready, n["var"].next())
                nc.scalar.activation(std[:], sq_tot[:], ACT.Sqrt, bias=eps[:, 1:2], scale=1.0 / ML_D)\
                    .then_inc(std_ready, 1)
                hand_over()
                copy_tiles(pair(headT), 4)
                post_norm_roots()
                for b in range(TB):
                    pre_norm_root(b)
                gained(PAR_FFN_G)

                def ffn_middle(j):
                    bank = arrived()
                    for i in range(2):
                        f = i * FT + j
                        last = nc.scalar.activation(fconv[:, j % 2, i, :], bank[:, i * S:(i + 1) * S], ACT.Identity,
                                                    bias=parL[:, PAR_FTAP_B + f:PAR_FTAP_B + f + 1],
                                                    scale=parL[:, PAR_FTAP + 3 * f + 1:PAR_FTAP + 3 * f + 2])
                    last.then_inc(lin_ready, 1)

                def ffn_act(j):
                    act.wait_ge(gtap_ready, n["gtap"].next())
                    nc.scalar.activation(acted[:, j % 2, :], fconv[:, j % 2, 0, :], ACT.Gelu_apprx_tanh)\
                        .then_inc(acted_ready, 1)

                for s in range(FT + 1):
                    if s < FT:
                        if s >= 2:
                            act.wait_ge(h_ready, n["h"].next())
                        ffn_middle(s)
                    if s >= 1:
                        ffn_act(s - 1)
                n["h"].next(), n["h"].next()
                post_norm_roots()
            n.leave(LAYERS)

        @block.vector
        def _(vec):
            n = Counts("tile", "sum", "step", "std", "acted", "log", "wexp", "square", "gexp",
                       "flog", "dexp", "lin", "rot")
            tt, stt, ts = nc.vector.tensor_tensor, nc.vector.scalar_tensor_tensor, nc.vector.tensor_scalar

            def step(ins):
                ins.then_inc(vec_step, 1)
                vec.wait_ge(vec_step, n["step"].next())

            def arrived():
                i = n["tile"].index
                vec.wait_ge(tile_ready, n["tile"].next())
                return tiles[i % 4]

            def arrived_sum():
                i = n["sum"].index
                vec.wait_ge(sum_ready, n["sum"].next())
                return sums[i % 4]

            def hand_over():
                vec.wait_ge(tile_taken, n["tile"].value)

            def skip(count):
                for _ in range(count):
                    n["tile"].next()

            def layer_norm(k, experts=False):
                for b in range(TB):
                    for h in range(2):
                        xs = x_tok[:, b, h * HALF:(h + 1) * HALF]
                        if experts:
                            step(stt(xs, xs, ALPHA, y_tok[:, b, h * HALF:(h + 1) * HALF], ALU.mult, ALU.add))
                        else:
                            bank = arrived_sum()
                            stt(xs, xs, ALPHA, bank[:], ALU.mult, ALU.add).then_inc(sum_taken, 1)
                            vec.wait_ge(sum_taken, n["sum"].value)
                        last = nc.vector.bn_stats(stats[:, b, h, :], xs)
                    step(last)
                    nc.vector.bn_aggr(mean_var[:, b, :], stats[:, b, :, :].rearrange("p h s -> p (h s)"))\
                        .then_inc(var_ready, 1)
                vec.wait_ge(gain_in[k % 2], 32 * (k // 2 + 1))
                g = gain[:, (k % 2) * 2 * D:(k % 2) * 2 * D + D]
                shift = gain[:, (k % 2) * 2 * D + D:(k % 2) * 2 * D + 2 * D]
                for b in range(TB):
                    xs = x_tok[:, b, :]
                    vec.wait_ge(std_ready, n["std"].next())
                    step(nc.vector.reciprocal(rstd[:, b:b + 1], std[:, b:b + 1]))
                    step(ts(xs, xs, mean_var[:, b, 0:1], rstd[:, b:b + 1], ALU.subtract, ALU.mult))
                    step(tt(xs, xs, g, ALU.mult))
                    tt(xs, xs, shift, ALU.add).then_inc(x_ready, 1)

            def gated_tiles(count):
                for j in range(count):
                    bank = arrived()
                    vec.wait_ge(acted_ready, n["acted"].next())
                    tt(hT[:, j, :], acted[:, j % 2, :], bank[:, S:2 * S], ALU.mult).then_inc(tile_taken, 1)

            vec.wait_ge(consts_in, CONSTS_IN)
            skip(4)
            hand_over()
            cos = ret_rope[:, 0, :].unsqueeze(1).to_broadcast([P, 2, S])
            sin = ret_rope[:, 1, :].unsqueeze(1).to_broadcast([P, 2, S])
            for h in range(2 * RET_H):
                bank = arrived()[:].rearrange("p (i t) -> p i t", i=2)
                tt(ret_tmp[:, 0:2, :], bank, cos, ALU.mult)
                step(tt(ret_tmp[:, 2:4, :], bank, sin, ALU.mult))
                tt(headT[:, 2 * h, :], ret_tmp[:, 0, :], ret_tmp[:, 3, :], ALU.subtract)
                tt(headT[:, 2 * h + 1, :], ret_tmp[:, 2, :], ret_tmp[:, 1, :], ALU.add).then_inc(tile_taken, 1)
                vec.wait_ge(tile_taken, n["tile"].value)
            skip(16)
            hand_over()
            for h in range(RET_H):
                bank = arrived()
                tt(ret_p[:, h, :], bank[:, 0:3 * P], ret_decay[:, h, :], ALU.mult).then_inc(tile_taken, 1)
            for g in range(RET_H * TB // 4):
                got = []
                for i in range(4):
                    bank = arrived()
                    got.append(bank)
                    step(nc.vector.bn_stats(stats[:, i, 0, :], bank[:]))
                    nc.vector.bn_aggr(mean_var[:, i, :], stats[:, i, 0, :]).then_inc(var_ready, 1)
                for i in range(4):
                    h, b = (4 * g + i) // TB, i % TB
                    o = ret_tmp[:, (i % 2) * 2:(i % 2) * 2 + 2, :].rearrange("p i t -> p (i t)")
                    gs = g_tok[:, b, h * HALF:(h + 1) * HALF]
                    vec.wait_ge(std_ready, n["std"].next())
                    step(nc.vector.reciprocal(rstd[:, i:i + 1], std[:, 4 + i:5 + i]))
                    ts(o, got[i][:], mean_var[:, i, 0:1], rstd[:, i:i + 1], ALU.subtract, ALU.mult)\
                        .then_inc(tile_taken, 1)
                    vec.wait_ge(tile_taken, n["tile"].value - 3 + i)
                    tt(gs, gs, o, ALU.mult).then_inc(og_ready, 1)
            skip(8)
            layer_norm(0)
            skip(4)
            hand_over()
            gated_tiles(FT)
            layer_norm(1)
            skip(4)

            skip(8 + 4)
            hand_over()
            mask2 = earlier[:].unsqueeze(1).to_broadcast([P, 2, P])
            zs = {}

            def edge(t):
                return t.rearrange("p (i n) -> p i n", i=3)[:, 0:3:2, :]

            def sb_abs(h):
                zs[h] = bank = tiles[(first + h) % 4]
                vec.wait_ge(z_ready, h + 1)
                size = sb_size[:, h % 4, :]
                step(ts(size, bank[:, 0:384], 0.0, None, ALU.min))
                stt(size, bank[:, 0:384], 0.0, size, ALU.max, ALU.subtract).then_inc(abs_ready, 1)

            def sb_soft(h):
                keep = sb_keep[:, h % 4, :]
                vec.wait_ge(log_ready, n["log"].next())
                step(stt(keep, zs[h][:, 0:384], 0.0, sb_e[:, h % 4, :], ALU.max, ALU.add))
                tt(edge(keep), edge(keep), mask2, ALU.mult).then_inc(keep_ready, 1)

            def sb_bound(h):
                bank = arrived()
                ts(sb_w[:, h % 4, :], bank[:, 0:384], 0.0, None, ALU.min).then_inc(tile_taken, 1)

            def sb_mask(h):
                vec.wait_ge(wexp_ready, n["wexp"].next())
                w = sb_w[:, h % 4, :]
                tt(edge(w), edge(w), mask2, ALU.mult).then_inc(w_ready, 1)

            first = n["tile"].index
            for s in range(SB_H + 3):
                if s < SB_H:
                    sb_abs(s)
                if 1 <= s <= SB_H:
                    sb_soft(s - 1)
                if 2 <= s <= SB_H + 1:
                    sb_bound(s - 2)
                if s >= 3:
                    sb_mask(s - 3)
            for _ in range(SB_H // 2):
                n["sum"].next()
            layer_norm(2)
            skip(4)

            hand_over()
            bank = arrived()
            nc.vector.tensor_copy(logits[:].rearrange("p b e -> p (b e)"), bank[:, 0:TB * EXPERTS]).then_inc(tile_taken, 1)
            vec.wait_ge(tile_taken, n["tile"].value)
            for e in range(EXPERTS):
                rival = logits[:, :, e:e + 1]
                tt(beaten[:, :, 0:e + 1, e], logits[:, :, 0:e + 1], rival.to_broadcast([P, TB, e + 1]), ALU.is_lt)
                if e < EXPERTS - 1:
                    tt(beaten[:, :, e + 1:, e], logits[:, :, e + 1:],
                       rival.to_broadcast([P, TB, EXPERTS - 1 - e]), ALU.is_le)
            step(nc.vector.tensor_reduce(top[:, :, 0], logits[:], AX.X, ALU.max))
            step(nc.vector.tensor_reduce(rank[:], beaten[:], AX.X, ALU.add))
            ts(rank[:], rank[:], float(2), None, ALU.is_lt)
            tt(gate[:], logits[:], top[:, :, 0:1].to_broadcast([P, TB, EXPERTS]), ALU.subtract).then_inc(gexp_in, 1)
            nc.vector.memset(y_tok[:].rearrange("p b n -> p (b n)"), 0.0)
            vec.wait_ge(gexp_ready, n["gexp"].next())
            step(tt(gate[:], gate[:], rank[:], ALU.mult))
            step(nc.vector.tensor_reduce(top[:, :, 1], gate[:], AX.X, ALU.add))
            step(nc.vector.reciprocal(top[:, :, 1], top[:, :, 1]))
            step(tt(gate[:], gate[:], top[:, :, 1:2].to_broadcast([P, TB, EXPERTS]), ALU.mult))
            with vec.Fori(0, EXPERTS) as e:
                n.enter(e, tile=ET, sum=4, acted=ET, step=1)
                step(nc.vector.tensor_copy(gate_e[:], gate[:, :, bass.ds(e, 1)].rearrange("p b e -> p (b e)")))
                gated_tiles(ET)
                for b in range(TB):
                    for h in range(2):
                        bank = arrived_sum()
                        ys = y_tok[:, b, h * HALF:(h + 1) * HALF]
                        stt(ys, bank[:], gate_e[:, b:b + 1], ys, ALU.mult, ALU.add).then_inc(sum_taken, 1)
                vec.wait_ge(sum_taken, n["sum"].value)
            n.leave(EXPERTS)
            layer_norm(3, experts=True)

            with vec.Fori(0, LAYERS) as l:
                n.enter(l, tile=LAYER_TURN["tile"], sum=LAYER_TURN["sum"], std=2 * 4 + 1, square=4, acted=FT,
                        flog=1, dexp=ML_H, lin=FT, rot=2, step=VEC_STEPS)
                nc.vector.memset(conv[:, :, 0:PAD], 0.0)
                nc.vector.memset(conv[:, :, PAD + S:], 0.0)
                nc.vector.memset(at_v[:, :, :, AT_D:VA], 1.0)
                nc.vector.memset(ml_v[:, :, :, ML_D:VM], 1.0)
                nc.vector.tensor_copy(parL[:], par[:, bass.ds(l, 1), :].rearrange("p l n -> p (l n)"))
                nc.vector.tensor_copy(gates_wL[:], gates_w[:, bass.ds(l, 1), :].rearrange("p l n -> p (l n)"))
                nc.vector.tensor_copy(gate_biasL[0:ML_H, :], gate_bias[0:ML_H, bass.ds(l, 1), :].rearrange("p l n -> p (l n)"))\
                    .then_inc(lay_ready, 1)

                def layer_gain(at, w):
                    return gain[:, bass.ds(l * GAINS + at, w)]

                def pre_norm():
                    for b in range(TB):
                        vec.wait_ge(std_ready, n["std"].next())
                        step(nc.vector.reciprocal(rstd[:, b:b + 1], std[:, b:b + 1]))
                        ts(y_tok[:, b, :], x_tok[:, b, :], rstd[:, b:b + 1], None, ALU.mult).then_inc(tok_ready, 1)

                def post_norm(at):
                    for b in range(TB):
                        got = [sums[(n["sum"].index + h) % 4] for h in range(2)]
                        n["sum"].more(2)
                        vec.wait_ge(sum_ready, n["sum"].value)
                        vec.wait_ge(square_ready, n["square"].next())
                        nc.vector.tensor_reduce(sq_tot[:, b:b + 1], sq_sum[:, b, :], AX.X, ALU.add).then_inc(var_ready, 1)
                        vec.wait_ge(std_ready, n["std"].next())
                        step(nc.vector.reciprocal(rstd[:, b:b + 1], std[:, b:b + 1]))
                        for h in range(2):
                            stt(y_tok[:, b, h * HALF:(h + 1) * HALF], got[h][:], rstd[:, b:b + 1],
                                layer_gain(at + h * HALF, HALF), ALU.mult, ALU.mult).then_inc(sum_taken, 1)
                        vec.wait_ge(sum_taken, n["sum"].value)
                        tt(x_tok[:, b, :], x_tok[:, b, :], y_tok[:, b, :], ALU.add).then_inc(x_ready, 1)

                pre_norm()
                skip(4)
                hand_over()
                bank = arrived()
                nc.vector.tensor_copy(gate_tok[:].rearrange("p b g -> p (b g)"), bank[:, 0:TB * 16]).then_inc(tile_taken, 1)
                for i in range(2):
                    for b in range(TB):
                        bank = arrived()[:].rearrange("p (h c n) -> p h c n", h=AT_H, c=2)
                        dst = rot[:, i, b, :].rearrange("p (h c n) -> p h c n", h=AT_H, c=2)
                        for t in range(2):
                            tr = rope[:, b, t, :].unsqueeze(1).to_broadcast([P, AT_H, AT_D // 2])
                            for c in range(2):
                                last = tt(rot_tmp[:, t, :, c, :], bank[:, :, c, :], tr, ALU.mult)
                        last.then_inc(tile_taken, 1)
                        vec.wait_ge(tile_taken, n["tile"].value)
                        tt(dst[:, :, 0, :], rot_tmp[:, 0, :, 0, :], rot_tmp[:, 1, :, 1, :], ALU.subtract)
                        last = tt(dst[:, :, 1, :], rot_tmp[:, 0, :, 1, :], rot_tmp[:, 1, :, 0, :], ALU.add)
                        if b == 0:
                            step(last)
                    last.then_inc(rot_ready, 1)
                    vec.wait_ge(rot_ready, n["rot"].next())
                skip(2)
                for j in range(4):
                    vec.wait_ge(tile_taken, n["tile"].next())
                    for t in range(ML_TAPS):
                        for f in (2 * j, 2 * j + 1):
                            w = parL[:, PAR_TAP + f * ML_TAPS + t:PAR_TAP + f * ML_TAPS + t + 1]
                            if t == 0:
                                last = ts(ml_qk[:, f, :], conv[:, f, 0:S], w, None, ALU.mult)
                            else:
                                last = stt(ml_qk[:, f, :], conv[:, f, t:t + S], w, ml_qk[:, f, :], ALU.mult, ALU.add)
                            if t == ML_TAPS - 1:
                                last.then_inc(conv_ready, 1)
                        if t < ML_TAPS - 1:
                            step(last)
                skip(4)
                hand_over()
                li, lf, lw, mx, tmp = [row[0:ML_H, i, :, :] for i in range(5)]
                for kind, dst in ((0, li), (1, lf)):
                    bank = arrived()
                    for d in range(2):
                        last = ts(dst[:, d, :], bank[0:ML_H, d * S:(d + 1) * S],
                                  gate_biasL[0:ML_H, 2 * d + kind:2 * d + kind + 1], None, ALU.add)
                    last.then_inc(tile_taken, 1)
                vec.wait_ge(tile_taken, n["tile"].value)
                stt(tmp, lf, -1.0, lf, ALU.mult, ALU.min).then_inc(forget_in, 1)
                vec.wait_ge(forget_log, n["flog"].next())
                step(stt(lf, lf, 0.0, tmp, ALU.min, ALU.subtract))
                scan = nc.vector.tensor_tensor_scan
                one = ones_row[0:ML_H, :]
                scan(tmp[:, 0, :], one, lf[:, 0, :], 0.0, ALU.mult, ALU.add)
                step(scan(tmp[:, 1, ::-1], one, lf[:, 1, ::-1], 0.0, ALU.mult, ALU.add))
                step(tt(lw, li, tmp, ALU.subtract))
                scan(mx[:, 0, :], lw[:, 0, :], lw[:, 0, :], 0.0, ALU.max, ALU.max)
                step(scan(mx[:, 1, ::-1], lw[:, 1, ::-1], lw[:, 1, ::-1], 0.0, ALU.max, ALU.max))
                stt(tmp, tmp, -1.0, mx, ALU.mult, ALU.subtract).then_inc(rows_ready, 1)
                skip(4)
                hand_over()

                def at_mask(h):
                    bank = arrived()
                    p = at_p[h % 2]
                    stt(p.rearrange("p b s -> p (b s)"), bank[:], AT_D ** -0.5,
                        reach[:].rearrange("p b s -> p (b s)"), ALU.mult, ALU.add).then_inc(tile_taken, 1)
                    vec.wait_ge(tile_taken, n["tile"].value)
                    step(nc.vector.tensor_reduce(neg_max[:, h % 2, :], p, AX.X, ALU.max))
                    ts(neg_max[:, h % 2, :], neg_max[:, h % 2, :], -1.0, None, ALU.mult).then_inc(p_in, 1)

                def at_weight(h):
                    bank = arrived()
                    tt(at_pT[h % 2].rearrange("p b t -> p (b t)"), bank[:], windows[:].rearrange("p b t -> p (b t)"),
                       ALU.mult).then_inc(tile_taken, 1)

                def at_norm(h):
                    got = arrived_sum()[:, 0:TB * VA].rearrange("p (b d) -> p b d", b=TB)
                    step(nc.vector.reciprocal(den[:, 2 + h % 2, :], got[:, :, AT_D]))
                    for b in range(TB):
                        last = ts(o_tok[:, b, h * AT_D:(h + 1) * AT_D], got[:, b, 0:AT_D], den[:, 2 + h % 2, b:b + 1], None, ALU.mult)
                    last.then_inc(sum_taken, 1)

                for s in range(AT_H + 2):
                    if s < AT_H:
                        at_mask(s)
                    if 1 <= s <= AT_H:
                        at_weight(s - 1)
                    if s >= 2:
                        at_norm(s - 2)

                bank = arrived()
                nc.vector.tensor_copy(ml_col[:].rearrange("p k d b h -> p (k d b h)"), bank[:, 0:8 * ML_H])\
                    .then_inc(tile_taken, 1)
                vec.wait_ge(tile_taken, n["tile"].value)

                def ml_decay(h):
                    bank = arrived()
                    e = ml_e[h % 2]
                    for d in range(2):
                        for kb in range(TB):
                            last = ts(e[:, d, kb, :], bank[:, d * S:(d + 1) * S], ml_col[:, 0, d, kb, h:h + 1], 0.0,
                                      ALU.add, ALU.min)
                    last.then_inc(tile_taken, 1)
                    vec.wait_ge(d_exp, n["dexp"].next())
                    flat = e.rearrange("p d s t -> p (d s t)")
                    step(tt(flat, flat, ml_mask[:].rearrange("p d s t -> p (d s t)"), ALU.mult))
                    bank = arrived()
                    both = e.rearrange("p d s t -> p d (s t)")
                    tt(both, both, bank[:].unsqueeze(1).to_broadcast([P, 2, HALF]), ALU.mult).then_inc(tile_taken, 1)

                def ml_norm(h):
                    for d in range(2):
                        got = arrived_sum()[:, 0:TB * VM].rearrange("p (b d) -> p b d", b=TB)
                        step(nc.vector.tensor_copy(den[:, d, :], got[:, :, ML_D]))
                        step(stt(den[:, d, :], den[:, d, :], -1.0, den[:, d, :], ALU.mult, ALU.max))
                        step(tt(den[:, d, :], den[:, d, :], ml_col[:, 1, d, :, h], ALU.max))
                        step(nc.vector.reciprocal(den[:, d, :], den[:, d, :]))
                        for b in range(TB):
                            o = o_tok[:, b, AT_W + h * ML_D:AT_W + (h + 1) * ML_D]
                            if d == 0:
                                last = ts(o, got[:, b, 0:ML_D], den[:, d, b:b + 1], None, ALU.mult)
                            else:
                                last = stt(o, got[:, b, 0:ML_D], den[:, d, b:b + 1], o, ALU.mult, ALU.add)
                        last.then_inc(sum_taken, 1)
                        vec.wait_ge(sum_taken, n["sum"].value)

                for s in range(ML_H + 1):
                    if s < ML_H:
                        ml_decay(s)
                    if s >= 1:
                        ml_norm(s - 1)
                hm = o_tok[:, :, AT_W:]
                sq = y_tok[:, :, 0:ML_W]
                step(tt(sq, hm, hm, ALU.mult))
                nc.vector.tensor_reduce(sq_tot[:].rearrange("p (b h) -> p b h", b=TB),
                                        sq.rearrange("p b (h d) -> p b h d", h=ML_H), AX.X, ALU.add).then_inc(var_ready, 1)
                vec.wait_ge(gains_in, 16 * 3 * LAYERS)
                for b in range(TB):
                    last = tt(ml_o[:, b, :], ml_o[:, b, :], layer_gain(2 * D, ML_W), ALU.mult)
                vec.wait_ge(std_ready, n["std"].next())
                step(nc.vector.reciprocal(rstd[:], std[:]))
                for b in range(TB):
                    last = tt(hm[:, b, :].rearrange("p (h d) -> p h d", h=ML_H),
                              hm[:, b, :].rearrange("p (h d) -> p h d", h=ML_H),
                              rstd[:, b * ML_H:(b + 1) * ML_H].unsqueeze(2).to_broadcast([P, ML_H, ML_D]), ALU.mult)
                step(last)
                tt(hm, hm, ml_o, ALU.mult).then_inc(mixed_ready, 1)
                skip(4)
                post_norm(0)
                pre_norm()
                skip(4)
                hand_over()

                def ffn_taps(j):
                    bank = arrived()
                    vec.wait_ge(lin_ready, n["lin"].next())
                    c = fconv[:, j % 2, :, :]
                    for i in range(2):
                        w = PAR_FTAP + FF_TAPS * (i * FT + j)
                        last = stt(c[:, i, 1:S], bank[:, i * S:i * S + S - 1], parL[:, w:w + 1], c[:, i, 1:S],
                                   ALU.mult, ALU.add)
                    step(last)
                    for i in range(2):
                        w = PAR_FTAP + FF_TAPS * (i * FT + j) + 2
                        last = stt(c[:, i, 0:S - 1], bank[:, i * S + 1:(i + 1) * S], parL[:, w:w + 1], c[:, i, 0:S - 1],
                                   ALU.mult, ALU.add)
                        last.then_inc(gtap_ready if i == 0 else tile_taken, 1)
                    taken[j] = n["tile"].value

                def ffn_mul(j):
                    vec.wait_ge(acted_ready, n["acted"].next())
                    vec.wait_ge(tile_taken, taken[j])
                    tt(hT[:, j, :], acted[:, j % 2, :], fconv[:, j % 2, 1, :], ALU.mult).then_inc(h_ready, 1)

                taken = {}
                for s in range(FT + 1):
                    if s < FT:
                        ffn_taps(s)
                    if s >= 1:
                        ffn_mul(s - 1)
                post_norm(D)
            n.leave(LAYERS)


def constants():
    f32 = np.float32
    c = {}
    r = np.arange(P)
    c["c_ident"] = np.eye(P, dtype=f32)
    c["c_suffix"] = -np.stack([r[:, None] >= r[None, :], np.ones((P, P), bool)], 1).astype(f32).reshape(P, -1)
    c["c_earlier"] = (r[:, None] < r[None, :]).astype(f32)
    t = np.arange(S, dtype=f32)

    def angles(d, base):
        inv = (1.0 / (base ** (np.arange(0, d, 2, dtype=f32) / f32(d)))).astype(f32)
        return (t[:, None] * inv[None, :]).astype(f32).astype(np.float64)

    ang = angles(AT_D, 10000.0)
    c["c_rope"] = np.stack([np.cos(ang), np.sin(ang)], 1).reshape(TB, P, -1).transpose(1, 0, 2).reshape(P, -1).astype(f32)
    ang = angles(D // RET_H, 10000.0).T
    c["c_ret_rope"] = np.concatenate([np.cos(ang), np.sin(ang)], 1).astype(f32)
    ti, si = np.arange(S)[:, None], np.arange(S)[None, :]
    held = [(np.abs(ti - si) <= w // (2 * d) * d) & ((ti - si) % d == 0) for w, d in ((128, 1), (512, 4), (2048, 16))]
    count = sum(h.astype(f32) for h in held)
    c["c_windows"] = count.reshape(TB, P, S).transpose(1, 0, 2).reshape(P, -1)
    c["c_reach"] = np.where(c["c_windows"] > 0, 0.0, NEG).astype(f32)
    seen = np.stack([si.T <= ti.T, si.T >= ti.T]) * ML_D ** -0.5
    c["c_ml_mask"] = seen.reshape(2, TB, P, S).transpose(2, 0, 1, 3).reshape(P, -1).astype(f32)
    c["c_neg_row"] = -np.repeat(np.eye(ML_H, dtype=f32), P, axis=1)
    gamma = 1.0 - 2.0 ** (-5.0 - np.arange(RET_H))
    full = np.where(si.T // CHUNK <= ti.T // CHUNK, gamma[:, None, None] ** np.abs(ti.T - si.T), 0.0)
    full = full * (D // RET_H) ** -0.5
    dec = np.concatenate([full[:, :P, :], full[:, P:, P:]], axis=2)
    c["c_decay"] = dec.transpose(1, 0, 2).reshape(P, -1).astype(f32)
    return {k: np.ascontiguousarray(v) for k, v in c.items()}


def feature_chunks(w):
    return w.reshape(KT, P, -1, 256).transpose(2, 1, 0, 3).reshape(-1, P, SLOT)


def paired_chunks(w):
    lead = w.shape[:-2]
    w = w.reshape(*lead, KT, P, 2, -1, P)
    k = len(lead)
    w = w.transpose(*range(k), k + 3, k + 1, k, k + 2, k + 4)
    return w.reshape(*lead, -1, P, SLOT)


def token_chunks(w):
    return w.reshape(2, KT // 2, P, -1, HALF).transpose(3, 0, 2, 1, 4).reshape(-1, 2, P, SLOT)


def by_partition(w, *lead):
    w = w.reshape(w.shape[0], -1, w.shape[-1] // P, P)
    return w.transpose(3, 0, 2, 1).reshape(P, w.shape[0], -1)


def layout(i):
    o = {name: i[name] for name in ("x", "ret_w_out", "ffn_w_out", "sb_w_out", "moe_w_out", "ln_mix_g", "ln_mix_b",
                                    "ln_ffn_g", "ln_ffn_b", "w_out_2", "w_down_2", "mix_post_g_2", "ffn_post_g_2",
                                    "mlstm_head_g_2")}
    o["ret_qk"] = feature_chunks(i["ret_w_in"][0][:, :2 * D])
    o["ret_vg"] = token_chunks(i["ret_w_in"][0][:, 2 * D:])
    o["ffn_up"] = paired_chunks(i["ffn_w_in"][0])
    o["sb_k"] = feature_chunks(i["sb_w_kv"][:, :D])
    o["sb_v"] = token_chunks(i["sb_w_kv"][:, D:])
    o["sb_q"] = feature_chunks(i["sb_w_q"][0])
    o["moe_up"] = paired_chunks(i["moe_w_in"][0])
    o["router_w"] = i["moe_w_router"][0].reshape(KT, P, EXPERTS).transpose(1, 0, 2).reshape(P, -1)
    w = i["w_in_2"]
    a3, m2, m4 = 3 * AT_W, 3 * AT_W + 2 * ML_W, 3 * AT_W + 4 * ML_W
    o["w2_attn"] = np.stack([token_chunks(w[l][:, :a3]) for l in range(LAYERS)])
    o["w2_mqk"] = np.stack([feature_chunks(w[l][:, a3:m2]) for l in range(LAYERS)])
    o["w2_mvo"] = np.stack([token_chunks(w[l][:, m2:m4]) for l in range(LAYERS)])
    o["gates_w"] = w[:, :, m4:].reshape(LAYERS, KT, P, 16).transpose(2, 0, 1, 3).reshape(P, -1)
    o["gate_bias"] = i["mlstm_gate_b_2"].reshape(LAYERS, 4, ML_H).transpose(2, 0, 1).reshape(ML_H, -1)
    o["w2_up"] = paired_chunks(i["w_up_2"])
    o["mix_pre_g"] = by_partition(i["mix_pre_g_2"])
    o["ffn_pre_g"] = by_partition(i["ffn_pre_g_2"])
    o["taps"] = by_partition(i["mlstm_conv_w_2"])
    o["taps_b"] = by_partition(i["mlstm_conv_b_2"])
    o["ffn_taps"] = by_partition(i["ffn_conv_w_2"])
    o["ffn_taps_b"] = by_partition(i["ffn_conv_b_2"])
    return {k: np.ascontiguousarray(v) for k, v in o.items()}


def kernel(**inputs):
    import concourse.bacc as bacc
    from concourse.bass_utils import run_bass_kernel_spmd

    nc = bacc.Bacc("TRN2", target_bir_lowering=False, num_devices=1)
    arrays = layout({k: np.asarray(v) for k, v in inputs.items()}) | constants()
    arrays = {f"in_{k}": v for k, v in arrays.items()}
    aps = {k[3:]: nc.dram_tensor(k, v.shape, mybir.dt.from_np(v.dtype), kind="ExternalInput").ap()
           for k, v in arrays.items()}
    out = nc.dram_tensor("out", (1, S, D), F32, kind="ExternalOutput").ap()
    program(nc, aps, out)
    return run_bass_kernel_spmd(nc, [arrays], core_ids=[0]).results[0]["out"]
```

```python
from contextlib import ExitStack

import numpy as np

import concourse.bass as bass
from concourse import mybir

ACT_STEPS, VEC_STEPS = 5, 107

P = 128
D = 1024
S = 256
TB = S // P
KT = D // P
HALF = 512
F32 = mybir.dt.float32
ALU = mybir.AluOpType
ACT = mybir.ActivationFunctionType
AX = mybir.AxisListType

SLOTS = 6
SLOT = 2048

RET_H, RET_V = 4, 2048
SB_H = 16
FF = 2816
FT = FF // P
EXPERTS = 8
EF = 3584
ET = EF // P
ALPHA = 4.0 ** 0.25
LN_EPS = 1e-5
LAYERS = 2
AT_H, AT_D, AT_W = 8, 64, 512
ML_H, ML_D, ML_W = 4, 128, 512
ML_TAPS, FF_TAPS = 5, 3
PAD = ML_TAPS // 2
RMS_EPS = 1e-6
NEG = -1e30
CHUNK = 64

RET_ROWS = [2] * (RET_V // P // 2)
MIX_ROWS = [2] * (KT // 2)
FFN_ROWS = [2] * (FT // 2)
EXPERT_ROWS = [2] * (ET // 2)
EG = EF // HALF
LAYER_ROWS = [2] * (FT // 2)

PAR_MIX_G, PAR_FFN_G, PAR_TAP, PAR_TAP_B = 0, KT, 2 * KT, 2 * KT + 8 * ML_TAPS
PAR_FTAP = PAR_TAP_B + 8
PAR_FTAP_B = PAR_FTAP + 2 * FT * FF_TAPS
PARS = PAR_FTAP_B + 2 * FT
GAINS = 2 * D + ML_W
DECAY = RET_H * 3 * P

PAIR_TURN = dict(chunk=2 * (4 * EG + len(EXPERT_ROWS)), tile=2 * (3 * EG + 3), sum=2 * 6)
LAYER_TURN = dict(chunk=9 + 4 + 4 + len(MIX_ROWS) + FT + len(LAYER_ROWS), tile=80, sum=24)
assert all(t["chunk"] % SLOTS == 0 and t["tile"] % 4 == 0 and t["sum"] % 4 == 0
           for t in (PAIR_TURN, LAYER_TURN))


MOE_SUMS = 4 + 4 + SB_H // 2 + 4 + EXPERTS // 2 * PAIR_TURN["sum"]


class Count:

    def __init__(self, group=1, unit=1):
        self.index, self.skew, self.group, self.unit = 0, 0, group, unit

    @property
    def value(self):
        return self.skew + self.unit * (self.index // self.group)

    def next(self):
        self.index += 1
        return self.value

    def more(self, count):
        self.index += count

    def enter(self, turn, per_turn):
        self.began, self.before, self.per_turn = self.index, self.skew, per_turn
        self.skew = turn * (per_turn * self.unit // self.group) + self.before

    def leave(self, turns):
        assert self.index - self.began == self.per_turn, (self.index - self.began, self.per_turn)
        self.skew = self.before + (turns - 1) * self.per_turn * self.unit // self.group


class Counts(dict):

    def __init__(self, *names, **made):
        for name in names:
            self[name] = Count()
        self.update(made)

    def enter(self, turn, **per_turn):
        self.inside = per_turn
        for name, events in per_turn.items():
            self[name].enter(turn, events)

    def leave(self, turns):
        for name in self.inside:
            self[name].leave(turns)


class Flow:

    def __init__(self, sem, tag):
        self.landed = [sem(f"{tag}landed{i}") for i in range(SLOTS)]
        self.w_used = sem(tag + "w_used")
        self.tile_ready = sem(tag + "tile_ready")
        self.tile_taken = sem(tag + "tile_taken")
        self.sum_ready = sem(tag + "sum_ready")
        self.sum_taken = sem(tag + "sum_taken")
        self.choice_ready = sem(tag + "choice_ready")
        self.vec_step = sem(tag + "vec_step")
        self.act_step = sem(tag + "act_step")


def program(nc, a, out):
    with ExitStack() as ctx:
        def sb(name, *shape):
            return ctx.enter_context(nc.sbuf_tensor(name, [P, *shape], F32))

        def sem(name):
            return ctx.enter_context(nc.semaphore(name))

        ring = sb("ring", SLOTS, SLOT)
        ident = sb("ident", P)
        suffix = sb("suffix", 2, P)
        earlier = sb("earlier", P)
        rope = sb("rope", TB, 2, AT_D // 2)
        reach = sb("reach", TB, S)
        windows = sb("windows", TB, S)
        ml_mask = sb("ml_mask", 2, TB, S)
        neg_row = sb("neg_row", ML_H, P)
        ones_row = sb("ones_row", S)
        x_tok = sb("x_tok", TB, D)
        y_tok = sb("y_tok", TB, D)
        xT = sb("xT", KT, S)
        headT = sb("headT", 2 * KT, S)
        v_tok = sb("v_tok", TB * RET_V)
        g_tok = sb("g_tok", TB, RET_V)
        hT = sb("hT", ET, S)
        gain = sb("gain", 2 * GAINS)
        par = sb("par", LAYERS, PARS)
        parL = sb("parL", PARS)
        gate_bias = sb("gate_bias", LAYERS, 4)
        gate_biasL = sb("gate_biasL", 4)
        router_w = sb("router_w", KT, EXPERTS)
        gates_w = sb("gates_w", LAYERS, KT * 16)
        gates_wL = sb("gates_wL", KT * 16)
        acted = sb("acted", 2, HALF)
        junk = sb("junk", D)
        stats = sb("stats", 4, 2, 6)
        mean_var = sb("mean_var", 4, 2)
        std = sb("std", 8)
        rstd = sb("rstd", 8)
        sq_sum = sb("sq_sum", TB, 2)
        sq_tot = sb("sq_tot", 8)
        eps = sb("eps", 2)
        logits = sb("logits", TB, EXPERTS)
        beaten = sb("beaten", TB, EXPERTS, EXPERTS)
        rank = sb("rank", TB, EXPERTS)
        top = sb("top", TB, 2)
        gate = sb("gate", TB, EXPERTS)
        route = sb("route", 3, TB, EXPERTS + 1)
        route_e = sb("route_e", 2, 3 * TB)
        places = sb("places", 2, P)
        most = ctx.enter_context(nc.sbuf_tensor("most", [P, 1], mybir.dt.int32))

        hflat = hT[:].rearrange("p k t -> p (k t)")
        gflat = g_tok[:].rearrange("p b n -> p (b n)")
        yflat = y_tok[:].rearrange("p b n -> p (b n)")
        tflat = headT[:].rearrange("p k t -> p (k t)")

        ret_decay = hflat[:, 0:DECAY].rearrange("p (h n) -> p h n", h=RET_H)
        ret_rope = hflat[:, DECAY:DECAY + 2 * S].rearrange("p (i t) -> p i t", i=2)
        ret_p = hflat[:, 2048:2048 + DECAY].rearrange("p (h n) -> p h n", h=RET_H)
        ret_tmp = hflat[:, 4096:4096 + 4 * S].rearrange("p (i t) -> p i t", i=4)
        ret_v = v_tok[:].rearrange("p (b n) -> p b n", b=TB)
        sb_v = v_tok[:, 0:TB * D].rearrange("p (b n) -> p b n", b=TB)
        sb_w, sb_keep, sb_e, sb_size = [hflat[:, i * 1536:(i + 1) * 1536].rearrange("p (i n) -> p i n", i=4)
                                     for i in range(3)] + [gflat[:, 0:1536].rearrange("p (i n) -> p i n", i=4)]
        choice = tflat[:, 0:512].rearrange("p (i b j) -> p i b j", i=2, b=TB)
        choiceT = tflat[:, 512:1024].rearrange("p (i b t) -> p i b t", i=2, b=TB)
        chosenT = tflat[:, 1024:3072].rearrange("p (i k j) -> p i k j", i=2, k=KT)
        h_tok = tflat[:, 3072:4096].rearrange("p (i n) -> p i n", i=2)
        eT = hflat[:, 0:ET * P].rearrange("p (k j) -> p k j", k=ET)
        rows_e = v_tok[:, 0:D]
        rot = gflat[:, 0:2 * TB * AT_W].rearrange("p (i b n) -> p i b n", i=2, b=TB)
        o_tok = gflat[:, 2 * TB * AT_W:4 * TB * AT_W].rearrange("p (b n) -> p b n", b=TB)
        rot_tmp = yflat[:, 0:2 * AT_W].rearrange("p (i h c n) -> p i h c n", i=2, h=AT_H, c=2)
        at_p = [tflat[:, 2048 + i * 512:2560 + i * 512].rearrange("p (b s) -> p b s", b=TB) for i in range(2)]
        at_pT = [tflat[:, 3072 + i * 512:3584 + i * 512].rearrange("p (b t) -> p b t", b=TB) for i in range(2)]
        VA = AT_D + 1
        at_v = v_tok[:, 0:TB * AT_H * VA].rearrange("p (b h d) -> p b h d", b=TB, h=AT_H)
        V0 = TB * AT_H * VA
        VM = ML_D + 1
        ml_v = v_tok[:, V0:V0 + TB * ML_H * VM].rearrange("p (b h d) -> p b h d", b=TB, h=ML_H)
        V1 = V0 + TB * ML_H * VM
        ml_o = v_tok[:, V1:V1 + TB * ML_W].rearrange("p (b n) -> p b n", b=TB)
        conv = hflat[:, 0:8 * (S + 2 * PAD)].rearrange("p (f t) -> p f t", f=8)
        ml_qk = hflat[:, 2080:2080 + 8 * S].rearrange("p (f t) -> p f t", f=8)
        ml_e = [hflat[:, 4128 + i * 1024:5152 + i * 1024].rearrange("p (d s t) -> p d s t", d=2, s=TB)
                for i in range(2)]
        row = sb("row", 5, 2, S)
        gate_tok = sb("gate_tok", TB, 16)
        ml_col = sb("ml_col", 2, 2, TB, ML_H)
        neg_max = sb("neg_max", 2, TB)
        den = sb("den", 4, TB)
        fconv = tflat[:, 0:4 * S].rearrange("p (i c t) -> p i c t", i=2, c=2)

        banks = [ctx.enter_context(nc.psum_tensor(f"bank{i}", [P, HALF], F32)) for i in range(8)]
        sums, tiles = banks[:4], banks[4:]

        main = Flow(sem, "")
        crowd = Flow(sem, "crowd_")
        consts_in = sem("consts_in")
        x_in = sem("x_in")
        gain_in = [sem(f"gain_in{i}") for i in range(2)]
        gains_in = sem("gains_in")
        eps_set = sem("eps_set")
        var_ready = sem("var_ready")
        std_ready = sem("std_ready")
        square_ready = sem("square_ready")
        chosen_ready = sem("chosen_ready")
        most_ready = sem("most_ready")
        x_ready = sem("x_ready")
        tok_ready = sem("tok_ready")
        og_ready = sem("og_ready")
        acted_ready = sem("acted_ready")
        z_ready = sem("z_ready")
        abs_ready = sem("abs_ready")
        log_ready = sem("log_ready")
        keep_ready = sem("keep_ready")
        wexp_ready = sem("wexp_ready")
        w_ready = sem("w_ready")
        gexp_in = sem("gexp_in")
        gexp_ready = sem("gexp_ready")
        lay_ready = sem("lay_ready")
        rot_ready = sem("rot_ready")
        conv_ready = sem("conv_ready")
        mqk_ready = sem("mqk_ready")
        forget_in = sem("forget_in")
        forget_log = sem("forget_log")
        rows_ready = sem("rows_ready")
        floor_ready = sem("floor_ready")
        p_in = sem("p_in")
        p_exp = sem("p_exp")
        d_exp = sem("d_exp")
        mixed_ready = sem("mixed_ready")
        lin_ready = sem("lin_ready")
        gtap_ready = sem("gtap_ready")
        h_ready = sem("h_ready")
        out_done = sem("out_done")

        block = ctx.enter_context(nc.Block())

        @block.sync
        def _(sp):
            n, flow = Counts("chunk"), main

            def load(src, kt=None, cols=SLOT, in_loop=False):
                i = n["chunk"].index
                if i >= SLOTS:
                    sp.wait_ge(flow.w_used, n["chunk"].value - SLOTS + 2)
                    if in_loop:
                        sp.nop(nofuse=True)
                dst = ring[:, i % SLOTS, 0:cols]
                if kt:
                    dst = ring[:, i % SLOTS, 0:kt * D].rearrange("p (k n) -> p k n", k=kt)
                sp.dma_start(dst, src).then_inc(flow.landed[i % SLOTS], 16)
                n["chunk"].next()

            def load_rows(w, kts, **kw):
                k = 0
                for kt in kts:
                    load(w[k * P:(k + kt) * P, :].rearrange("(k p) n -> p k n", p=P), kt=kt, **kw)
                    k += kt

            for b in range(TB):
                sp.dma_start(x_tok[:, b, :], a["x"][0, b * P:(b + 1) * P, :]).then_inc(x_in, 16)
            for h in range(2 * RET_H):
                load(a["ret_qk"][h])
            for g in range(2 * RET_V // HALF):
                for part in range(2):
                    load(a["ret_vg"][g, part])
            load_rows(a["ret_w_out"][0], RET_ROWS)
            for j in range(FT):
                load(a["ffn_up"][j])
            load_rows(a["ffn_w_out"][0], FFN_ROWS)
            for name in ("sb_k", "sb_q"):
                for j in range(4):
                    load(a[name][j])
            for g in range(2):
                for part in range(2):
                    load(a["sb_v"][g, part])
            load_rows(a["sb_w_out"][0], MIX_ROWS)

            def expert_pair(turn):
                for i in range(2):
                    for j in range(4 * EG):
                        load(a["moe_up"][bass.ds(2 * turn + i, 1), j].rearrange("a p n -> (a p) n"), in_loop=True)
                    load_rows(a["moe_w_out"][0, bass.ds(2 * turn + i, 1)].rearrange("a r n -> (a r) n"), EXPERT_ROWS,
                              in_loop=True)

            with sp.Fori(0, EXPERTS // 2) as turn:
                n.enter(turn, chunk=PAIR_TURN["chunk"])
                expert_pair(turn)
            n.leave(EXPERTS // 2)

            sp.wait_ge(most_ready, 1)
            with sp.If(sp.value_load(most[0:1, 0:1], min_val=0, max_val=S) > P):
                sp.wait_ge(main.sum_ready, MOE_SUMS)
                n_main, n, flow = n, Counts("chunk"), crowd
                with sp.Fori(0, EXPERTS // 2) as turn:
                    n.enter(turn, chunk=PAIR_TURN["chunk"])
                    expert_pair(turn)
                    sp.wait_ge(crowd.sum_ready, (turn + 1) * PAIR_TURN["sum"])
                    sp.nop(nofuse=True)
                n, flow = n_main, main

            with sp.Fori(0, LAYERS) as l:
                n.enter(l, chunk=LAYER_TURN["chunk"])
                for g in range(3):
                    w = a["w2_attn"][bass.ds(l, 1), g].rearrange("a c p n -> (a c) p n")
                    load(w[0, :, 0:SLOT // 2], cols=SLOT // 2, in_loop=True)
                    load(w[0, :, SLOT // 2:SLOT], cols=SLOT // 2, in_loop=True)
                    load(w[1], in_loop=True)
                for j in range(4):
                    load(a["w2_mqk"][bass.ds(l, 1), j].rearrange("a p n -> (a p) n"), in_loop=True)
                for g in range(2):
                    for part in range(2):
                        load(a["w2_mvo"][bass.ds(l, 1), g, part].rearrange("a p n -> (a p) n"), in_loop=True)
                load_rows(a["w_out_2"][bass.ds(l, 1)].rearrange("a r n -> (a r) n"), MIX_ROWS, in_loop=True)
                for j in range(FT):
                    load(a["w2_up"][bass.ds(l, 1), j].rearrange("a p n -> (a p) n"), in_loop=True)
                load_rows(a["w_down_2"][bass.ds(l, 1)].rearrange("a r n -> (a r) n"), LAYER_ROWS, in_loop=True)
            n.leave(LAYERS)
            for b in range(TB):
                sp.wait_ge(x_ready, 4 * TB + LAYERS * 2 * TB - TB + b + 1)
                sp.dma_start(out[0, b * P:(b + 1) * P, :], x_tok[:, b, :]).then_inc(out_done, 16)
            sp.wait_ge(out_done, 16 * TB)

        CONSTS = ((ident, "c_ident"), (suffix, "c_suffix"), (earlier, "c_earlier"), (rope, "c_rope"),
                  (reach, "c_reach"), (windows, "c_windows"), (ml_mask, "c_ml_mask"), (router_w, "router_w"),
                  (gates_w, "gates_w"), (places, "c_places"), (ret_decay, "c_decay"), (ret_rope, "c_ret_rope"))
        PARAMS = ((PAR_MIX_G, PAR_FFN_G, "mix_pre_g"), (PAR_FFN_G, PAR_TAP, "ffn_pre_g"), (PAR_TAP, PAR_TAP_B, "taps"),
                  (PAR_TAP_B, PAR_FTAP, "taps_b"), (PAR_FTAP, PAR_FTAP_B, "ffn_taps"), (PAR_FTAP_B, PARS, "ffn_taps_b"))
        CONSTS_IN = 16 * (len(CONSTS) + len(PARAMS) + 2)

        @block.gpsimd
        def _(pool):
            nc.gpsimd.memset(eps[:, 0:1], LN_EPS)
            nc.gpsimd.memset(eps[:, 1:2], RMS_EPS).then_inc(eps_set, 1)
            nc.gpsimd.memset(ones_row[:], 1.0).then_inc(eps_set, 1)
            for dst, name in CONSTS:
                ap = dst[:] if not isinstance(dst, bass.AP) else dst
                if len(ap.shape) > 2:
                    free = "abc"[:len(ap.shape) - 1]
                    ap = ap.rearrange(f"p {' '.join(free)} -> p ({' '.join(free)})")
                pool.dma_start(ap, a[name]).then_inc(consts_in, 16)
            for c0, c1, name in PARAMS:
                pool.dma_start(par[:, :, c0:c1], a[name]).then_inc(consts_in, 16)
            pool.dma_start(neg_row[0:ML_H, :, :].rearrange("p a b -> p (a b)"), a["c_neg_row"]).then_inc(consts_in, 16)
            pool.dma_start(gate_bias[0:ML_H, :, :].rearrange("p a b -> p (a b)"), a["gate_bias"]).then_inc(consts_in, 16)
            for k, (g, b_) in enumerate((("ln_mix_g", "ln_mix_b"), ("ln_ffn_g", "ln_ffn_b")) * 2):
                if k >= 2:
                    pool.wait_ge(x_ready, TB * (k - 1))
                for i, name in enumerate((g, b_)):
                    at = (k % 2) * 2 * D + i * D
                    pool.dma_start(gain[:, at:at + D], a[name][k // 2].partition_broadcast(P))\
                        .then_inc(gain_in[k % 2], 16)
            pool.wait_ge(x_ready, TB * 4)
            for l in range(LAYERS):
                for at, name, w in ((0, "mix_post_g_2", D), (D, "ffn_post_g_2", D), (2 * D, "mlstm_head_g_2", ML_W)):
                    pool.dma_start(gain[:, l * GAINS + at:l * GAINS + at + w],
                                   a[name][l].partition_broadcast(P)).then_inc(gains_in, 16)

        @block.tensor
        def _(pe):
            n = Counts("tile", "sum", "chunk", "x", "tok", "og", "z", "keep", "w", "lay", "rot", "mqk",
                       "rows", "floor", "pexp", "mixed", "h", "choice", land=Count(SLOTS, 16))
            flow = main
            fresh = [False]

            def slot():
                i = n["chunk"].index
                pe.wait_ge(flow.landed[i % SLOTS], n["land"].value + 16)
                fresh[0] = True
                n["chunk"].next(), n["land"].next()
                return ring[:, i % SLOTS, :]

            def mm(*args, **kw):
                ins = nc.tensor.matmul(*args, **kw)
                if fresh[0]:
                    ins.then_inc(flow.w_used, 1)
                    fresh[0] = False
                return ins

            def open_tile():
                return open_tiles(1)[0]

            def open_tiles(count):
                i = n["tile"].index
                n["tile"].more(count)
                if i + count > 4:
                    pe.wait_ge(flow.tile_taken, n["tile"].value - 4)
                return [tiles[(i + k) % 4] for k in range(count)]

            def open_sum():
                return open_sums(1)[0]

            def open_sums(count):
                i = n["sum"].index
                n["sum"].more(count)
                if i + count > 4:
                    pe.wait_ge(flow.sum_taken, n["sum"].value - 4)
                return [sums[(i + k) % 4] for k in range(count)]

            def all_taken():
                pe.wait_ge(flow.tile_taken, n["tile"].value)

            def transposes(block_of, count):
                for j in range(count // 2):
                    bank = open_tile()
                    for i in range(2):
                        for b in range(TB):
                            last = nc.tensor.transpose(bank[:, i * S + b * P:i * S + (b + 1) * P],
                                                       block_of(b, 2 * j + i), ident[:])
                    last.then_inc(flow.tile_ready, 1)

            def feature_tile():
                w = slot().rearrange("p (k n) -> p k n", k=KT)
                bank = open_tile()
                for i in range(2):
                    for k in range(KT):
                        last = mm(bank[:, i * S:(i + 1) * S], w[:, k, i * P:(i + 1) * P], xT[:, k, :],
                                  start=(k == 0), stop=(k == KT - 1))
                last.then_inc(flow.tile_ready, 1)

            def token_tiles(kts=(4, 4)):
                pair = open_tiles(TB)
                k = 0
                for kt in kts:
                    w = slot()
                    for kk in range(kt):
                        for b in range(TB):
                            last = mm(pair[b][:], xT[:, k, b * P:(b + 1) * P], w[:, kk * HALF:(kk + 1) * HALF],
                                      start=(k == 0), stop=(k == KT - 1))
                            if k == KT - 1:
                                last.then_inc(flow.tile_ready, 1)
                        k += 1

            def down(lhs, kts, ready=None):
                acc = open_sums(4)
                k, total = 0, sum(kts)
                for kt in kts:
                    w = slot()
                    for kk in range(kt):
                        if ready is not None:
                            ready(k)
                        for b in range(TB):
                            for h in range(2):
                                last = mm(acc[2 * b + h][:], lhs(k, b), w[:, kk * D + h * HALF:kk * D + (h + 1) * HALF],
                                          start=(k == 0), stop=(k == total - 1))
                                if k == total - 1:
                                    last.then_inc(flow.sum_ready, 1)
                        k += 1

            def ffn(kts):
                first = n["tile"].value
                for _ in range(sum(kts)):
                    feature_tile()
                down(lambda k, b: hT[:, k, b * P:(b + 1) * P], kts,
                     lambda k: pe.wait_ge(flow.tile_taken, first + k + 1))

            def x_transposes():
                n["x"].more(TB)
                pe.wait_ge(x_ready, n["x"].value)
                transposes(lambda b, d: x_tok[:, b, d * P:(d + 1) * P], KT)
                all_taken()

            pe.wait_ge(consts_in, CONSTS_IN)
            pe.wait_ge(x_in, 16 * TB)
            transposes(lambda b, d: x_tok[:, b, d * P:(d + 1) * P], KT)
            all_taken()
            for _ in range(2 * RET_H):
                feature_tile()
            for _ in range(2 * RET_V // HALF):
                token_tiles()
            all_taken()
            first = n["tile"].value
            for h in range(RET_H):
                q, k = headT[:, 2 * h:2 * h + 2, :], headT[:, KT + 2 * h:KT + 2 * h + 2, :]
                bank = open_tile()
                for c in range(2):
                    nc.tensor.matmul(bank[:, 0:S], k[:, c, 0:P], q[:, c, :], start=(c == 0), stop=(c == 1))
                for c in range(2):
                    last = nc.tensor.matmul(bank[:, S:S + P], k[:, c, P:S], q[:, c, P:S],
                                            start=(c == 0), stop=(c == 1))
                last.then_inc(flow.tile_ready, 1)
            for h in range(RET_H):
                pe.wait_ge(flow.tile_taken, first + h + 1)
                v = [ret_v[:, b, h * HALF:(h + 1) * HALF] for b in range(TB)]
                bank = open_tile()
                nc.tensor.matmul(bank[:], ret_p[:, h, 0:P], v[0], start=True, stop=True).then_inc(flow.tile_ready, 1)
                bank = open_tile()
                nc.tensor.matmul(bank[:], ret_p[:, h, P:S], v[0], start=True, stop=False)
                nc.tensor.matmul(bank[:], ret_p[:, h, S:S + P], v[1], start=False, stop=True).then_inc(flow.tile_ready, 1)
            n["og"].more(RET_H * TB)
            pe.wait_ge(og_ready, n["og"].value)
            transposes(lambda b, d: g_tok[:, b, d * P:(d + 1) * P], 2 * KT)
            all_taken()
            down(lambda k, b: headT[:, k, b * P:(b + 1) * P], RET_ROWS)
            x_transposes()
            ffn(FFN_ROWS)
            x_transposes()

            for _ in range(8):
                feature_tile()
            for _ in range(2):
                token_tiles()
            all_taken()
            opened = {}

            def sb_scores(h):
                po = (h % 2) * 64
                q, k = headT[po:po + 64, KT + h // 2, :], headT[po:po + 64, h // 2, :]
                opened[h] = bank = open_tile()
                nc.tensor.matmul(bank[:, 0:S], k[:, 0:P], q, start=True, stop=False, skip_group_check=True)
                nc.tensor.matmul(bank[:, S:S + P], k[:, P:S], q[:, P:S], start=False, stop=False,
                                 skip_group_check=True).then_inc(z_ready, 1)

            def sb_suffix(h):
                pe.wait_ge(keep_ready, n["keep"].next())
                bank, keep = opened[h], sb_keep[:, h % 4, :]
                nc.tensor.matmul(bank[:, 0:S], suffix[:, 0, :], keep[:, 0:S], start=False, stop=False,
                                 skip_group_check=True)
                nc.tensor.matmul(bank[:, P:S], suffix[:, 1, :], keep[:, S:S + P], start=False, stop=False,
                                 skip_group_check=True)
                nc.tensor.matmul(bank[:, S:S + P], suffix[:, 0, :], keep[:, S:S + P], start=False, stop=True,
                                 skip_group_check=True).then_inc(flow.tile_ready, 1)

            def sb_out(m):
                bank = open_sum()
                for i in range(2):
                    h = 2 * m + i
                    pe.wait_ge(w_ready, n["w"].next())
                    o, w = bank[64 * i:64 * i + 64, 0:S], sb_w[:, h % 4, :]
                    nc.tensor.matmul(o, sb_v[:, 0, h * 64:(h + 1) * 64], w[:, 0:S], start=True, stop=False)
                    last = nc.tensor.matmul(o[:, P:S], sb_v[:, 1, h * 64:(h + 1) * 64], w[:, S:S + P],
                                            start=False, stop=True)
                last.then_inc(flow.sum_ready, 1)

            for s in range(SB_H + 3):
                if s < SB_H:
                    sb_scores(s)
                if 1 <= s <= SB_H:
                    sb_suffix(s - 1)
                if s >= 4 and s % 2 == 0:
                    sb_out((s - 4) // 2)
            pe.wait_ge(flow.sum_taken, n["sum"].value)
            down(lambda k, b: xT[:, k, b * P:(b + 1) * P], MIX_ROWS)
            x_transposes()

            bank = open_tile()
            for b in range(TB):
                for k in range(KT):
                    last = nc.tensor.matmul(bank[:, b * EXPERTS:(b + 1) * EXPERTS], xT[:, k, b * P:(b + 1) * P],
                                            router_w[:, k, :], start=(k == 0), stop=(k == KT - 1))
            last.then_inc(flow.tile_ready, 1)
            pe.wait_ge(chosen_ready, 1)
            bank = open_tile()
            nc.tensor.matmul(bank[:, 0:16], earlier[:], rank[:].rearrange("p b e -> p (b e)"), start=True, stop=True)
            nc.tensor.matmul(bank[:, 16:32], suffix[:, 1, :], rank[:].rearrange("p b e -> p (b e)"),
                             start=True, stop=True).then_inc(flow.tile_ready, 1)

            def gather(i):
                pe.wait_ge(flow.choice_ready, n["choice"].next())
                for half in range(2):
                    bank = open_tile()
                    for q in range(4):
                        f = 4 * half + q
                        for b in range(TB):
                            last = nc.tensor.matmul(bank[:, q * P:(q + 1) * P], x_tok[:, b, f * P:(f + 1) * P],
                                                    choice[:, i, b, :], start=(b == 0), stop=(b == TB - 1))
                    last.then_inc(flow.tile_ready, 1)
                bank = open_tile()
                for b in range(TB):
                    last = nc.tensor.transpose(bank[:, b * P:(b + 1) * P], choice[:, i, b, :], ident[:])
                last.then_inc(flow.tile_ready, 1)

            def expert(i):
                hidden, turned = {}, {}
                all_taken()

                def turn_over(g):
                    pe.wait_ge(flow.tile_taken, hidden[g])
                    bank = open_tile()
                    for q in range(4):
                        last = nc.tensor.transpose(bank[:, q * P:(q + 1) * P], h_tok[:, g % 2, q * P:(q + 1) * P], ident[:])
                    last.then_inc(flow.tile_ready, 1)
                    turned[g] = n["tile"].value

                for g in range(EG):
                    for _ in range(2):
                        bank = open_tile()
                        for part in range(2):
                            w = slot()
                            for kk in range(4):
                                k = 4 * part + kk
                                last = mm(bank[:], chosenT[:, i, k, :], w[:, kk * HALF:(kk + 1) * HALF],
                                          start=(k == 0), stop=(k == KT - 1))
                        last.then_inc(flow.tile_ready, 1)
                    hidden[g] = n["tile"].value
                    if g:
                        turn_over(g - 1)
                acc = open_sums(2)
                k = 0
                for kt in EXPERT_ROWS:
                    w = slot()
                    for kk in range(kt):
                        if k == 4 * (EG - 2):
                            turn_over(EG - 1)
                        if k % 4 == 0:
                            pe.wait_ge(flow.tile_taken, turned[k // 4])
                        for h in range(2):
                            last = mm(acc[h][:], eT[:, k, :], w[:, kk * D + h * HALF:kk * D + (h + 1) * HALF],
                                      start=(k == 0), stop=(k == ET - 1))
                            if k == ET - 1:
                                last.then_inc(flow.sum_ready, 1)
                        k += 1
                down_done = n["sum"].value
                gather(1 - i)
                pe.wait_ge(flow.sum_taken, down_done)
                acc = open_sums(4)
                for b in range(TB):
                    for h in range(2):
                        nc.tensor.matmul(acc[2 * b + h][:], choiceT[:, i, b, :], rows_e[:, h * HALF:(h + 1) * HALF],
                                         start=True, stop=True).then_inc(flow.sum_ready, 1)

            gather(0)
            with pe.Fori(0, EXPERTS // 2) as turn:
                n.enter(turn, land=PAIR_TURN["chunk"], choice=2, **PAIR_TURN)
                expert(0)
                expert(1)
            n.leave(EXPERTS // 2)
            assert n["sum"].value == MOE_SUMS

            pe.wait_ge(most_ready, 1)
            with pe.If(pe.value_load(most[0:1, 0:1], min_val=0, max_val=S) > P):
                pe.wait_ge(main.tile_taken, n["tile"].value)
                pe.wait_ge(main.sum_taken, n["sum"].value)
                n_main, n, flow = n, Counts("tile", "sum", "chunk", "choice", land=Count(SLOTS, 16)), crowd
                gather(0)
                with pe.Fori(0, EXPERTS // 2) as turn:
                    n.enter(turn, land=PAIR_TURN["chunk"], choice=2, **PAIR_TURN)
                    expert(0)
                    expert(1)
                    pe.wait_ge(crowd.sum_taken, n["sum"].value)
                n.leave(EXPERTS // 2)
                pe.wait_ge(crowd.tile_taken, n["tile"].value)
                n, flow = n_main, main

            with pe.Fori(0, LAYERS) as l:
                n.enter(l, land=LAYER_TURN["chunk"], tok=4, lay=1, rot=2, mqk=8, rows=1, floor=1, pexp=AT_H,
                        mixed=1, h=FT, **LAYER_TURN)
                pe.wait_ge(lay_ready, n["lay"].next())

                def y_transposes():
                    n["tok"].more(TB)
                    pe.wait_ge(tok_ready, n["tok"].value)
                    transposes(lambda b, d: y_tok[:, b, d * P:(d + 1) * P], KT)
                    all_taken()

                y_transposes()
                bank = open_tile()
                for b in range(TB):
                    for k in range(KT):
                        last = nc.tensor.matmul(bank[:, b * 16:(b + 1) * 16], xT[:, k, b * P:(b + 1) * P],
                                                gates_wL[:, k * 16:(k + 1) * 16], start=(k == 0), stop=(k == KT - 1))
                last.then_inc(flow.tile_ready, 1)
                for _ in range(3):
                    token_tiles((2, 2, 4))
                for _ in range(4):
                    feature_tile()
                for _ in range(2):
                    token_tiles()
                for kind in range(2):
                    bank = open_tile()
                    pe.nop(nofuse=True)
                    for d in range(2):
                        for b in range(TB):
                            c = (2 * d + kind) * ML_H
                            last = nc.tensor.transpose(bank[0:ML_H, d * S + b * P:d * S + (b + 1) * P],
                                                       gate_tok[:, b, c:c + ML_H], ident[:])
                    last.then_inc(flow.tile_ready, 1)
                for i in range(2):
                    pe.wait_ge(rot_ready, n["rot"].next())
                    transposes(lambda b, d: rot[:, i, b, d * P:(d + 1) * P], AT_W // P)
                all_taken()
                turned = {}

                def at_scores(h):
                    po = (h % 2) * 64
                    q, k = headT[po:po + 64, h // 2, :], headT[po:po + 64, 4 + h // 2, :]
                    bank = open_tile()
                    for b in range(TB):
                        last = nc.tensor.matmul(bank[:, b * S:(b + 1) * S], q[:, b * P:(b + 1) * P], k,
                                                start=True, stop=True)
                    last.then_inc(flow.tile_ready, 1)

                def at_turn(h):
                    pe.wait_ge(p_exp, n["pexp"].next())
                    bank = open_tile()
                    for kb in range(TB):
                        for b in range(TB):
                            last = nc.tensor.transpose(bank[:, kb * S + b * P:kb * S + (b + 1) * P],
                                                       at_p[h % 2][:, b, kb * P:(kb + 1) * P], ident[:])
                    last.then_inc(flow.tile_ready, 1)
                    turned[h] = n["tile"].value

                def at_out(h):
                    pe.wait_ge(flow.tile_taken, turned[h])
                    bank = open_sum()
                    for b in range(TB):
                        for kb in range(TB):
                            last = nc.tensor.matmul(bank[:, b * VA:(b + 1) * VA], at_pT[h % 2][:, kb, b * P:(b + 1) * P],
                                                    at_v[:, kb, h, :], start=(kb == 0), stop=(kb == 1))
                    last.then_inc(flow.sum_ready, 1)

                for s in range(AT_H + 2):
                    if s < AT_H:
                        at_scores(s)
                    if 1 <= s <= AT_H:
                        at_turn(s - 1)
                    if s >= 2:
                        at_out(s - 2)

                pe.wait_ge(rows_ready, n["rows"].next())
                pe.wait_ge(floor_ready, n["floor"].next())
                bank = open_tile()
                pe.nop(nofuse=True)
                for kind, r in enumerate((2, 4)):
                    for d in range(2):
                        for b in range(TB):
                            c = ((kind * 2 + d) * TB + b) * ML_H
                            last = nc.tensor.transpose(bank[:, c:c + ML_H], row[0:ML_H, r, d, b * P:(b + 1) * P],
                                                       ident[0:ML_H, 0:ML_H])
                last.then_inc(flow.tile_ready, 1)
                n["mqk"].more(8)
                pe.wait_ge(mqk_ready, n["mqk"].value)
                decayed = {}

                def ml_scores(h):
                    bank = open_tile()
                    nc.tensor.matmul(bank[:], neg_row[0:ML_H, h, :], row[0:ML_H, 3, :, :].rearrange("p d t -> p (d t)"),
                                     start=True, stop=True).then_inc(flow.tile_ready, 1)
                    bank = open_tile()
                    for kb in range(TB):
                        last = nc.tensor.matmul(bank[:, kb * S:(kb + 1) * S], ml_qk[:, ML_H + h, kb * P:(kb + 1) * P],
                                                ml_qk[:, h, :], start=True, stop=True)
                    last.then_inc(flow.tile_ready, 1)
                    decayed[h] = n["tile"].value

                def ml_out(h):
                    pe.wait_ge(flow.tile_taken, decayed[h])
                    for d in range(2):
                        bank = open_sum()
                        for b in range(TB):
                            seen = range(0, b + 1) if d == 0 else range(b, TB)
                            for i, kb in enumerate(seen):
                                last = nc.tensor.matmul(bank[:, b * VM:(b + 1) * VM], ml_e[h % 2][:, d, kb, b * P:(b + 1) * P],
                                                        ml_v[:, kb, h, :], start=(i == 0), stop=(i == len(seen) - 1))
                        last.then_inc(flow.sum_ready, 1)

                for s in range(ML_H + 1):
                    if s < ML_H:
                        ml_scores(s)
                    if s >= 1:
                        ml_out(s - 1)
                pe.wait_ge(mixed_ready, n["mixed"].next())
                transposes(lambda b, d: o_tok[:, b, d * P:(d + 1) * P], KT)
                all_taken()
                down(lambda k, b: headT[:, k, b * P:(b + 1) * P], MIX_ROWS)
                y_transposes()
                for _ in range(FT):
                    feature_tile()
                down(lambda k, b: hT[:, k, b * P:(b + 1) * P], LAYER_ROWS,
                     lambda k: pe.wait_ge(h_ready, n["h"].next()))
            n.leave(LAYERS)

        @block.scalar
        def _(act):
            n = Counts("tile", "sum", "step", "var", "x", "tok", "abs", "gexp", "lay", "conv", "forget",
                       "rows", "pin", "gtap", "h")
            flow = main

            def step(ins):
                ins.then_inc(flow.act_step, 1)
                act.wait_ge(flow.act_step, n["step"].next())

            def arrived():
                i = n["tile"].index
                act.wait_ge(flow.tile_ready, n["tile"].next())
                return tiles[i % 4]

            def hand_over():
                act.wait_ge(flow.tile_taken, n["tile"].value)

            def copy_tiles(dst, count, func=ACT.Copy, scale=1.0):
                for j in range(count):
                    bank = arrived()
                    nc.scalar.activation(dst(j), bank[:], func, scale=scale).then_inc(flow.tile_taken, 1)

            def pair(t):
                return lambda j: t[:, 2 * j:2 * j + 2, :].rearrange("p k t -> p (k t)")

            def layer_norm_roots():
                for b in range(TB):
                    act.wait_ge(var_ready, n["var"].next())
                    nc.scalar.activation(std[:, b:b + 1], mean_var[:, b, 1:2], ACT.Sqrt,
                                         bias=eps[:, 0:1]).then_inc(std_ready, 1)

            def silu_tiles(count):
                for j in range(count):
                    bank = arrived()
                    act.wait_ge(flow.tile_taken, n["tile"].value - 2)
                    nc.scalar.activation(acted[:, j % 2, 0:S], bank[:, 0:S], ACT.Silu).then_inc(acted_ready, 1)

            act.wait_ge(eps_set, 2)
            copy_tiles(pair(xT), 4)
            for _ in range(2 * RET_H):
                n["tile"].next()
            hand_over()
            copy_tiles(lambda j: ret_v[:, j % 2, (j // 2) * HALF:(j // 2 + 1) * HALF], 8)
            copy_tiles(lambda j: g_tok[:, j % 2, (j // 2) * HALF:(j // 2 + 1) * HALF], 8, ACT.Silu)
            for _ in range(RET_H):
                n["tile"].next()
            for g in range(RET_H * TB // 4):
                for i in range(4):
                    n["tile"].next()
                    act.wait_ge(var_ready, n["var"].next())
                    nc.scalar.activation(std[:, 4 + i:5 + i], mean_var[:, i, 1:2], ACT.Sqrt,
                                         bias=eps[:, 0:1]).then_inc(std_ready, 1)
            hand_over()
            copy_tiles(pair(headT), 8)
            n["sum"].next(), n["sum"].next(), n["sum"].next(), n["sum"].next()
            layer_norm_roots()
            copy_tiles(pair(xT), 4)
            silu_tiles(FT)
            for _ in range(4):
                n["sum"].next()
            layer_norm_roots()
            hand_over()
            copy_tiles(pair(xT), 4)

            copy_tiles(pair(headT), 4)
            copy_tiles(lambda j: headT[:, KT + 2 * j:KT + 2 * j + 2, :].rearrange("p k t -> p (k t)"), 4,
                       scale=64 ** -0.5)
            copy_tiles(lambda j: sb_v[:, j % 2, (j // 2) * HALF:(j // 2 + 1) * HALF], 4)

            def sb_log(h):
                act.wait_ge(abs_ready, n["abs"].next())
                e = sb_e[:, h % 4, :]
                step(nc.scalar.activation(e, sb_size[:, h % 4, :], ACT.Exp, scale=-1.0))
                nc.scalar.activation(e, e, ACT.Ln, bias=1.0).then_inc(log_ready, 1)

            def sb_exp(h):
                act.wait_ge(flow.tile_taken, n["tile"].next())
                nc.scalar.activation(sb_w[:, h % 4, :], sb_w[:, h % 4, :], ACT.Exp).then_inc(wexp_ready, 1)

            def sb_take(m):
                i = n["sum"].index
                act.wait_ge(flow.sum_ready, n["sum"].next())
                nc.scalar.activation(xT[:, m, :], sums[i % 4][:, 0:S], ACT.Copy).then_inc(flow.sum_taken, 1)

            for s in range(SB_H + 2):
                if s < SB_H:
                    sb_log(s)
                if s >= 2:
                    sb_exp(s - 2)
                if s >= 5 and s % 2 == 1:
                    sb_take((s - 5) // 2)
            sb_take(SB_H // 2 - 1)
            for _ in range(4):
                n["sum"].next()
            layer_norm_roots()
            hand_over()
            copy_tiles(pair(xT), 4)

            n["tile"].next()
            act.wait_ge(gexp_in, n["gexp"].next())
            nc.scalar.activation(gate[:].rearrange("p b e -> p (b e)"), gate[:].rearrange("p b e -> p (b e)"),
                                 ACT.Exp).then_inc(gexp_ready, 1)
            n["tile"].next()
            hand_over()

            def gathered(i):
                copy_tiles(lambda j: chosenT[:, i, 4 * j:4 * j + 4, :].rearrange("p k j -> p (k j)"), 2)
                bank = arrived()
                nc.scalar.activation(choiceT[:, i, :, :].rearrange("p b t -> p (b t)"), bank[:, 0:S], ACT.Copy)\
                    .then_inc(flow.tile_taken, 1)

            def turned_over(g):
                hand_over()
                copy_tiles(lambda j: eT[:, 4 * g:4 * g + 4, :].rearrange("p k j -> p (k j)"), 1)

            def expert(i):
                for g in range(EG):
                    if g == 1:
                        hand_over()
                    copy_tiles(lambda j: acted[:, g % 2, :], 1, ACT.Silu)
                    n["tile"].next()
                    if g:
                        turned_over(g - 1)
                turned_over(EG - 1)
                if n["sum"].index:
                    act.wait_ge(flow.sum_taken, n["sum"].value)
                for h in range(2):
                    j = n["sum"].index % 4
                    act.wait_ge(flow.sum_ready, n["sum"].next())
                    nc.scalar.activation(rows_e[:, h * HALF:(h + 1) * HALF], sums[j][:], ACT.Copy).then_inc(flow.sum_taken, 1)
                gathered(1 - i)
                n["sum"].more(4)

            gathered(0)
            with act.Fori(0, EXPERTS // 2) as turn:
                n.enter(turn, tile=PAIR_TURN["tile"], sum=PAIR_TURN["sum"])
                expert(0)
                expert(1)
            n.leave(EXPERTS // 2)

            act.wait_ge(most_ready, 1)
            with act.If(act.value_load(most[0:1, 0:1], min_val=0, max_val=S) > P):
                n_main, n, flow = n, Counts("tile", "sum"), crowd
                gathered(0)
                with act.Fori(0, EXPERTS // 2) as turn:
                    n.enter(turn, tile=PAIR_TURN["tile"], sum=PAIR_TURN["sum"])
                    expert(0)
                    expert(1)
                n.leave(EXPERTS // 2)
                n, flow = n_main, main
            layer_norm_roots()

            for _ in range(TB * 3):
                n["x"].next()
            with act.Fori(0, LAYERS) as l:
                n.enter(l, tile=LAYER_TURN["tile"], sum=LAYER_TURN["sum"], x=4, var=5, lay=1, conv=8, forget=1,
                        rows=1, pin=AT_H, gtap=FT, h=FT, step=ACT_STEPS)

                def pre_norm_root(b):
                    act.wait_ge(x_ready, n["x"].next())
                    step(nc.scalar.activation(junk[:], x_tok[:, b, :], ACT.Square, accum_out=sq_tot[:, b:b + 1]))
                    nc.scalar.activation(std[:, b:b + 1], sq_tot[:, b:b + 1], ACT.Sqrt, bias=eps[:, 1:2],
                                         scale=1.0 / D).then_inc(std_ready, 1)

                def gained(g0):
                    for j in range(4):
                        bank = arrived()
                        for i in range(2):
                            last = nc.scalar.activation(xT[:, 2 * j + i, :], bank[:, i * S:(i + 1) * S], ACT.Copy,
                                                        scale=parL[:, g0 + 2 * j + i:g0 + 2 * j + i + 1])
                        last.then_inc(flow.tile_taken, 1)

                def post_norm_roots():
                    for b in range(TB):
                        for h in range(2):
                            i = n["sum"].index
                            act.wait_ge(flow.sum_ready, n["sum"].next())
                            last = nc.scalar.activation(junk[:, h * HALF:(h + 1) * HALF], sums[i % 4][:], ACT.Square,
                                                        accum_out=sq_sum[:, b, h:h + 1])
                        last.then_inc(square_ready, 1)
                        act.wait_ge(var_ready, n["var"].next())
                        nc.scalar.activation(std[:, b:b + 1], sq_tot[:, b:b + 1], ACT.Sqrt, bias=eps[:, 1:2],
                                             scale=1.0 / D).then_inc(std_ready, 1)

                act.wait_ge(lay_ready, n["lay"].next())
                for b in range(TB):
                    pre_norm_root(b)
                hand_over()
                gained(PAR_MIX_G)
                for _ in range(5):
                    n["tile"].next()
                hand_over()
                for b in range(TB):
                    bank = arrived()
                    nc.scalar.activation(at_v[:, b, :, 0:AT_D], bank[:].rearrange("p (h d) -> p h d", h=AT_H),
                                         ACT.Copy).then_inc(flow.tile_taken, 1)
                for j in range(4):
                    bank = arrived()
                    nc.scalar.activation(conv[:, 2 * j:2 * j + 2, PAD:PAD + S],
                                         bank[:].rearrange("p (f t) -> p f t", f=2), ACT.Copy).then_inc(flow.tile_taken, 1)
                for b in range(TB):
                    bank = arrived()
                    nc.scalar.activation(ml_v[:, b, :, 0:ML_D], bank[:].rearrange("p (h d) -> p h d", h=ML_H),
                                         ACT.Copy).then_inc(flow.tile_taken, 1)
                copy_tiles(lambda b: ml_o[:, b, :], TB, ACT.Sigmoid)
                n["tile"].next(), n["tile"].next()
                act.wait_ge(forget_in, n["forget"].next())
                r = row[0:ML_H, 4, :, :].rearrange("p d t -> p (d t)")
                step(nc.scalar.activation(r, r, ACT.Exp))
                nc.scalar.activation(r, r, ACT.Ln, bias=1.0).then_inc(forget_log, 1)
                act.wait_ge(rows_ready, n["rows"].next())
                nc.scalar.activation(r, r, ACT.Exp).then_inc(floor_ready, 1)
                for f in range(8):
                    act.wait_ge(conv_ready, n["conv"].next())
                    nc.scalar.activation(ml_qk[:, f, :], ml_qk[:, f, :], ACT.Silu,
                                         bias=parL[:, PAR_TAP_B + f:PAR_TAP_B + f + 1]).then_inc(mqk_ready, 1)
                hand_over()
                copy_tiles(pair(headT), 4)
                for h in range(AT_H):
                    n["tile"].next(), n["tile"].next(), n["sum"].next()
                    act.wait_ge(p_in, n["pin"].next())
                    for b in range(TB):
                        last = nc.scalar.activation(at_p[h % 2][:, b, :], at_p[h % 2][:, b, :], ACT.Exp,
                                                    bias=neg_max[:, h % 2, b:b + 1])
                    last.then_inc(p_exp, 1)
                n["tile"].next()
                for h in range(ML_H):
                    act.wait_ge(flow.tile_taken, n["tile"].next())
                    e = ml_e[h % 2].rearrange("p d s t -> p (d s t)")
                    nc.scalar.activation(e, e, ACT.Exp).then_inc(d_exp, 1)
                    n["tile"].next(), n["sum"].next(), n["sum"].next()
                act.wait_ge(var_ready, n["var"].next())
                nc.scalar.activation(std[:], sq_tot[:], ACT.Sqrt, bias=eps[:, 1:2], scale=1.0 / ML_D)\
                    .then_inc(std_ready, 1)
                hand_over()
                copy_tiles(pair(headT), 4)
                post_norm_roots()
                for b in range(TB):
                    pre_norm_root(b)
                gained(PAR_FFN_G)

                def ffn_middle(j):
                    bank = arrived()
                    for i in range(2):
                        f = i * FT + j
                        last = nc.scalar.activation(fconv[:, j % 2, i, :], bank[:, i * S:(i + 1) * S], ACT.Identity,
                                                    bias=parL[:, PAR_FTAP_B + f:PAR_FTAP_B + f + 1],
                                                    scale=parL[:, PAR_FTAP + 3 * f + 1:PAR_FTAP + 3 * f + 2])
                    last.then_inc(lin_ready, 1)

                def ffn_act(j):
                    act.wait_ge(gtap_ready, n["gtap"].next())
                    nc.scalar.activation(acted[:, j % 2, 0:S], fconv[:, j % 2, 0, :], ACT.Gelu_apprx_tanh)\
                        .then_inc(acted_ready, 1)

                for s in range(FT + 1):
                    if s < FT:
                        if s >= 2:
                            act.wait_ge(h_ready, n["h"].next())
                        ffn_middle(s)
                    if s >= 1:
                        ffn_act(s - 1)
                n["h"].next(), n["h"].next()
                post_norm_roots()
            n.leave(LAYERS)

        @block.vector
        def _(vec):
            n = Counts("tile", "sum", "step", "std", "acted", "log", "wexp", "square", "gexp",
                       "flog", "dexp", "lin", "rot")
            flow = main
            tt, stt, ts = nc.vector.tensor_tensor, nc.vector.scalar_tensor_tensor, nc.vector.tensor_scalar

            def step(ins):
                ins.then_inc(flow.vec_step, 1)
                vec.wait_ge(flow.vec_step, n["step"].next())

            def arrived():
                i = n["tile"].index
                vec.wait_ge(flow.tile_ready, n["tile"].next())
                return tiles[i % 4]

            def arrived_sum():
                i = n["sum"].index
                vec.wait_ge(flow.sum_ready, n["sum"].next())
                return sums[i % 4]

            def hand_over():
                vec.wait_ge(flow.tile_taken, n["tile"].value)

            def skip(count):
                for _ in range(count):
                    n["tile"].next()

            def layer_norm(k, experts=False):
                for b in range(TB):
                    for h in range(2):
                        xs = x_tok[:, b, h * HALF:(h + 1) * HALF]
                        if experts:
                            step(stt(xs, xs, ALPHA, y_tok[:, b, h * HALF:(h + 1) * HALF], ALU.mult, ALU.add))
                        else:
                            bank = arrived_sum()
                            stt(xs, xs, ALPHA, bank[:], ALU.mult, ALU.add).then_inc(flow.sum_taken, 1)
                            vec.wait_ge(flow.sum_taken, n["sum"].value)
                        last = nc.vector.bn_stats(stats[:, b, h, :], xs)
                    step(last)
                    nc.vector.bn_aggr(mean_var[:, b, :], stats[:, b, :, :].rearrange("p h s -> p (h s)"))\
                        .then_inc(var_ready, 1)
                vec.wait_ge(gain_in[k % 2], 32 * (k // 2 + 1))
                g = gain[:, (k % 2) * 2 * D:(k % 2) * 2 * D + D]
                shift = gain[:, (k % 2) * 2 * D + D:(k % 2) * 2 * D + 2 * D]
                for b in range(TB):
                    xs = x_tok[:, b, :]
                    vec.wait_ge(std_ready, n["std"].next())
                    step(nc.vector.reciprocal(rstd[:, b:b + 1], std[:, b:b + 1]))
                    step(ts(xs, xs, mean_var[:, b, 0:1], rstd[:, b:b + 1], ALU.subtract, ALU.mult))
                    step(tt(xs, xs, g, ALU.mult))
                    tt(xs, xs, shift, ALU.add).then_inc(x_ready, 1)

            def gated_tiles(count):
                for j in range(count):
                    bank = arrived()
                    vec.wait_ge(acted_ready, n["acted"].next())
                    tt(hT[:, j, :], acted[:, j % 2, 0:S], bank[:, S:2 * S], ALU.mult).then_inc(flow.tile_taken, 1)

            vec.wait_ge(consts_in, CONSTS_IN)
            skip(4)
            hand_over()
            cos = ret_rope[:, 0, :].unsqueeze(1).to_broadcast([P, 2, S])
            sin = ret_rope[:, 1, :].unsqueeze(1).to_broadcast([P, 2, S])
            for h in range(2 * RET_H):
                bank = arrived()[:].rearrange("p (i t) -> p i t", i=2)
                tt(ret_tmp[:, 0:2, :], bank, cos, ALU.mult)
                step(tt(ret_tmp[:, 2:4, :], bank, sin, ALU.mult))
                tt(headT[:, 2 * h, :], ret_tmp[:, 0, :], ret_tmp[:, 3, :], ALU.subtract)
                tt(headT[:, 2 * h + 1, :], ret_tmp[:, 2, :], ret_tmp[:, 1, :], ALU.add).then_inc(flow.tile_taken, 1)
                vec.wait_ge(flow.tile_taken, n["tile"].value)
            skip(16)
            hand_over()
            for h in range(RET_H):
                bank = arrived()
                tt(ret_p[:, h, :], bank[:, 0:3 * P], ret_decay[:, h, :], ALU.mult).then_inc(flow.tile_taken, 1)
            for g in range(RET_H * TB // 4):
                got = []
                for i in range(4):
                    bank = arrived()
                    got.append(bank)
                    step(nc.vector.bn_stats(stats[:, i, 0, :], bank[:]))
                    nc.vector.bn_aggr(mean_var[:, i, :], stats[:, i, 0, :]).then_inc(var_ready, 1)
                for i in range(4):
                    h, b = (4 * g + i) // TB, i % TB
                    o = ret_tmp[:, (i % 2) * 2:(i % 2) * 2 + 2, :].rearrange("p i t -> p (i t)")
                    gs = g_tok[:, b, h * HALF:(h + 1) * HALF]
                    vec.wait_ge(std_ready, n["std"].next())
                    step(nc.vector.reciprocal(rstd[:, i:i + 1], std[:, 4 + i:5 + i]))
                    ts(o, got[i][:], mean_var[:, i, 0:1], rstd[:, i:i + 1], ALU.subtract, ALU.mult)\
                        .then_inc(flow.tile_taken, 1)
                    vec.wait_ge(flow.tile_taken, n["tile"].value - 3 + i)
                    tt(gs, gs, o, ALU.mult).then_inc(og_ready, 1)
            skip(8)
            layer_norm(0)
            skip(4)
            hand_over()
            gated_tiles(FT)
            layer_norm(1)
            skip(4)

            skip(8 + 4)
            hand_over()
            mask2 = earlier[:].unsqueeze(1).to_broadcast([P, 2, P])
            zs = {}

            def edge(t):
                return t.rearrange("p (i n) -> p i n", i=3)[:, 0:3:2, :]

            def sb_abs(h):
                zs[h] = bank = tiles[(first + h) % 4]
                vec.wait_ge(z_ready, h + 1)
                size = sb_size[:, h % 4, :]
                step(ts(size, bank[:, 0:384], 0.0, None, ALU.min))
                stt(size, bank[:, 0:384], 0.0, size, ALU.max, ALU.subtract).then_inc(abs_ready, 1)

            def sb_soft(h):
                keep = sb_keep[:, h % 4, :]
                vec.wait_ge(log_ready, n["log"].next())
                step(stt(keep, zs[h][:, 0:384], 0.0, sb_e[:, h % 4, :], ALU.max, ALU.add))
                tt(edge(keep), edge(keep), mask2, ALU.mult).then_inc(keep_ready, 1)

            def sb_bound(h):
                bank = arrived()
                ts(sb_w[:, h % 4, :], bank[:, 0:384], 0.0, None, ALU.min).then_inc(flow.tile_taken, 1)

            def sb_mask(h):
                vec.wait_ge(wexp_ready, n["wexp"].next())
                w = sb_w[:, h % 4, :]
                tt(edge(w), edge(w), mask2, ALU.mult).then_inc(w_ready, 1)

            first = n["tile"].index
            for s in range(SB_H + 3):
                if s < SB_H:
                    sb_abs(s)
                if 1 <= s <= SB_H:
                    sb_soft(s - 1)
                if 2 <= s <= SB_H + 1:
                    sb_bound(s - 2)
                if s >= 3:
                    sb_mask(s - 3)
            for _ in range(SB_H // 2):
                n["sum"].next()
            layer_norm(2)
            skip(4)

            hand_over()
            bank = arrived()
            nc.vector.tensor_copy(logits[:].rearrange("p b e -> p (b e)"), bank[:, 0:TB * EXPERTS]).then_inc(flow.tile_taken, 1)
            vec.wait_ge(flow.tile_taken, n["tile"].value)
            for e in range(EXPERTS):
                rival = logits[:, :, e:e + 1]
                tt(beaten[:, :, 0:e + 1, e], logits[:, :, 0:e + 1], rival.to_broadcast([P, TB, e + 1]), ALU.is_lt)
                if e < EXPERTS - 1:
                    tt(beaten[:, :, e + 1:, e], logits[:, :, e + 1:],
                       rival.to_broadcast([P, TB, EXPERTS - 1 - e]), ALU.is_le)
            step(nc.vector.tensor_reduce(top[:, :, 0], logits[:], AX.X, ALU.max))
            step(nc.vector.tensor_reduce(rank[:], beaten[:], AX.X, ALU.add))
            ts(rank[:], rank[:], float(2), None, ALU.is_lt).then_inc(chosen_ready, 1)
            tt(gate[:], logits[:], top[:, :, 0:1].to_broadcast([P, TB, EXPERTS]), ALU.subtract).then_inc(gexp_in, 1)
            nc.vector.memset(y_tok[:].rearrange("p b n -> p (b n)"), 0.0)
            vec.wait_ge(gexp_ready, n["gexp"].next())
            step(tt(gate[:], gate[:], rank[:], ALU.mult))
            step(nc.vector.tensor_reduce(top[:, :, 1], gate[:], AX.X, ALU.add))
            step(nc.vector.reciprocal(top[:, :, 1], top[:, :, 1]))
            step(tt(gate[:], gate[:], top[:, :, 1:2].to_broadcast([P, TB, EXPERTS]), ALU.mult))
            nc.vector.memset(route[:, :, :, EXPERTS], 0.0)
            nc.vector.tensor_copy(route[:, 0, :, 0:EXPERTS], rank[:])
            nc.vector.tensor_copy(route[:, 2, :, 0:EXPERTS], gate[:])
            bank = arrived()
            nc.vector.tensor_copy(logits[:].rearrange("p b e -> p (b e)"), bank[:, 16:32])
            step(nc.vector.tensor_copy(route[:, 1, :, 0:EXPERTS], bank[:, 0:16].rearrange("p (b e) -> p b e", b=TB)))
            tt(route[:, 1, 1, 0:EXPERTS], route[:, 1, 1, 0:EXPERTS], logits[:, 0, :], ALU.subtract)
            step(tt(logits[:, 0, :], logits[:, 0, :], logits[:, 1, :], ALU.add))
            step(nc.vector.tensor_reduce(top[:, 0:1, 0], logits[:, 0, :], AX.X, ALU.min))
            ts(most[:], top[:, 0:1, 0], -1.0, None, ALU.mult).then_inc(most_ready, 1)
            nc.vector.tensor_copy(route[:, :, :, EXPERTS], route[:, :, :, EXPERTS]).then_inc(flow.tile_taken, 1)
            vec.wait_ge(flow.tile_taken, n["tile"].value)

            def choose(e, i, second):
                step(nc.vector.tensor_copy(route_e[:, i, :], route[:, :, :, bass.ds(e, 1)].rearrange("p r b e -> p (r b e)")))
                for b in range(TB):
                    last = ts(choice[:, i, b, :], places[:, second, :], route_e[:, i, TB + b:TB + b + 1],
                              route_e[:, i, b:b + 1], ALU.is_equal, ALU.mult)
                last.then_inc(flow.choice_ready, 1)

            def expert(e, i, second):
                choose(e + 1, 1 - i, second)
                for g in range(EG):
                    n["tile"].next()
                    vec.wait_ge(flow.tile_taken, n["tile"].value)
                    bank = arrived()
                    tt(h_tok[:, g % 2, :], acted[:, g % 2, :], bank[:], ALU.mult).then_inc(flow.tile_taken, 1)
                    if g:
                        skip(1)
                skip(1 + 3)
                n["sum"].more(2)
                for b in range(TB):
                    for h in range(2):
                        bank = arrived_sum()
                        ys = y_tok[:, b, h * HALF:(h + 1) * HALF]
                        stt(ys, bank[:], route_e[:, i, 2 * TB + b:2 * TB + b + 1], ys, ALU.mult, ALU.add)\
                            .then_inc(flow.sum_taken, 1)
                vec.wait_ge(flow.sum_taken, n["sum"].value)

            def experts(second, n):
                choose(0, 0, second)
                skip(3)
                with vec.Fori(0, EXPERTS // 2) as turn:
                    n.enter(turn, tile=PAIR_TURN["tile"], sum=PAIR_TURN["sum"], step=2)
                    expert(2 * turn, 0, second)
                    expert(2 * turn + 1, 1, second)
                n.leave(EXPERTS // 2)

            experts(0, n)
            with vec.If(vec.value_load(most[0:1, 0:1], min_val=0, max_val=S) > P):
                n_main, n, flow = n, Counts("tile", "sum", "step"), crowd
                experts(1, n)
                n, flow = n_main, main
            layer_norm(3, experts=True)

            with vec.Fori(0, LAYERS) as l:
                n.enter(l, tile=LAYER_TURN["tile"], sum=LAYER_TURN["sum"], std=2 * 4 + 1, square=4, acted=FT,
                        flog=1, dexp=ML_H, lin=FT, rot=2, step=VEC_STEPS)
                nc.vector.memset(conv[:, :, 0:PAD], 0.0)
                nc.vector.memset(conv[:, :, PAD + S:], 0.0)
                nc.vector.memset(at_v[:, :, :, AT_D:VA], 1.0)
                nc.vector.memset(ml_v[:, :, :, ML_D:VM], 1.0)
                nc.vector.tensor_copy(parL[:], par[:, bass.ds(l, 1), :].rearrange("p l n -> p (l n)"))
                nc.vector.tensor_copy(gates_wL[:], gates_w[:, bass.ds(l, 1), :].rearrange("p l n -> p (l n)"))
                nc.vector.tensor_copy(gate_biasL[0:ML_H, :], gate_bias[0:ML_H, bass.ds(l, 1), :].rearrange("p l n -> p (l n)"))\
                    .then_inc(lay_ready, 1)

                def layer_gain(at, w):
                    return gain[:, bass.ds(l * GAINS + at, w)]

                def pre_norm():
                    for b in range(TB):
                        vec.wait_ge(std_ready, n["std"].next())
                        step(nc.vector.reciprocal(rstd[:, b:b + 1], std[:, b:b + 1]))
                        ts(y_tok[:, b, :], x_tok[:, b, :], rstd[:, b:b + 1], None, ALU.mult).then_inc(tok_ready, 1)

                def post_norm(at):
                    for b in range(TB):
                        got = [sums[(n["sum"].index + h) % 4] for h in range(2)]
                        n["sum"].more(2)
                        vec.wait_ge(flow.sum_ready, n["sum"].value)
                        vec.wait_ge(square_ready, n["square"].next())
                        nc.vector.tensor_reduce(sq_tot[:, b:b + 1], sq_sum[:, b, :], AX.X, ALU.add).then_inc(var_ready, 1)
                        vec.wait_ge(std_ready, n["std"].next())
                        step(nc.vector.reciprocal(rstd[:, b:b + 1], std[:, b:b + 1]))
                        for h in range(2):
                            stt(y_tok[:, b, h * HALF:(h + 1) * HALF], got[h][:], rstd[:, b:b + 1],
                                layer_gain(at + h * HALF, HALF), ALU.mult, ALU.mult).then_inc(flow.sum_taken, 1)
                        vec.wait_ge(flow.sum_taken, n["sum"].value)
                        tt(x_tok[:, b, :], x_tok[:, b, :], y_tok[:, b, :], ALU.add).then_inc(x_ready, 1)

                pre_norm()
                skip(4)
                hand_over()
                bank = arrived()
                nc.vector.tensor_copy(gate_tok[:].rearrange("p b g -> p (b g)"), bank[:, 0:TB * 16]).then_inc(flow.tile_taken, 1)
                for i in range(2):
                    for b in range(TB):
                        bank = arrived()[:].rearrange("p (h c n) -> p h c n", h=AT_H, c=2)
                        dst = rot[:, i, b, :].rearrange("p (h c n) -> p h c n", h=AT_H, c=2)
                        for t in range(2):
                            tr = rope[:, b, t, :].unsqueeze(1).to_broadcast([P, AT_H, AT_D // 2])
                            for c in range(2):
                                last = tt(rot_tmp[:, t, :, c, :], bank[:, :, c, :], tr, ALU.mult)
                        last.then_inc(flow.tile_taken, 1)
                        vec.wait_ge(flow.tile_taken, n["tile"].value)
                        tt(dst[:, :, 0, :], rot_tmp[:, 0, :, 0, :], rot_tmp[:, 1, :, 1, :], ALU.subtract)
                        last = tt(dst[:, :, 1, :], rot_tmp[:, 0, :, 1, :], rot_tmp[:, 1, :, 0, :], ALU.add)
                        if b == 0:
                            step(last)
                    last.then_inc(rot_ready, 1)
                    vec.wait_ge(rot_ready, n["rot"].next())
                skip(2)
                for j in range(4):
                    vec.wait_ge(flow.tile_taken, n["tile"].next())
                    for t in range(ML_TAPS):
                        for f in (2 * j, 2 * j + 1):
                            w = parL[:, PAR_TAP + f * ML_TAPS + t:PAR_TAP + f * ML_TAPS + t + 1]
                            if t == 0:
                                last = ts(ml_qk[:, f, :], conv[:, f, 0:S], w, None, ALU.mult)
                            else:
                                last = stt(ml_qk[:, f, :], conv[:, f, t:t + S], w, ml_qk[:, f, :], ALU.mult, ALU.add)
                            if t == ML_TAPS - 1:
                                last.then_inc(conv_ready, 1)
                        if t < ML_TAPS - 1:
                            step(last)
                skip(4)
                hand_over()
                li, lf, lw, mx, tmp = [row[0:ML_H, i, :, :] for i in range(5)]
                for kind, dst in ((0, li), (1, lf)):
                    bank = arrived()
                    for d in range(2):
                        last = ts(dst[:, d, :], bank[0:ML_H, d * S:(d + 1) * S],
                                  gate_biasL[0:ML_H, 2 * d + kind:2 * d + kind + 1], None, ALU.add)
                    last.then_inc(flow.tile_taken, 1)
                vec.wait_ge(flow.tile_taken, n["tile"].value)
                stt(tmp, lf, -1.0, lf, ALU.mult, ALU.min).then_inc(forget_in, 1)
                vec.wait_ge(forget_log, n["flog"].next())
                step(stt(lf, lf, 0.0, tmp, ALU.min, ALU.subtract))
                scan = nc.vector.tensor_tensor_scan
                one = ones_row[0:ML_H, :]
                scan(tmp[:, 0, :], one, lf[:, 0, :], 0.0, ALU.mult, ALU.add)
                step(scan(tmp[:, 1, ::-1], one, lf[:, 1, ::-1], 0.0, ALU.mult, ALU.add))
                step(tt(lw, li, tmp, ALU.subtract))
                scan(mx[:, 0, :], lw[:, 0, :], lw[:, 0, :], 0.0, ALU.max, ALU.max)
                step(scan(mx[:, 1, ::-1], lw[:, 1, ::-1], lw[:, 1, ::-1], 0.0, ALU.max, ALU.max))
                stt(tmp, tmp, -1.0, mx, ALU.mult, ALU.subtract).then_inc(rows_ready, 1)
                skip(4)
                hand_over()

                def at_mask(h):
                    bank = arrived()
                    p = at_p[h % 2]
                    stt(p.rearrange("p b s -> p (b s)"), bank[:], AT_D ** -0.5,
                        reach[:].rearrange("p b s -> p (b s)"), ALU.mult, ALU.add).then_inc(flow.tile_taken, 1)
                    vec.wait_ge(flow.tile_taken, n["tile"].value)
                    step(nc.vector.tensor_reduce(neg_max[:, h % 2, :], p, AX.X, ALU.max))
                    ts(neg_max[:, h % 2, :], neg_max[:, h % 2, :], -1.0, None, ALU.mult).then_inc(p_in, 1)

                def at_weight(h):
                    bank = arrived()
                    tt(at_pT[h % 2].rearrange("p b t -> p (b t)"), bank[:], windows[:].rearrange("p b t -> p (b t)"),
                       ALU.mult).then_inc(flow.tile_taken, 1)

                def at_norm(h):
                    got = arrived_sum()[:, 0:TB * VA].rearrange("p (b d) -> p b d", b=TB)
                    step(nc.vector.reciprocal(den[:, 2 + h % 2, :], got[:, :, AT_D]))
                    for b in range(TB):
                        last = ts(o_tok[:, b, h * AT_D:(h + 1) * AT_D], got[:, b, 0:AT_D], den[:, 2 + h % 2, b:b + 1], None, ALU.mult)
                    last.then_inc(flow.sum_taken, 1)

                for s in range(AT_H + 2):
                    if s < AT_H:
                        at_mask(s)
                    if 1 <= s <= AT_H:
                        at_weight(s - 1)
                    if s >= 2:
                        at_norm(s - 2)

                bank = arrived()
                nc.vector.tensor_copy(ml_col[:].rearrange("p k d b h -> p (k d b h)"), bank[:, 0:8 * ML_H])\
                    .then_inc(flow.tile_taken, 1)
                vec.wait_ge(flow.tile_taken, n["tile"].value)

                def ml_decay(h):
                    bank = arrived()
                    e = ml_e[h % 2]
                    for d in range(2):
                        for kb in range(TB):
                            last = ts(e[:, d, kb, :], bank[:, d * S:(d + 1) * S], ml_col[:, 0, d, kb, h:h + 1], 0.0,
                                      ALU.add, ALU.min)
                    last.then_inc(flow.tile_taken, 1)
                    vec.wait_ge(d_exp, n["dexp"].next())
                    flat = e.rearrange("p d s t -> p (d s t)")
                    step(tt(flat, flat, ml_mask[:].rearrange("p d s t -> p (d s t)"), ALU.mult))
                    bank = arrived()
                    both = e.rearrange("p d s t -> p d (s t)")
                    tt(both, both, bank[:].unsqueeze(1).to_broadcast([P, 2, HALF]), ALU.mult).then_inc(flow.tile_taken, 1)

                def ml_norm(h):
                    for d in range(2):
                        got = arrived_sum()[:, 0:TB * VM].rearrange("p (b d) -> p b d", b=TB)
                        step(nc.vector.tensor_copy(den[:, d, :], got[:, :, ML_D]))
                        step(stt(den[:, d, :], den[:, d, :], -1.0, den[:, d, :], ALU.mult, ALU.max))
                        step(tt(den[:, d, :], den[:, d, :], ml_col[:, 1, d, :, h], ALU.max))
                        step(nc.vector.reciprocal(den[:, d, :], den[:, d, :]))
                        for b in range(TB):
                            o = o_tok[:, b, AT_W + h * ML_D:AT_W + (h + 1) * ML_D]
                            if d == 0:
                                last = ts(o, got[:, b, 0:ML_D], den[:, d, b:b + 1], None, ALU.mult)
                            else:
                                last = stt(o, got[:, b, 0:ML_D], den[:, d, b:b + 1], o, ALU.mult, ALU.add)
                        last.then_inc(flow.sum_taken, 1)
                        vec.wait_ge(flow.sum_taken, n["sum"].value)

                for s in range(ML_H + 1):
                    if s < ML_H:
                        ml_decay(s)
                    if s >= 1:
                        ml_norm(s - 1)
                hm = o_tok[:, :, AT_W:]
                sq = y_tok[:, :, 0:ML_W]
                step(tt(sq, hm, hm, ALU.mult))
                nc.vector.tensor_reduce(sq_tot[:].rearrange("p (b h) -> p b h", b=TB),
                                        sq.rearrange("p b (h d) -> p b h d", h=ML_H), AX.X, ALU.add).then_inc(var_ready, 1)
                vec.wait_ge(gains_in, 16 * 3 * LAYERS)
                for b in range(TB):
                    last = tt(ml_o[:, b, :], ml_o[:, b, :], layer_gain(2 * D, ML_W), ALU.mult)
                vec.wait_ge(std_ready, n["std"].next())
                step(nc.vector.reciprocal(rstd[:], std[:]))
                for b in range(TB):
                    last = tt(hm[:, b, :].rearrange("p (h d) -> p h d", h=ML_H),
                              hm[:, b, :].rearrange("p (h d) -> p h d", h=ML_H),
                              rstd[:, b * ML_H:(b + 1) * ML_H].unsqueeze(2).to_broadcast([P, ML_H, ML_D]), ALU.mult)
                step(last)
                tt(hm, hm, ml_o, ALU.mult).then_inc(mixed_ready, 1)
                skip(4)
                post_norm(0)
                pre_norm()
                skip(4)
                hand_over()

                def ffn_taps(j):
                    bank = arrived()
                    vec.wait_ge(lin_ready, n["lin"].next())
                    c = fconv[:, j % 2, :, :]
                    for i in range(2):
                        w = PAR_FTAP + FF_TAPS * (i * FT + j)
                        last = stt(c[:, i, 1:S], bank[:, i * S:i * S + S - 1], parL[:, w:w + 1], c[:, i, 1:S],
                                   ALU.mult, ALU.add)
                    step(last)
                    for i in range(2):
                        w = PAR_FTAP + FF_TAPS * (i * FT + j) + 2
                        last = stt(c[:, i, 0:S - 1], bank[:, i * S + 1:(i + 1) * S], parL[:, w:w + 1], c[:, i, 0:S - 1],
                                   ALU.mult, ALU.add)
                        last.then_inc(gtap_ready if i == 0 else flow.tile_taken, 1)
                    taken[j] = n["tile"].value

                def ffn_mul(j):
                    vec.wait_ge(acted_ready, n["acted"].next())
                    vec.wait_ge(flow.tile_taken, taken[j])
                    tt(hT[:, j, :], acted[:, j % 2, 0:S], fconv[:, j % 2, 1, :], ALU.mult).then_inc(h_ready, 1)

                taken = {}
                for s in range(FT + 1):
                    if s < FT:
                        ffn_taps(s)
                    if s >= 1:
                        ffn_mul(s - 1)
                post_norm(D)
            n.leave(LAYERS)


def constants():
    f32 = np.float32
    c = {}
    r = np.arange(P)
    c["c_ident"] = np.eye(P, dtype=f32)
    c["c_suffix"] = -np.stack([r[:, None] >= r[None, :], np.ones((P, P), bool)], 1).astype(f32).reshape(P, -1)
    c["c_earlier"] = (r[:, None] < r[None, :]).astype(f32)
    t = np.arange(S, dtype=f32)

    def angles(d, base):
        inv = (1.0 / (base ** (np.arange(0, d, 2, dtype=f32) / f32(d)))).astype(f32)
        return (t[:, None] * inv[None, :]).astype(f32).astype(np.float64)

    ang = angles(AT_D, 10000.0)
    c["c_rope"] = np.stack([np.cos(ang), np.sin(ang)], 1).reshape(TB, P, -1).transpose(1, 0, 2).reshape(P, -1).astype(f32)
    ang = angles(D // RET_H, 10000.0).T
    c["c_ret_rope"] = np.concatenate([np.cos(ang), np.sin(ang)], 1).astype(f32)
    ti, si = np.arange(S)[:, None], np.arange(S)[None, :]
    held = [(np.abs(ti - si) <= w // (2 * d) * d) & ((ti - si) % d == 0) for w, d in ((128, 1), (512, 4), (2048, 16))]
    count = sum(h.astype(f32) for h in held)
    c["c_windows"] = count.reshape(TB, P, S).transpose(1, 0, 2).reshape(P, -1)
    c["c_reach"] = np.where(c["c_windows"] > 0, 0.0, NEG).astype(f32)
    seen = np.stack([si.T <= ti.T, si.T >= ti.T]) * ML_D ** -0.5
    c["c_ml_mask"] = seen.reshape(2, TB, P, S).transpose(2, 0, 1, 3).reshape(P, -1).astype(f32)
    c["c_places"] = np.tile(np.arange(2 * P, dtype=f32), (P, 1))
    c["c_neg_row"] = -np.repeat(np.eye(ML_H, dtype=f32), P, axis=1)
    gamma = 1.0 - 2.0 ** (-5.0 - np.arange(RET_H))
    full = np.where(si.T // CHUNK <= ti.T // CHUNK, gamma[:, None, None] ** np.abs(ti.T - si.T), 0.0)
    full = full * (D // RET_H) ** -0.5
    dec = np.concatenate([full[:, :P, :], full[:, P:, P:]], axis=2)
    c["c_decay"] = dec.transpose(1, 0, 2).reshape(P, -1).astype(f32)
    return {k: np.ascontiguousarray(v) for k, v in c.items()}


def feature_chunks(w):
    return w.reshape(KT, P, -1, 256).transpose(2, 1, 0, 3).reshape(-1, P, SLOT)


def paired_chunks(w):
    lead = w.shape[:-2]
    w = w.reshape(*lead, KT, P, 2, -1, P)
    k = len(lead)
    w = w.transpose(*range(k), k + 3, k + 1, k, k + 2, k + 4)
    return w.reshape(*lead, -1, P, SLOT)


def token_chunks(w):
    return w.reshape(2, KT // 2, P, -1, HALF).transpose(3, 0, 2, 1, 4).reshape(-1, 2, P, SLOT)


def by_partition(w, *lead):
    w = w.reshape(w.shape[0], -1, w.shape[-1] // P, P)
    return w.transpose(3, 0, 2, 1).reshape(P, w.shape[0], -1)


def layout(i):
    o = {name: i[name] for name in ("x", "ret_w_out", "ffn_w_out", "sb_w_out", "moe_w_out", "ln_mix_g", "ln_mix_b",
                                    "ln_ffn_g", "ln_ffn_b", "w_out_2", "w_down_2", "mix_post_g_2", "ffn_post_g_2",
                                    "mlstm_head_g_2")}
    o["ret_qk"] = feature_chunks(i["ret_w_in"][0][:, :2 * D])
    o["ret_vg"] = token_chunks(i["ret_w_in"][0][:, 2 * D:])
    o["ffn_up"] = paired_chunks(i["ffn_w_in"][0])
    o["sb_k"] = feature_chunks(i["sb_w_kv"][:, :D])
    o["sb_v"] = token_chunks(i["sb_w_kv"][:, D:])
    o["sb_q"] = feature_chunks(i["sb_w_q"][0])
    o["moe_up"] = i["moe_w_in"][0].reshape(EXPERTS, 2, KT // 2, P, 2, EG, HALF)\
        .transpose(0, 5, 4, 1, 3, 2, 6).reshape(EXPERTS, -1, P, SLOT)
    o["router_w"] = i["moe_w_router"][0].reshape(KT, P, EXPERTS).transpose(1, 0, 2).reshape(P, -1)
    w = i["w_in_2"]
    a3, m2, m4 = 3 * AT_W, 3 * AT_W + 2 * ML_W, 3 * AT_W + 4 * ML_W
    o["w2_attn"] = np.stack([token_chunks(w[l][:, :a3]) for l in range(LAYERS)])
    o["w2_mqk"] = np.stack([feature_chunks(w[l][:, a3:m2]) for l in range(LAYERS)])
    o["w2_mvo"] = np.stack([token_chunks(w[l][:, m2:m4]) for l in range(LAYERS)])
    o["gates_w"] = w[:, :, m4:].reshape(LAYERS, KT, P, 16).transpose(2, 0, 1, 3).reshape(P, -1)
    o["gate_bias"] = i["mlstm_gate_b_2"].reshape(LAYERS, 4, ML_H).transpose(2, 0, 1).reshape(ML_H, -1)
    o["w2_up"] = paired_chunks(i["w_up_2"])
    o["mix_pre_g"] = by_partition(i["mix_pre_g_2"])
    o["ffn_pre_g"] = by_partition(i["ffn_pre_g_2"])
    o["taps"] = by_partition(i["mlstm_conv_w_2"])
    o["taps_b"] = by_partition(i["mlstm_conv_b_2"])
    o["ffn_taps"] = by_partition(i["ffn_conv_w_2"])
    o["ffn_taps_b"] = by_partition(i["ffn_conv_b_2"])
    return {k: np.ascontiguousarray(v) for k, v in o.items()}


def kernel(**inputs):
    import concourse.bacc as bacc
    from concourse.bass_utils import run_bass_kernel_spmd

    nc = bacc.Bacc("TRN2", target_bir_lowering=False, num_devices=1)
    arrays = layout({k: np.asarray(v) for k, v in inputs.items()}) | constants()
    arrays = {f"in_{k}": v for k, v in arrays.items()}
    aps = {k[3:]: nc.dram_tensor(k, v.shape, mybir.dt.from_np(v.dtype), kind="ExternalInput").ap()
           for k, v in arrays.items()}
    out = nc.dram_tensor("out", (1, S, D), F32, kind="ExternalOutput").ap()
    program(nc, aps, out)
    return run_bass_kernel_spmd(nc, [arrays], core_ids=[0]).results[0]["out"]
```

```python
from contextlib import ExitStack

import numpy as np

import concourse.bass as bass
from concourse import mybir

ACT_STEPS, VEC_STEPS = 5, 107

P = 128
D = 1024
S = 256
TB = S // P
KT = D // P
HALF = 512
F32 = mybir.dt.float32
F32R = mybir.dt.float32r
ALU = mybir.AluOpType
ACT = mybir.ActivationFunctionType
AX = mybir.AxisListType

SLOTS = 6
SLOT = 2048
SPLITS = 3
SPLIT_AT = 1408

RET_H, RET_V = 4, 2048
SB_H = 16
FF = 2816
FT = FF // P
EXPERTS = 8
EF = 3584
ET = EF // P
ALPHA = 4.0 ** 0.25
LN_EPS = 1e-5
LAYERS = 2
AT_H, AT_D, AT_W = 8, 64, 512
ML_H, ML_D, ML_W = 4, 128, 512
ML_TAPS, FF_TAPS = 5, 3
PAD = ML_TAPS // 2
RMS_EPS = 1e-6
NEG = -1e30
CHUNK = 64

RET_ROWS = [2] * (RET_V // P // 2)
MIX_ROWS = [2] * (KT // 2)
FFN_ROWS = [2] * (FT // 2)
EXPERT_ROWS = [2] * (ET // 2)
EG = EF // HALF
CAP = 96
PASSES = -(-S // CAP)
LAYER_ROWS = [2] * (FT // 2)

PAR_MIX_G, PAR_FFN_G, PAR_TAP, PAR_TAP_B = 0, KT, 2 * KT, 2 * KT + 8 * ML_TAPS
PAR_FTAP = PAR_TAP_B + 8
PAR_FTAP_B = PAR_FTAP + 2 * FT * FF_TAPS
PARS = PAR_FTAP_B + 2 * FT
GAINS = 2 * D + ML_W
DECAY = RET_H * 3 * P

EXPERT_CHUNKS = 4 * EG + len(EXPERT_ROWS)
PAIR_TURN = dict(chunk=2 * EXPERT_CHUNKS, tile=2 * (3 * EG + 3), sum=2 * 6)
LAYER_TURN = dict(chunk=9 + 4 + 4 + len(MIX_ROWS) + FT + len(LAYER_ROWS), tile=80, sum=24)
assert all(t["chunk"] % SLOTS == 0 and t["tile"] % 4 == 0 and t["sum"] % 4 == 0
           for t in (PAIR_TURN, LAYER_TURN))


FIRST_CHUNKS = 2 * RET_H + 4 * RET_V // HALF + len(RET_ROWS) + FT + len(FFN_ROWS) + 8 + 4 + len(MIX_ROWS)
FFN_CHUNK = 2 * RET_H + 4 * RET_V // HALF + len(RET_ROWS)
LAYER_FFN_CHUNK = FIRST_CHUNKS + EXPERTS * EXPERT_CHUNKS + 9 + 4 + 4 + len(MIX_ROWS)
MOE_SUMS = 4 + 4 + SB_H // 2 + 4 + EXPERTS // 2 * PAIR_TURN["sum"]


class Count:

    def __init__(self, group=1, unit=1):
        self.index, self.skew, self.group, self.unit = 0, 0, group, unit

    @property
    def value(self):
        return self.skew + self.unit * (self.index // self.group)

    def next(self):
        self.index += 1
        return self.value

    def more(self, count):
        self.index += count

    def enter(self, turn, per_turn):
        self.began, self.before, self.per_turn = self.index, self.skew, per_turn
        self.skew = turn * (per_turn * self.unit // self.group) + self.before

    def leave(self, turns):
        assert self.index - self.began == self.per_turn, (self.index - self.began, self.per_turn)
        self.skew = self.before + (turns - 1) * self.per_turn * self.unit // self.group


class Counts(dict):

    def __init__(self, *names, **made):
        for name in names:
            self[name] = Count()
        self.update(made)

    def enter(self, turn, **per_turn):
        self.inside = per_turn
        for name, events in per_turn.items():
            self[name].enter(turn, events)

    def leave(self, turns):
        for name in self.inside:
            self[name].leave(turns)


class Flow:

    def __init__(self, sem, tag):
        self.landed = [sem(f"{tag}landed{i}") for i in range(SLOTS)]
        self.w_used = sem(tag + "w_used")
        self.tile_ready = sem(tag + "tile_ready")
        self.tile_taken = sem(tag + "tile_taken")
        self.sum_ready = sem(tag + "sum_ready")
        self.sum_taken = sem(tag + "sum_taken")
        self.high_ready = sem(tag + "high_ready")
        self.low_vec = sem(tag + "low_vec")
        self.low_pool = sem(tag + "low_pool")
        self.part_ready = sem(tag + "part_ready")
        self.acted_ready = sem(tag + "acted_ready")
        self.choice_ready = sem(tag + "choice_ready")
        self.vec_step = sem(tag + "vec_step")
        self.act_step = sem(tag + "act_step")


def program(nc, a, out):
    with ExitStack() as ctx:
        def sb(name, *shape):
            return ctx.enter_context(nc.sbuf_tensor(name, [P, *shape], F32))

        def sem(name):
            return ctx.enter_context(nc.semaphore(name))

        ring = sb("ring", SLOTS, SLOT)
        ident = sb("ident", P)
        suffix = sb("suffix", 2, P)
        earlier = sb("earlier", P)
        rope = sb("rope", TB, 2, AT_D // 2)
        reach = sb("reach", TB, S)
        windows = sb("windows", TB, S)
        ml_mask = sb("ml_mask", 2, TB, S)
        neg_row = sb("neg_row", ML_H, P)
        ones_row = sb("ones_row", S)
        x_tok = sb("x_tok", TB, D)
        y_tok = sb("y_tok", TB, D)
        with ExitStack() as shared:
            x_high = shared.enter_context(nc.sbuf_tensor("x_high", [P, KT, S], F32R))
        xT = sb("xT", KT, S)
        gain = sb("gain", 2 * GAINS)
        par = sb("par", LAYERS, PARS)
        parL = sb("parL", PARS)
        gate_bias = sb("gate_bias", LAYERS, 4)
        gate_biasL = sb("gate_biasL", 4)
        router_w = sb("router_w", KT, EXPERTS)
        gates_w = sb("gates_w", LAYERS, KT * 16)
        gates_wL = sb("gates_wL", KT * 16)
        acted = sb("acted", 2, HALF)
        junk = sb("junk", D)
        stats = sb("stats", 4, 2, 6)
        mean_var = sb("mean_var", 4, 2)
        std = sb("std", 8)
        rstd = sb("rstd", 8)
        sq_sum = sb("sq_sum", TB, 2)
        sq_tot = sb("sq_tot", 8)
        eps = sb("eps", 2)
        logits = sb("logits", TB, EXPERTS)
        beaten = sb("beaten", TB, EXPERTS, EXPERTS)
        rank = sb("rank", TB, EXPERTS)
        top = sb("top", TB, 2)
        gate = sb("gate", TB, EXPERTS)
        route = sb("route", 3, TB, PASSES * EXPERTS + 1)
        route_e = sb("route_e", 2, 3 * TB)
        places = sb("places", CAP)
        most = ctx.enter_context(nc.sbuf_tensor("most", [P, 1], mybir.dt.int32))

        with ExitStack() as shared:
            def split(name, *shape):
                return [shared.enter_context(nc.sbuf_tensor(f"{name}_{part}", [P, *shape], F32R)) for part in ("high", "low")]

            w_high, w_low = split("w", SPLITS, SLOT)
            with ExitStack() as hidden:
                hidden.enter_context(nc.sbuf_tensor("hidden_layer", [P, FT, S], F32))
                x_low = hidden.enter_context(nc.sbuf_tensor("x_low", [P, KT, S], F32R))
            chosen_high, chosen_low = split("chosen", 2, KT, CAP)
            e_high, e_low = split("e", ET, CAP)
        headT = sb("headT", 2 * KT, S)
        v_tok = sb("v_tok", TB * RET_V)
        g_tok = sb("g_tok", TB, RET_V)
        hT = sb("hT", ET, S)
        row = sb("row", 5, 2, S)

        hflat = hT[:].rearrange("p k t -> p (k t)")
        gflat = g_tok[:].rearrange("p b n -> p (b n)")
        yflat = y_tok[:].rearrange("p b n -> p (b n)")
        tflat = headT[:].rearrange("p k t -> p (k t)")

        ret_decay = hflat[:, 0:DECAY].rearrange("p (h n) -> p h n", h=RET_H)
        ret_rope = hflat[:, DECAY:DECAY + 2 * S].rearrange("p (i t) -> p i t", i=2)
        ret_p = hflat[:, 2048:2048 + DECAY].rearrange("p (h n) -> p h n", h=RET_H)
        ret_tmp = hflat[:, 4096:4096 + 4 * S].rearrange("p (i t) -> p i t", i=4)
        ret_v = v_tok[:].rearrange("p (b n) -> p b n", b=TB)
        sb_v = v_tok[:, 0:TB * D].rearrange("p (b n) -> p b n", b=TB)
        sb_w, sb_keep, sb_e, sb_size = [hflat[:, i * 1536:(i + 1) * 1536].rearrange("p (i n) -> p i n", i=4)
                                     for i in range(3)] + [gflat[:, 0:1536].rearrange("p (i n) -> p i n", i=4)]
        xflat = xT[:].rearrange("p k t -> p (k t)")
        choice = xflat[:, 0:4 * CAP].rearrange("p (i b j) -> p i b j", i=2, b=TB)
        choiceT = xflat[:, 512:1024].rearrange("p (i b t) -> p i b t", i=2, b=TB)
        h_tok = xflat[:, 1024:2048].rearrange("p (i n) -> p i n", i=2)
        rows_e = junk
        rot = gflat[:, 0:2 * TB * AT_W].rearrange("p (i b n) -> p i b n", i=2, b=TB)
        o_tok = gflat[:, 2 * TB * AT_W:4 * TB * AT_W].rearrange("p (b n) -> p b n", b=TB)
        rot_tmp = yflat[:, 0:2 * AT_W].rearrange("p (i h c n) -> p i h c n", i=2, h=AT_H, c=2)
        at_p = [tflat[:, 2048 + i * 512:2560 + i * 512].rearrange("p (b s) -> p b s", b=TB) for i in range(2)]
        at_pT = [tflat[:, 3072 + i * 512:3584 + i * 512].rearrange("p (b t) -> p b t", b=TB) for i in range(2)]
        VA = AT_D + 1
        at_v = v_tok[:, 0:TB * AT_H * VA].rearrange("p (b h d) -> p b h d", b=TB, h=AT_H)
        V0 = TB * AT_H * VA
        VM = ML_D + 1
        ml_v = v_tok[:, V0:V0 + TB * ML_H * VM].rearrange("p (b h d) -> p b h d", b=TB, h=ML_H)
        V1 = V0 + TB * ML_H * VM
        ml_o = v_tok[:, V1:V1 + TB * ML_W].rearrange("p (b n) -> p b n", b=TB)
        conv = hflat[:, 0:8 * (S + 2 * PAD)].rearrange("p (f t) -> p f t", f=8)
        ml_qk = hflat[:, 2080:2080 + 8 * S].rearrange("p (f t) -> p f t", f=8)
        ml_e = [hflat[:, c:c + 4 * S].rearrange("p (d s t) -> p d s t", d=2, s=TB) for c in (4128, 5152, 0)]
        gate_tok = sb("gate_tok", TB, 16)
        ml_col = sb("ml_col", 2, 2, TB, ML_H)
        neg_max = sb("neg_max", 2, TB)
        den = sb("den", 4, TB)
        fconv = row[:].rearrange("p i c t -> p (i c t)")[:, 6 * S:10 * S].rearrange("p (i c t) -> p i c t", i=2, c=2)

        banks = [ctx.enter_context(nc.psum_tensor(f"bank{i}", [P, HALF], F32)) for i in range(8)]
        sums, tiles = banks[:4], banks[4:]

        main = Flow(sem, "")
        crowd = Flow(sem, "crowd_")
        consts_in = sem("consts_in")
        x_in = sem("x_in")
        gain_in = [sem(f"gain_in{i}") for i in range(2)]
        gains_in = sem("gains_in")
        eps_set = sem("eps_set")
        var_ready = sem("var_ready")
        std_ready = sem("std_ready")
        square_ready = sem("square_ready")
        chosen_ready = sem("chosen_ready")
        most_ready = sem("most_ready")
        x_ready = sem("x_ready")
        tok_ready = sem("tok_ready")
        og_ready = sem("og_ready")
        z_ready = sem("z_ready")
        abs_ready = sem("abs_ready")
        log_ready = sem("log_ready")
        keep_ready = sem("keep_ready")
        wexp_ready = sem("wexp_ready")
        w_ready = sem("w_ready")
        gexp_in = sem("gexp_in")
        gexp_ready = sem("gexp_ready")
        lay_ready = sem("lay_ready")
        rot_ready = sem("rot_ready")
        conv_ready = sem("conv_ready")
        mqk_ready = sem("mqk_ready")
        forget_in = sem("forget_in")
        forget_log = sem("forget_log")
        rows_ready = sem("rows_ready")
        floor_ready = sem("floor_ready")
        p_in = sem("p_in")
        p_exp = sem("p_exp")
        d_exp = sem("d_exp")
        mixed_ready = sem("mixed_ready")
        lin_ready = sem("lin_ready")
        gtap_ready = sem("gtap_ready")
        h_ready = sem("h_ready")
        out_done = sem("out_done")

        block = ctx.enter_context(nc.Block())

        @block.sync
        def _(sp):
            n, flow = Counts("chunk"), main

            def load(src, kt=None, cols=SLOT, in_loop=False, split=False):
                i = n["chunk"].index
                if split:
                    sp.wait_ge(flow.low_vec, n["chunk"].value - FIRST_CHUNKS - SLOTS + 1 + FT)
                    sp.wait_ge(flow.low_pool, n["chunk"].value - FIRST_CHUNKS - SLOTS + 1 + FT)
                    if in_loop:
                        sp.nop(nofuse=True)
                elif i >= SLOTS:
                    sp.wait_ge(flow.w_used, n["chunk"].value - SLOTS + 2)
                    if in_loop:
                        sp.nop(nofuse=True)
                dst = ring[:, i % SLOTS, 0:cols]
                if kt:
                    dst = ring[:, i % SLOTS, 0:kt * D].rearrange("p (k n) -> p k n", k=kt)
                sp.dma_start(dst, src).then_inc(flow.landed[i % SLOTS], 16)
                n["chunk"].next()

            def load_rows(w, kts, **kw):
                k = 0
                for kt in kts:
                    load(w[k * P:(k + kt) * P, :].rearrange("(k p) n -> p k n", p=P), kt=kt, **kw)
                    k += kt

            sp.dma_start(ident[:], a["c_ident"]).then_inc(x_in, 16)
            for b in range(TB):
                sp.dma_start(x_tok[:, b, :], a["x"][0, b * P:(b + 1) * P, :]).then_inc(x_in, 16)
            for h in range(2 * RET_H):
                load(a["ret_qk"][h])
            for g in range(2 * RET_V // HALF):
                for part in range(2):
                    load(a["ret_vg"][g, part])
            load_rows(a["ret_w_out"][0], RET_ROWS)
            for j in range(FT):
                load(a["ffn_up"][j])
            load_rows(a["ffn_w_out"][0], FFN_ROWS)
            for name in ("sb_k", "sb_q"):
                for j in range(4):
                    load(a[name][j])
            for g in range(2):
                for part in range(2):
                    load(a["sb_v"][g, part])
            load_rows(a["sb_w_out"][0], MIX_ROWS)

            def pair_chunks(turn, first, last, **kw):
                for c in range(first, last):
                    e, c = 2 * turn + c // EXPERT_CHUNKS, c % EXPERT_CHUNKS
                    if c < 4 * EG:
                        load(a["moe_up"][bass.ds(e, 1), c].rearrange("a p n -> (a p) n"), **kw)
                    else:
                        r = (c - 4 * EG) * 2 * P
                        load(a["moe_w_out"][0, bass.ds(e, 1), r:r + 2 * P, :].rearrange("a (k p) n -> (a p) k n", p=P),
                             kt=2, **kw)

            pair_chunks(0, 0, SLOTS)
            with sp.Fori(0, EXPERTS // 2 - 1) as turn:
                n.enter(turn, chunk=PAIR_TURN["chunk"])
                pair_chunks(turn, SLOTS, PAIR_TURN["chunk"], in_loop=True, split=True)
                pair_chunks(turn + 1, 0, SLOTS, in_loop=True, split=True)
            n.leave(EXPERTS // 2 - 1)
            pair_chunks(EXPERTS // 2 - 1, SLOTS, PAIR_TURN["chunk"], split=True)

            sp.wait_ge(most_ready, 1)
            with sp.If(sp.value_load(most[0:1, 0:1], min_val=0, max_val=S) > CAP):
                sp.wait_ge(main.sum_ready, MOE_SUMS)
                n_main, n, flow = n, Counts("chunk"), crowd
                with sp.Fori(0, PASSES - 1) as again:
                    with sp.Fori(0, EXPERTS // 2) as turn:
                        n.enter(again * (EXPERTS // 2) + turn, chunk=PAIR_TURN["chunk"])
                        pair_chunks(turn, 0, PAIR_TURN["chunk"], in_loop=True)
                        sp.wait_ge(crowd.sum_ready, (again * (EXPERTS // 2) + turn + 1) * PAIR_TURN["sum"])
                        sp.nop(nofuse=True)
                n, flow = n_main, main

            with sp.Fori(0, LAYERS) as l:
                n.enter(l, chunk=LAYER_TURN["chunk"])
                for g in range(3):
                    w = a["w2_attn"][bass.ds(l, 1), g].rearrange("a c p n -> (a c) p n")
                    load(w[0, :, 0:SLOT // 2], cols=SLOT // 2, in_loop=True)
                    load(w[0, :, SLOT // 2:SLOT], cols=SLOT // 2, in_loop=True)
                    load(w[1], in_loop=True)
                for j in range(4):
                    load(a["w2_mqk"][bass.ds(l, 1), j].rearrange("a p n -> (a p) n"), in_loop=True)
                for g in range(2):
                    for part in range(2):
                        load(a["w2_mvo"][bass.ds(l, 1), g, part].rearrange("a p n -> (a p) n"), in_loop=True)
                load_rows(a["w_out_2"][bass.ds(l, 1)].rearrange("a r n -> (a r) n"), MIX_ROWS, in_loop=True)
                for j in range(FT):
                    load(a["w2_up"][bass.ds(l, 1), j].rearrange("a p n -> (a p) n"), in_loop=True)
                load_rows(a["w_down_2"][bass.ds(l, 1)].rearrange("a r n -> (a r) n"), LAYER_ROWS, in_loop=True)
            n.leave(LAYERS)
            for b in range(TB):
                sp.wait_ge(x_ready, 4 * TB + LAYERS * 2 * TB - TB + b + 1)
                sp.dma_start(out[0, b * P:(b + 1) * P, :], x_tok[:, b, :]).then_inc(out_done, 16)
            sp.wait_ge(out_done, 16 * TB)

        CONSTS = ((ret_rope, "c_ret_rope"), (ret_decay, "c_decay"), (suffix, "c_suffix"), (earlier, "c_earlier"), (rope, "c_rope"),
                  (reach, "c_reach"), (windows, "c_windows"), (ml_mask, "c_ml_mask"), (router_w, "router_w"),
                  (gates_w, "gates_w"), (places, "c_places"))
        PARAMS = ((PAR_MIX_G, PAR_FFN_G, "mix_pre_g"), (PAR_FFN_G, PAR_TAP, "ffn_pre_g"), (PAR_TAP, PAR_TAP_B, "taps"),
                  (PAR_TAP_B, PAR_FTAP, "taps_b"), (PAR_FTAP, PAR_FTAP_B, "ffn_taps"), (PAR_FTAP_B, PARS, "ffn_taps_b"))
        CONSTS_IN = 16 * (len(CONSTS) + len(PARAMS) + 2)

        @block.gpsimd
        def _(pool):
            nc.gpsimd.memset(eps[:, 0:1], LN_EPS)
            nc.gpsimd.memset(eps[:, 1:2], RMS_EPS).then_inc(eps_set, 1)
            nc.gpsimd.memset(ones_row[:], 1.0).then_inc(eps_set, 1)
            for dst, name in CONSTS:
                ap = dst[:] if not isinstance(dst, bass.AP) else dst
                if len(ap.shape) > 2:
                    free = "abc"[:len(ap.shape) - 1]
                    ap = ap.rearrange(f"p {' '.join(free)} -> p ({' '.join(free)})")
                pool.dma_start(ap, a[name]).then_inc(consts_in, 16)
            for c0, c1, name in PARAMS:
                pool.dma_start(par[:, :, c0:c1], a[name]).then_inc(consts_in, 16)
            pool.dma_start(neg_row[0:ML_H, :, :].rearrange("p a b -> p (a b)"), a["c_neg_row"]).then_inc(consts_in, 16)
            pool.dma_start(gate_bias[0:ML_H, :, :].rearrange("p a b -> p (a b)"), a["gate_bias"]).then_inc(consts_in, 16)

            def low_part(flow, count, i, j):
                pool.wait_ge(flow.high_ready, count)
                nc.gpsimd.tensor_tensor(w_low[:, j, SPLIT_AT:], ring[:, i, SPLIT_AT:],
                                        w_high[:, j, SPLIT_AT:].bitcast(F32), ALU.subtract).then_inc(flow.low_pool, 1)

            for k, (g, b_) in enumerate((("ln_mix_g", "ln_mix_b"), ("ln_ffn_g", "ln_ffn_b")) * 2):
                if k == 2:
                    for j in range(FT):
                        low_part(main, j + 1, (FFN_CHUNK + j) % SLOTS, j % SPLITS)
                if k >= 2:
                    pool.wait_ge(x_ready, TB * (k - 1))
                for i, name in enumerate((g, b_)):
                    at = (k % 2) * 2 * D + i * D
                    pool.dma_start(gain[:, at:at + D], a[name][k // 2].partition_broadcast(P))\
                        .then_inc(gain_in[k % 2], 16)

            def low_parts(flow, experts, before):
                with pool.Fori(0, experts * EXPERT_CHUNKS // SLOTS) as turn:
                    for j in range(SLOTS):
                        low_part(flow, turn * SLOTS + before + j + 1, (FIRST_CHUNKS + j) % SLOTS if flow is main else j, j % SPLITS)

            low_parts(main, EXPERTS, FT)
            pool.wait_ge(most_ready, 1)
            with pool.If(pool.value_load(most[0:1, 0:1], min_val=0, max_val=S) > CAP):
                low_parts(crowd, (PASSES - 1) * EXPERTS, 0)

            pool.wait_ge(x_ready, TB * 4)
            for l in range(LAYERS):
                for at, name, w in ((0, "mix_post_g_2", D), (D, "ffn_post_g_2", D), (2 * D, "mlstm_head_g_2", ML_W)):
                    pool.dma_start(gain[:, l * GAINS + at:l * GAINS + at + w],
                                   a[name][l].partition_broadcast(P)).then_inc(gains_in, 16)
            with pool.Fori(0, LAYERS) as l:
                for j in range(FT):
                    low_part(main, l * FT + FT + EXPERTS * EXPERT_CHUNKS + j + 1, (LAYER_FFN_CHUNK + j) % SLOTS, j % SPLITS)

        @block.tensor
        def _(pe):
            n = Counts("tile", "sum", "chunk", "x", "tok", "og", "z", "keep", "w", "lay", "rot", "mqk",
                       "rows", "floor", "pexp", "mixed", "h", "choice", "split", land=Count(SLOTS, 16))
            flow = main
            fresh = [False]

            def slot():
                i = n["chunk"].index
                pe.wait_ge(flow.landed[i % SLOTS], n["land"].value + 16)
                fresh[0] = True
                n["chunk"].next(), n["land"].next()
                return ring[:, i % SLOTS, :]

            def mm(*args, **kw):
                ins = nc.tensor.matmul(*args, **kw)
                if fresh[0]:
                    ins.then_inc(flow.w_used, 1)
                    fresh[0] = False
                return ins

            def open_tile():
                return open_tiles(1)[0]

            def open_tiles(count):
                i = n["tile"].index
                n["tile"].more(count)
                if i + count > 4:
                    pe.wait_ge(flow.tile_taken, n["tile"].value - 4)
                return [tiles[(i + k) % 4] for k in range(count)]

            def open_sum():
                return open_sums(1)[0]

            def open_sums(count):
                i = n["sum"].index
                n["sum"].more(count)
                if i + count > 4:
                    pe.wait_ge(flow.sum_taken, n["sum"].value - 4)
                return [sums[(i + k) % 4] for k in range(count)]

            def all_taken():
                pe.wait_ge(flow.tile_taken, n["tile"].value)

            def transposes(block_of, count):
                for j in range(count // 2):
                    bank = open_tile()
                    for i in range(2):
                        for b in range(TB):
                            last = nc.tensor.transpose(bank[:, i * S + b * P:i * S + (b + 1) * P],
                                                       block_of(b, 2 * j + i), ident[:])
                    last.then_inc(flow.tile_ready, 1)

            def row_transposes(t, ready, count):
                four = open_tiles(4)
                for b in range(TB):
                    pe.wait_ge(ready, count.next())
                    for d in range(KT):
                        o = (d % 2) * S + b * P
                        last = nc.tensor.transpose(four[d // 2][:, o:o + P], t[:, b, d * P:(d + 1) * P], ident[:])
                        if b == TB - 1 and d % 2:
                            last.then_inc(flow.tile_ready, 1)
                all_taken()

            def feature_tile():
                w = slot().rearrange("p (k n) -> p k n", k=KT)
                bank = open_tile()
                for i in range(2):
                    for k in range(KT):
                        last = mm(bank[:, i * S:(i + 1) * S], w[:, k, i * P:(i + 1) * P], xT[:, k, :],
                                  start=(k == 0), stop=(k == KT - 1))
                last.then_inc(flow.tile_ready, 1)

            def token_tiles(kts=(4, 4)):
                pair = open_tiles(TB)
                k = 0
                for kt in kts:
                    w = slot()
                    for kk in range(kt):
                        for b in range(TB):
                            last = mm(pair[b][:], xT[:, k, b * P:(b + 1) * P], w[:, kk * HALF:(kk + 1) * HALF],
                                      start=(k == 0), stop=(k == KT - 1))
                            if k == KT - 1:
                                last.then_inc(flow.tile_ready, 1)
                        k += 1

            def down(lhs, kts, ready=None):
                acc = open_sums(4)
                k, total = 0, sum(kts)
                for kt in kts:
                    w = slot()
                    for kk in range(kt):
                        if ready is not None:
                            ready(k)
                        for b in range(TB):
                            for h in range(2):
                                last = mm(acc[2 * b + h][:], lhs(k, b), w[:, kk * D + h * HALF:kk * D + (h + 1) * HALF],
                                          start=(k == 0), stop=(k == total - 1))
                                if k == total - 1:
                                    last.then_inc(flow.sum_ready, 1)
                        k += 1

            def split_slot(j):
                n["chunk"].next(), n["land"].next(), n["split"].next()
                pe.wait_ge(flow.low_vec, n["split"].value)
                pe.wait_ge(flow.low_pool, n["split"].value)
                fresh[0] = True
                return w_high[:, j, :], w_low[:, j, :]

            def split_feature_tile(j):
                wh, wl = [w.rearrange("p (k n) -> p k n", k=KT) for w in split_slot(j)]
                bank = open_tile()
                for i in range(2):
                    o, cols = bank[:, i * S:(i + 1) * S], slice(i * P, (i + 1) * P)
                    for k in range(KT):
                        mm(o, wh[:, k, cols], x_high[:, k, :], start=(k == 0), stop=False)
                        mm(o, wh[:, k, cols], x_low[:, k, :], start=False, stop=False)
                        last = mm(o, wl[:, k, cols], x_high[:, k, :], start=False, stop=(k == KT - 1))
                last.then_inc(flow.tile_ready, 1)

            def x_transposes():
                row_transposes(x_tok, x_ready, n["x"])

            pe.wait_ge(x_in, 16 * (TB + 1))
            transposes(lambda b, d: x_tok[:, b, d * P:(d + 1) * P], KT)
            all_taken()
            for _ in range(2 * RET_H):
                feature_tile()
            for _ in range(2 * RET_V // HALF):
                token_tiles()
            all_taken()
            first = n["tile"].value
            for h in range(RET_H):
                q, k = headT[:, 2 * h:2 * h + 2, :], headT[:, KT + 2 * h:KT + 2 * h + 2, :]
                bank = open_tile()
                for c in range(2):
                    nc.tensor.matmul(bank[:, 0:S], k[:, c, 0:P], q[:, c, :], start=(c == 0), stop=(c == 1))
                for c in range(2):
                    last = nc.tensor.matmul(bank[:, S:S + P], k[:, c, P:S], q[:, c, P:S],
                                            start=(c == 0), stop=(c == 1))
                last.then_inc(flow.tile_ready, 1)
            for h in range(RET_H):
                pe.wait_ge(flow.tile_taken, first + h + 1)
                v = [ret_v[:, b, h * HALF:(h + 1) * HALF] for b in range(TB)]
                bank = open_tile()
                nc.tensor.matmul(bank[:], ret_p[:, h, 0:P], v[0], start=True, stop=True).then_inc(flow.tile_ready, 1)
                bank = open_tile()
                nc.tensor.matmul(bank[:], ret_p[:, h, P:S], v[0], start=True, stop=False)
                nc.tensor.matmul(bank[:], ret_p[:, h, S:S + P], v[1], start=False, stop=True).then_inc(flow.tile_ready, 1)
            n["og"].more(RET_H * TB)
            pe.wait_ge(og_ready, n["og"].value)
            transposes(lambda b, d: g_tok[:, b, d * P:(d + 1) * P], 2 * KT)
            all_taken()
            down(lambda k, b: headT[:, k, b * P:(b + 1) * P], RET_ROWS)
            x_transposes()
            first = n["tile"].value
            for j in range(FT):
                split_feature_tile(j % SPLITS)
            down(lambda k, b: hT[:, k, b * P:(b + 1) * P], FFN_ROWS,
                 lambda k: pe.wait_ge(flow.tile_taken, first + k + 1))
            x_transposes()

            pe.wait_ge(consts_in, CONSTS_IN)
            for _ in range(8):
                feature_tile()
            for _ in range(2):
                token_tiles()
            all_taken()
            opened = {}

            def sb_scores(h):
                po = (h % 2) * 64
                q, k = headT[po:po + 64, KT + h // 2, :], headT[po:po + 64, h // 2, :]
                opened[h] = bank = open_tile()
                nc.tensor.matmul(bank[:, 0:S], k[:, 0:P], q, start=True, stop=False, skip_group_check=True)
                nc.tensor.matmul(bank[:, S:S + P], k[:, P:S], q[:, P:S], start=False, stop=False,
                                 skip_group_check=True).then_inc(z_ready, 1)

            def sb_suffix(h):
                pe.wait_ge(keep_ready, n["keep"].next())
                bank, keep = opened[h], sb_keep[:, h % 4, :]
                nc.tensor.matmul(bank[:, 0:S], suffix[:, 0, :], keep[:, 0:S], start=False, stop=False,
                                 skip_group_check=True)
                nc.tensor.matmul(bank[:, P:S], suffix[:, 1, :], keep[:, S:S + P], start=False, stop=False,
                                 skip_group_check=True)
                nc.tensor.matmul(bank[:, S:S + P], suffix[:, 0, :], keep[:, S:S + P], start=False, stop=True,
                                 skip_group_check=True).then_inc(flow.tile_ready, 1)

            def sb_out(m):
                bank = open_sum()
                for i in range(2):
                    h = 2 * m + i
                    pe.wait_ge(w_ready, n["w"].next())
                    o, w = bank[64 * i:64 * i + 64, 0:S], sb_w[:, h % 4, :]
                    nc.tensor.matmul(o, sb_v[:, 0, h * 64:(h + 1) * 64], w[:, 0:S], start=True, stop=False)
                    last = nc.tensor.matmul(o[:, P:S], sb_v[:, 1, h * 64:(h + 1) * 64], w[:, S:S + P],
                                            start=False, stop=True)
                last.then_inc(flow.sum_ready, 1)

            for s in range(SB_H + 5):
                if s < SB_H:
                    sb_scores(s)
                if s >= 6 and s % 2 == 0:
                    sb_out((s - 6) // 2)
                if 2 <= s <= SB_H + 1:
                    sb_suffix(s - 2)
            pe.wait_ge(flow.sum_taken, n["sum"].value)
            down(lambda k, b: xT[:, k, b * P:(b + 1) * P], MIX_ROWS)
            x_transposes()

            bank = open_tile()
            for b in range(TB):
                for k in range(KT):
                    last = nc.tensor.matmul(bank[:, b * EXPERTS:(b + 1) * EXPERTS], xT[:, k, b * P:(b + 1) * P],
                                            router_w[:, k, :], start=(k == 0), stop=(k == KT - 1))
            last.then_inc(flow.tile_ready, 1)
            pe.wait_ge(chosen_ready, 1)
            bank = open_tile()
            nc.tensor.matmul(bank[:, 0:16], earlier[:], rank[:].rearrange("p b e -> p (b e)"), start=True, stop=True)
            nc.tensor.matmul(bank[:, 16:32], suffix[:, 1, :], rank[:].rearrange("p b e -> p (b e)"),
                             start=True, stop=True).then_inc(flow.tile_ready, 1)

            def gather(i):
                pe.wait_ge(flow.choice_ready, n["choice"].next())
                for half in range(2):
                    bank = open_tile()
                    for q in range(4):
                        f = 4 * half + q
                        for b in range(TB):
                            last = nc.tensor.matmul(bank[:, q * CAP:(q + 1) * CAP], x_tok[:, b, f * P:(f + 1) * P],
                                                    choice[:, i, b, :], start=(b == 0), stop=(b == TB - 1))
                    last.then_inc(flow.tile_ready, 1)
                bank = open_tile()
                for b in range(TB):
                    last = nc.tensor.transpose(bank[0:CAP, b * P:(b + 1) * P], choice[:, i, b, :], ident[:])
                last.then_inc(flow.tile_ready, 1)

            def mm3(o, x_parts, w_parts, cols, start, stop):
                (xh, xl), (wh, wl) = x_parts, [w[:, cols] for w in w_parts]
                mm(o, xh, wh, start=start, stop=False)
                nc.tensor.matmul(o, xh, wl, start=False, stop=False)
                return nc.tensor.matmul(o, xl, wh, start=False, stop=stop)

            def expert(i):
                hidden, turned = {}, {}
                chunks = iter(range(EXPERT_CHUNKS))
                all_taken()

                def turn_over(g):
                    pe.wait_ge(flow.tile_taken, hidden[g])
                    bank = open_tile()
                    for q in range(4):
                        last = nc.tensor.transpose(bank[:, q * CAP:(q + 1) * CAP], h_tok[0:CAP, g % 2, q * P:(q + 1) * P],
                                                   ident[0:CAP, 0:CAP])
                    last.then_inc(flow.tile_ready, 1)
                    turned[g] = n["tile"].value

                for g in range(EG):
                    for _ in range(2):
                        bank = open_tile()
                        for part in range(2):
                            w = split_slot(next(chunks) % SPLITS)
                            for kk in range(4):
                                k = 4 * part + kk
                                last = mm3(bank[0:CAP, :], (chosen_high[:, i, k, :], chosen_low[:, i, k, :]), w,
                                           slice(kk * HALF, (kk + 1) * HALF), k == 0, k == KT - 1)
                        last.then_inc(flow.tile_ready, 1)
                    hidden[g] = n["tile"].value
                    if g:
                        turn_over(g - 1)
                acc = open_sums(2)
                k = 0
                for kt in EXPERT_ROWS:
                    if k == 4 * (EG - 2):
                        turn_over(EG - 1)
                    if k % 4 == 0:
                        pe.wait_ge(flow.tile_taken, turned[k // 4])
                    w = split_slot(next(chunks) % SPLITS)
                    for kk in range(kt):
                        for h in range(2):
                            last = mm3(acc[h][0:CAP, :], (e_high[:, k, :], e_low[:, k, :]), w,
                                       slice(kk * D + h * HALF, kk * D + (h + 1) * HALF), k == 0, k == ET - 1)
                            if k == ET - 1:
                                last.then_inc(flow.sum_ready, 1)
                        k += 1
                down_done = n["sum"].value
                gather(1 - i)
                pe.wait_ge(flow.sum_taken, down_done)
                acc = open_sums(4)
                for b in range(TB):
                    for h in range(2):
                        nc.tensor.matmul(acc[2 * b + h][:], choiceT[0:CAP, i, b, :], rows_e[0:CAP, h * HALF:(h + 1) * HALF],
                                         start=True, stop=True).then_inc(flow.sum_ready, 1)

            assert n["chunk"].value == FIRST_CHUNKS
            gather(0)
            with pe.Fori(0, EXPERTS // 2) as turn:
                n.enter(turn, land=PAIR_TURN["chunk"], split=PAIR_TURN["chunk"], choice=2, **PAIR_TURN)
                expert(0)
                expert(1)
            n.leave(EXPERTS // 2)
            assert n["sum"].value == MOE_SUMS

            pe.wait_ge(most_ready, 1)
            with pe.If(pe.value_load(most[0:1, 0:1], min_val=0, max_val=S) > CAP):
                pe.wait_ge(main.tile_taken, n["tile"].value)
                pe.wait_ge(main.sum_taken, n["sum"].value)
                n_main, n, flow = n, Counts("tile", "sum", "chunk", "choice", "split", land=Count(SLOTS, 16)), crowd
                gather(0)
                with pe.Fori(0, (PASSES - 1) * EXPERTS // 2) as turn:
                    n.enter(turn, land=PAIR_TURN["chunk"], split=PAIR_TURN["chunk"], choice=2, **PAIR_TURN)
                    expert(0)
                    expert(1)
                    pe.wait_ge(crowd.sum_taken, n["sum"].value)
                n.leave((PASSES - 1) * EXPERTS // 2)
                pe.wait_ge(crowd.tile_taken, n["tile"].value)
                n, flow = n_main, main

            with pe.Fori(0, LAYERS) as l:
                n.enter(l, land=LAYER_TURN["chunk"], tok=4, lay=1, rot=2, mqk=8, rows=1, floor=1, pexp=AT_H,
                        mixed=1, h=FT, split=FT, **LAYER_TURN)
                pe.wait_ge(lay_ready, n["lay"].next())

                def y_transposes():
                    row_transposes(y_tok, tok_ready, n["tok"])

                y_transposes()
                bank = open_tile()
                for b in range(TB):
                    for k in range(KT):
                        last = nc.tensor.matmul(bank[:, b * 16:(b + 1) * 16], xT[:, k, b * P:(b + 1) * P],
                                                gates_wL[:, k * 16:(k + 1) * 16], start=(k == 0), stop=(k == KT - 1))
                last.then_inc(flow.tile_ready, 1)
                for _ in range(3):
                    token_tiles((2, 2, 4))
                for _ in range(4):
                    feature_tile()
                for _ in range(2):
                    token_tiles()
                for i in range(2):
                    pe.wait_ge(rot_ready, n["rot"].next())
                    transposes(lambda b, d: rot[:, i, b, d * P:(d + 1) * P], AT_W // P)
                all_taken()
                for kind in range(2):
                    bank = open_tile()
                    pe.nop(nofuse=True)
                    for d in range(2):
                        for b in range(TB):
                            c = (2 * d + kind) * ML_H
                            last = nc.tensor.transpose(bank[0:ML_H, d * S + b * P:d * S + (b + 1) * P],
                                                       gate_tok[:, b, c:c + ML_H], ident[:])
                    last.then_inc(flow.tile_ready, 1)
                turned = {}

                def at_scores(h):
                    po = (h % 2) * 64
                    q, k = headT[po:po + 64, h // 2, :], headT[po:po + 64, 4 + h // 2, :]
                    bank = open_tile()
                    for b in range(TB):
                        last = nc.tensor.matmul(bank[:, b * S:(b + 1) * S], q[:, b * P:(b + 1) * P], k,
                                                start=True, stop=True)
                    last.then_inc(flow.tile_ready, 1)

                def at_turn(h):
                    pe.wait_ge(p_exp, n["pexp"].next())
                    bank = open_tile()
                    for kb in range(TB):
                        for b in range(TB):
                            last = nc.tensor.transpose(bank[:, kb * S + b * P:kb * S + (b + 1) * P],
                                                       at_p[h % 2][:, b, kb * P:(kb + 1) * P], ident[:])
                    last.then_inc(flow.tile_ready, 1)
                    turned[h] = n["tile"].value

                def at_out(h):
                    pe.wait_ge(flow.tile_taken, turned[h])
                    bank = open_sum()
                    for b in range(TB):
                        for kb in range(TB):
                            last = nc.tensor.matmul(bank[:, b * VA:(b + 1) * VA], at_pT[h % 2][:, kb, b * P:(b + 1) * P],
                                                    at_v[:, kb, h, :], start=(kb == 0), stop=(kb == 1))
                    last.then_inc(flow.sum_ready, 1)

                for s in range(AT_H + 2):
                    if s < AT_H:
                        at_scores(s)
                    if 1 <= s <= AT_H:
                        at_turn(s - 1)
                    if s >= 2:
                        at_out(s - 2)

                pe.wait_ge(rows_ready, n["rows"].next())
                pe.wait_ge(floor_ready, n["floor"].next())
                bank = open_tile()
                pe.nop(nofuse=True)
                for kind, r in enumerate((2, 4)):
                    for d in range(2):
                        for b in range(TB):
                            c = ((kind * 2 + d) * TB + b) * ML_H
                            last = nc.tensor.transpose(bank[:, c:c + ML_H], row[0:ML_H, r, d, b * P:(b + 1) * P],
                                                       ident[0:ML_H, 0:ML_H])
                last.then_inc(flow.tile_ready, 1)
                n["mqk"].more(8)
                pe.wait_ge(mqk_ready, n["mqk"].value)
                decayed = {}

                def ml_maxima(h):
                    bank = open_tile()
                    nc.tensor.matmul(bank[:], neg_row[0:ML_H, h, :], row[0:ML_H, 3, :, :].rearrange("p d t -> p (d t)"),
                                     start=True, stop=True).then_inc(flow.tile_ready, 1)

                def ml_scores(h):
                    bank = open_tile()
                    for kb in range(TB):
                        last = nc.tensor.matmul(bank[:, kb * S:(kb + 1) * S], ml_qk[:, ML_H + h, kb * P:(kb + 1) * P],
                                                ml_qk[:, h, :], start=True, stop=True)
                    last.then_inc(flow.tile_ready, 1)
                    decayed[h] = n["tile"].value

                def ml_out(h):
                    pe.wait_ge(flow.tile_taken, decayed[h])
                    for d in range(2):
                        bank = open_sum()
                        for b in range(TB):
                            seen = range(0, b + 1) if d == 0 else range(b, TB)
                            for i, kb in enumerate(seen):
                                last = nc.tensor.matmul(bank[:, b * VM:(b + 1) * VM], ml_e[h % 3][:, d, kb, b * P:(b + 1) * P],
                                                        ml_v[:, kb, h, :], start=(i == 0), stop=(i == len(seen) - 1))
                        last.then_inc(flow.sum_ready, 1)

                ml_maxima(0)
                for s in range(ML_H + 1):
                    if s + 1 < ML_H:
                        ml_maxima(s + 1)
                    if s < ML_H:
                        ml_scores(s)
                    if s >= 1:
                        ml_out(s - 1)
                pe.wait_ge(mixed_ready, n["mixed"].next())
                transposes(lambda b, d: o_tok[:, b, d * P:(d + 1) * P], KT)
                all_taken()
                down(lambda k, b: headT[:, k, b * P:(b + 1) * P], MIX_ROWS)
                y_transposes()
                for j in range(FT):
                    split_feature_tile(j % SPLITS)
                down(lambda k, b: hT[:, k, b * P:(b + 1) * P], LAYER_ROWS,
                     lambda k: pe.wait_ge(h_ready, n["h"].next()))
            n.leave(LAYERS)

        @block.scalar
        def _(act):
            n = Counts("tile", "sum", "step", "var", "x", "tok", "abs", "gexp", "lay", "conv", "forget",
                       "rows", "pin", "gtap", "h", "chunk", land=Count(SLOTS, 16))
            flow = main

            def step(ins):
                ins.then_inc(flow.act_step, 1)
                act.wait_ge(flow.act_step, n["step"].next())

            def arrived():
                i = n["tile"].index
                act.wait_ge(flow.tile_ready, n["tile"].next())
                return tiles[i % 4]

            def hand_over():
                act.wait_ge(flow.tile_taken, n["tile"].value)

            def copy_tiles(dst, count, func=ACT.Copy, scale=1.0):
                for j in range(count):
                    bank = arrived()
                    nc.scalar.activation(dst(j), bank[:], func, scale=scale).then_inc(flow.tile_taken, 1)

            def pair(t):
                return lambda j: t[:, 2 * j:2 * j + 2, :].rearrange("p k t -> p (k t)")

            def layer_norm_roots():
                act.preload_act_table(ACT.Sqrt)
                for b in range(TB):
                    act.wait_ge(var_ready, n["var"].next())
                    nc.scalar.activation(std[:, b:b + 1], mean_var[:, b, 1:2], ACT.Sqrt,
                                         bias=eps[:, 0:1]).then_inc(std_ready, 1)

            def high_part(j, reused=True):
                i = n["chunk"].index
                act.wait_ge(flow.landed[i % SLOTS], n["land"].value + 16)
                if reused:
                    act.wait_ge(flow.w_used, n["chunk"].value - SPLITS + 2)
                nc.scalar.activation(w_high[:, j % SPLITS, :], ring[:, i % SLOTS, :], ACT.Copy).then_inc(flow.high_ready, 1)
                pass_chunks(1)

            def pass_chunks(count):
                n["chunk"].more(count), n["land"].more(count)

            def high_tiles():
                for j in range(4):
                    bank = arrived()
                    nc.scalar.activation(x_high[:, 2 * j:2 * j + 2, :].rearrange("p k t -> p (k t)"), bank[:], ACT.Copy)\
                        .then_inc(flow.part_ready, 1)

            def silu_tiles(count):
                for j in range(count):
                    if j + 2 < count:
                        high_part(j + 2, j + 2 >= SPLITS)
                    bank = arrived()
                    act.wait_ge(flow.tile_taken, n["tile"].value - 2)
                    nc.scalar.activation(acted[:, j % 2, 0:S], bank[:, 0:S], ACT.Silu).then_inc(flow.acted_ready, 1)

            act.wait_ge(eps_set, 2)
            copy_tiles(pair(xT), 4)
            for _ in range(2 * RET_H):
                n["tile"].next()
            hand_over()
            copy_tiles(lambda j: ret_v[:, j % 2, (j // 2) * HALF:(j // 2 + 1) * HALF], 8)
            copy_tiles(lambda j: g_tok[:, j % 2, (j // 2) * HALF:(j // 2 + 1) * HALF], 8, ACT.Silu)
            for _ in range(RET_H):
                n["tile"].next()
            for g in range(RET_H * TB // 4):
                for i in range(4):
                    n["tile"].next()
                    act.wait_ge(var_ready, n["var"].next())
                    nc.scalar.activation(std[:, 4 + i:5 + i], mean_var[:, i, 1:2], ACT.Sqrt,
                                         bias=eps[:, 0:1]).then_inc(std_ready, 1)
            hand_over()
            copy_tiles(pair(headT), 8)
            n["sum"].next(), n["sum"].next(), n["sum"].next(), n["sum"].next()
            layer_norm_roots()
            pass_chunks(FFN_CHUNK)
            high_part(0, False), high_part(1, False)
            high_tiles()
            silu_tiles(FT)
            for _ in range(4):
                n["sum"].next()
            layer_norm_roots()
            hand_over()
            copy_tiles(pair(xT), 4)

            copy_tiles(pair(headT), 4)
            copy_tiles(lambda j: headT[:, KT + 2 * j:KT + 2 * j + 2, :].rearrange("p k t -> p (k t)"), 4,
                       scale=64 ** -0.5)
            copy_tiles(lambda j: sb_v[:, j % 2, (j // 2) * HALF:(j // 2 + 1) * HALF], 4)

            act.preload_act_table_set("natural_log_exp_and_others")

            def sb_log(h):
                act.wait_ge(abs_ready, n["abs"].next())
                e = sb_e[:, h % 4, :]
                step(nc.scalar.activation(e, sb_size[:, h % 4, :], ACT.Exp, scale=-1.0))
                nc.scalar.activation(e, e, ACT.Ln, bias=1.0).then_inc(log_ready, 1)

            def sb_exp(h):
                act.wait_ge(flow.tile_taken, n["tile"].next())
                nc.scalar.activation(sb_w[:, h % 4, :], sb_w[:, h % 4, :], ACT.Exp).then_inc(wexp_ready, 1)

            def sb_take(m):
                i = n["sum"].index
                act.wait_ge(flow.sum_ready, n["sum"].next())
                nc.scalar.activation(xT[:, m, :], sums[i % 4][:, 0:S], ACT.Copy).then_inc(flow.sum_taken, 1)

            for s in range(SB_H + 6):
                if s < SB_H:
                    sb_log(s)
                if 3 <= s <= SB_H + 2:
                    sb_exp(s - 3)
                if s >= 7 and s % 2 == 1:
                    sb_take((s - 7) // 2)
            for _ in range(4):
                n["sum"].next()
            layer_norm_roots()
            hand_over()
            copy_tiles(pair(xT), 4)

            n["tile"].next()
            act.preload_act_table(ACT.Exp)
            act.wait_ge(gexp_in, n["gexp"].next())
            nc.scalar.activation(gate[:].rearrange("p b e -> p (b e)"), gate[:].rearrange("p b e -> p (b e)"),
                                 ACT.Exp).then_inc(gexp_ready, 1)
            n["tile"].next()
            hand_over()

            def gathered(i):
                for j in range(2):
                    bank = arrived()
                    nc.scalar.activation(chosen_high[:, i, 4 * j:4 * j + 4, :].rearrange("p k j -> p (k j)"),
                                         bank[:, 0:4 * CAP], ACT.Copy).then_inc(flow.part_ready, 1)
                bank = arrived()
                act.wait_ge(flow.tile_taken, n["tile"].value - 1)
                nc.scalar.activation(choiceT[0:CAP, i, :, :].rearrange("p b t -> p (b t)"), bank[0:CAP, 0:S], ACT.Copy)\
                    .then_inc(flow.tile_taken, 1)

            def turned_over(g):
                bank = arrived()
                nc.scalar.activation(e_high[:, 4 * g:4 * g + 4, :].rearrange("p k j -> p (k j)"), bank[:, 0:4 * CAP],
                                     ACT.Copy).then_inc(flow.part_ready, 1)

            def expert(i):
                chunks = iter(range(EXPERT_CHUNKS))

                def next_high():
                    high_part(next(chunks), flow is main or n["chunk"].index >= SPLITS)

                for _ in range(3):
                    next_high()
                for g in range(EG):
                    next_high(), next_high()
                    bank = arrived()
                    act.wait_ge(flow.tile_taken, n["tile"].value - 1)
                    nc.scalar.activation(acted[0:CAP, g % 2, :], bank[0:CAP, :], ACT.Silu).then_inc(flow.tile_taken, 1)
                    next_high(), next_high()
                    n["tile"].next()
                    if g:
                        turned_over(g - 1)
                for _ in range(EXPERT_CHUNKS - 4 * EG - 4):
                    next_high()
                turned_over(EG - 1)
                next_high()
                if n["sum"].index:
                    act.wait_ge(flow.sum_taken, n["sum"].value)
                for h in range(2):
                    j = n["sum"].index % 4
                    act.wait_ge(flow.sum_ready, n["sum"].next())
                    nc.scalar.activation(rows_e[0:CAP, h * HALF:(h + 1) * HALF], sums[j][0:CAP, :], ACT.Copy)\
                        .then_inc(flow.sum_taken, 1)
                gathered(1 - i)
                n["sum"].more(4)

            pass_chunks(FIRST_CHUNKS - FFN_CHUNK - FT)
            gathered(0)
            with act.Fori(0, EXPERTS // 2) as turn:
                n.enter(turn, land=PAIR_TURN["chunk"], **PAIR_TURN)
                expert(0)
                expert(1)
            n.leave(EXPERTS // 2)

            act.wait_ge(most_ready, 1)
            with act.If(act.value_load(most[0:1, 0:1], min_val=0, max_val=S) > CAP):
                n_main, n, flow = n, Counts("tile", "sum", "chunk", land=Count(SLOTS, 16)), crowd
                gathered(0)
                with act.Fori(0, (PASSES - 1) * EXPERTS // 2) as turn:
                    n.enter(turn, land=PAIR_TURN["chunk"], **PAIR_TURN)
                    expert(0)
                    expert(1)
                    act.wait_ge(crowd.sum_ready, n["sum"].value)
                n.leave((PASSES - 1) * EXPERTS // 2)
                n, flow = n_main, main
            layer_norm_roots()

            for _ in range(TB * 3):
                n["x"].next()
            with act.Fori(0, LAYERS) as l:
                n.enter(l, land=LAYER_TURN["chunk"], x=4, var=5, lay=1, conv=8, forget=1,
                        rows=1, pin=AT_H, gtap=FT, h=FT, step=ACT_STEPS, **LAYER_TURN)

                def pre_norm_root(b):
                    act.wait_ge(x_ready, n["x"].next())
                    step(nc.scalar.activation(junk[:], x_tok[:, b, :], ACT.Square, accum_out=sq_tot[:, b:b + 1]))
                    nc.scalar.activation(std[:, b:b + 1], sq_tot[:, b:b + 1], ACT.Sqrt, bias=eps[:, 1:2],
                                         scale=1.0 / D).then_inc(std_ready, 1)

                def gained(g0):
                    for j in range(4):
                        bank = arrived()
                        for i in range(2):
                            last = nc.scalar.activation(xT[:, 2 * j + i, :], bank[:, i * S:(i + 1) * S], ACT.Copy,
                                                        scale=parL[:, g0 + 2 * j + i:g0 + 2 * j + i + 1])
                        last.then_inc(flow.tile_taken, 1)

                def post_norm_roots():
                    for b in range(TB):
                        for h in range(2):
                            i = n["sum"].index
                            act.wait_ge(flow.sum_ready, n["sum"].next())
                            last = nc.scalar.activation(junk[:, h * HALF:(h + 1) * HALF], sums[i % 4][:], ACT.Square,
                                                        accum_out=sq_sum[:, b, h:h + 1])
                        last.then_inc(square_ready, 1)
                        act.wait_ge(var_ready, n["var"].next())
                        nc.scalar.activation(std[:, b:b + 1], sq_tot[:, b:b + 1], ACT.Sqrt, bias=eps[:, 1:2],
                                             scale=1.0 / D).then_inc(std_ready, 1)

                act.wait_ge(lay_ready, n["lay"].next())
                for b in range(TB):
                    pre_norm_root(b)
                hand_over()
                gained(PAR_MIX_G)
                for _ in range(5):
                    n["tile"].next()
                hand_over()
                for b in range(TB):
                    bank = arrived()
                    nc.scalar.activation(at_v[:, b, :, 0:AT_D], bank[:].rearrange("p (h d) -> p h d", h=AT_H),
                                         ACT.Copy).then_inc(flow.tile_taken, 1)
                for j in range(4):
                    bank = arrived()
                    nc.scalar.activation(conv[:, 2 * j:2 * j + 2, PAD:PAD + S],
                                         bank[:].rearrange("p (f t) -> p f t", f=2), ACT.Copy).then_inc(flow.tile_taken, 1)
                for b in range(TB):
                    bank = arrived()
                    nc.scalar.activation(ml_v[:, b, :, 0:ML_D], bank[:].rearrange("p (h d) -> p h d", h=ML_H),
                                         ACT.Copy).then_inc(flow.tile_taken, 1)
                copy_tiles(lambda b: ml_o[:, b, :], TB, ACT.Sigmoid)
                copy_tiles(pair(headT), 4)
                for f in range(8):
                    act.wait_ge(conv_ready, n["conv"].next())
                    nc.scalar.activation(ml_qk[:, f, :], ml_qk[:, f, :], ACT.Silu,
                                         bias=parL[:, PAR_TAP_B + f:PAR_TAP_B + f + 1]).then_inc(mqk_ready, 1)
                n["tile"].next(), n["tile"].next()
                act.preload_act_table_set("natural_log_exp_and_others")
                act.wait_ge(forget_in, n["forget"].next())
                r = row[0:ML_H, 4, :, :].rearrange("p d t -> p (d t)")
                step(nc.scalar.activation(r, r, ACT.Exp))
                nc.scalar.activation(r, r, ACT.Ln, bias=1.0).then_inc(forget_log, 1)
                act.wait_ge(rows_ready, n["rows"].next())
                nc.scalar.activation(r, r, ACT.Exp).then_inc(floor_ready, 1)
                for h in range(AT_H):
                    n["tile"].next(), n["tile"].next(), n["sum"].next()
                    act.wait_ge(p_in, n["pin"].next())
                    for b in range(TB):
                        last = nc.scalar.activation(at_p[h % 2][:, b, :], at_p[h % 2][:, b, :], ACT.Exp,
                                                    bias=neg_max[:, h % 2, b:b + 1])
                    last.then_inc(p_exp, 1)
                n["tile"].next()
                for h in range(ML_H):
                    n["tile"].more(1 if h < 2 else 2)
                    act.wait_ge(flow.tile_taken, n["tile"].value)
                    e = ml_e[h % 3].rearrange("p d s t -> p (d s t)")
                    nc.scalar.activation(e, e, ACT.Exp).then_inc(d_exp, 1)
                    n["sum"].more(2)
                n["tile"].more(2)
                act.preload_act_table(ACT.Sqrt)
                act.wait_ge(var_ready, n["var"].next())
                nc.scalar.activation(std[:], sq_tot[:], ACT.Sqrt, bias=eps[:, 1:2], scale=1.0 / ML_D)\
                    .then_inc(std_ready, 1)
                hand_over()
                copy_tiles(pair(headT), 4)
                post_norm_roots()
                for b in range(TB):
                    pre_norm_root(b)
                pass_chunks(LAYER_FFN_CHUNK - FIRST_CHUNKS - EXPERTS * EXPERT_CHUNKS)
                high_part(0, False), high_part(1, False)
                for j in range(4):
                    bank = arrived()
                    for i in range(2):
                        g = PAR_FFN_G + 2 * j + i
                        last = nc.scalar.activation(x_high[:, 2 * j + i, :], bank[:, i * S:(i + 1) * S], ACT.Copy,
                                                    scale=parL[:, g:g + 1])
                    last.then_inc(flow.part_ready, 1)

                def ffn_middle(j):
                    bank = arrived()
                    for i in range(2):
                        f = i * FT + j
                        last = nc.scalar.activation(fconv[:, j % 2, i, :], bank[:, i * S:(i + 1) * S], ACT.Identity,
                                                    bias=parL[:, PAR_FTAP_B + f:PAR_FTAP_B + f + 1],
                                                    scale=parL[:, PAR_FTAP + 3 * f + 1:PAR_FTAP + 3 * f + 2])
                    last.then_inc(lin_ready, 1)

                def ffn_act(j):
                    act.wait_ge(gtap_ready, n["gtap"].next())
                    nc.scalar.activation(acted[:, j % 2, 0:S], fconv[:, j % 2, 0, :], ACT.Gelu_apprx_tanh)\
                        .then_inc(flow.acted_ready, 1)

                for s in range(FT + 1):
                    if s + 2 < FT:
                        high_part(s + 2, s + 2 >= SPLITS)
                    if s < FT:
                        if s >= 2:
                            act.wait_ge(h_ready, n["h"].next())
                        ffn_middle(s)
                    if s >= 1:
                        ffn_act(s - 1)
                n["h"].next(), n["h"].next()
                pass_chunks(len(LAYER_ROWS))
                post_norm_roots()
            n.leave(LAYERS)

        @block.vector
        def _(vec):
            n = Counts("tile", "sum", "step", "std", "acted", "log", "wexp", "square", "gexp",
                       "flog", "dexp", "lin", "rot", "chunk", "split", "part")
            flow = main
            tt, stt, ts = nc.vector.tensor_tensor, nc.vector.scalar_tensor_tensor, nc.vector.tensor_scalar

            def step(ins):
                ins.then_inc(flow.vec_step, 1)
                vec.wait_ge(flow.vec_step, n["step"].next())

            def arrived():
                i = n["tile"].index
                vec.wait_ge(flow.tile_ready, n["tile"].next())
                return tiles[i % 4]

            def arrived_sum():
                i = n["sum"].index
                vec.wait_ge(flow.sum_ready, n["sum"].next())
                return sums[i % 4]

            def hand_over():
                vec.wait_ge(flow.tile_taken, n["tile"].value)

            def skip(count):
                for _ in range(count):
                    n["tile"].next()

            def layer_norm(k, experts=False):
                for b in range(TB):
                    for h in range(2):
                        xs = x_tok[:, b, h * HALF:(h + 1) * HALF]
                        if experts:
                            step(stt(xs, xs, ALPHA, y_tok[:, b, h * HALF:(h + 1) * HALF], ALU.mult, ALU.add))
                        else:
                            bank = arrived_sum()
                            stt(xs, xs, ALPHA, bank[:], ALU.mult, ALU.add).then_inc(flow.sum_taken, 1)
                            vec.wait_ge(flow.sum_taken, n["sum"].value)
                        last = nc.vector.bn_stats(stats[:, b, h, :], xs)
                    step(last)
                    nc.vector.bn_aggr(mean_var[:, b, :], stats[:, b, :, :].rearrange("p h s -> p (h s)"))\
                        .then_inc(var_ready, 1)
                vec.wait_ge(gain_in[k % 2], 32 * (k // 2 + 1))
                g = gain[:, (k % 2) * 2 * D:(k % 2) * 2 * D + D]
                shift = gain[:, (k % 2) * 2 * D + D:(k % 2) * 2 * D + 2 * D]
                vec.wait_ge(var_ready, RET_H * TB + TB * (k + 1))
                for b in range(TB):
                    xs = x_tok[:, b, :]
                    last = stt(xs, xs, mean_var[:, b, 0:1], g, ALU.subtract, ALU.mult)
                step(last)
                for b in range(TB):
                    xs = x_tok[:, b, :]
                    vec.wait_ge(std_ready, n["std"].next())
                    step(nc.vector.reciprocal(rstd[:, b:b + 1], std[:, b:b + 1]))
                    stt(xs, xs, rstd[:, b:b + 1], shift, ALU.mult, ALU.add).then_inc(x_ready, 1)

            def low_part(j):
                i, j = n["chunk"].index % SLOTS, j % SPLITS
                n["chunk"].next()
                vec.wait_ge(flow.high_ready, n["split"].next())
                tt(w_low[:, j, 0:SPLIT_AT], ring[:, i, 0:SPLIT_AT], w_high[:, j, 0:SPLIT_AT].bitcast(F32), ALU.subtract)\
                    .then_inc(flow.low_vec, 1)

            def low_tile(high, low, width):
                bank = arrived()
                vec.wait_ge(flow.part_ready, n["part"].next())
                tt(low.rearrange("p k j -> p (k j)"), bank[:, 0:width],
                   high.bitcast(F32).rearrange("p k j -> p (k j)"), ALU.subtract).then_inc(flow.tile_taken, 1)

            def gated_tiles(count):
                for j in range(count):
                    if j + 2 < count:
                        low_part(j + 2)
                    bank = arrived()
                    vec.wait_ge(flow.acted_ready, n["acted"].next())
                    tt(hT[:, j, :], acted[:, j % 2, 0:S], bank[:, S:2 * S], ALU.mult).then_inc(flow.tile_taken, 1)

            vec.wait_ge(consts_in, CONSTS_IN)
            skip(4)
            hand_over()
            cos = ret_rope[:, 0, :].unsqueeze(1).to_broadcast([P, 2, S])
            sin = ret_rope[:, 1, :].unsqueeze(1).to_broadcast([P, 2, S])
            for h in range(2 * RET_H):
                bank = arrived()[:].rearrange("p (i t) -> p i t", i=2)
                tt(ret_tmp[:, 0:2, :], bank, cos, ALU.mult)
                step(tt(ret_tmp[:, 2:4, :], bank, sin, ALU.mult))
                tt(headT[:, 2 * h, :], ret_tmp[:, 0, :], ret_tmp[:, 3, :], ALU.subtract)
                tt(headT[:, 2 * h + 1, :], ret_tmp[:, 2, :], ret_tmp[:, 1, :], ALU.add).then_inc(flow.tile_taken, 1)
                vec.wait_ge(flow.tile_taken, n["tile"].value)
            skip(16)
            hand_over()
            for h in range(RET_H):
                bank = arrived()
                tt(ret_p[:, h, :], bank[:, 0:3 * P], ret_decay[:, h, :], ALU.mult).then_inc(flow.tile_taken, 1)
            for g in range(RET_H * TB // 4):
                got = []
                for i in range(4):
                    bank = arrived()
                    got.append(bank)
                    step(nc.vector.bn_stats(stats[:, i, 0, :], bank[:]))
                    nc.vector.bn_aggr(mean_var[:, i, :], stats[:, i, 0, :]).then_inc(var_ready, 1)
                for i in range(4):
                    h, b = (4 * g + i) // TB, i % TB
                    o = ret_tmp[:, (i % 2) * 2:(i % 2) * 2 + 2, :].rearrange("p i t -> p (i t)")
                    gs = g_tok[:, b, h * HALF:(h + 1) * HALF]
                    vec.wait_ge(std_ready, n["std"].next())
                    step(nc.vector.reciprocal(rstd[:, i:i + 1], std[:, 4 + i:5 + i]))
                    ts(o, got[i][:], mean_var[:, i, 0:1], rstd[:, i:i + 1], ALU.subtract, ALU.mult)\
                        .then_inc(flow.tile_taken, 1)
                    vec.wait_ge(flow.tile_taken, n["tile"].value - 3 + i)
                    tt(gs, gs, o, ALU.mult).then_inc(og_ready, 1)
            skip(8)
            layer_norm(0)
            n["chunk"].more(FFN_CHUNK)
            low_part(0), low_part(1)
            for j in range(4):
                low_tile(x_high[:, 2 * j:2 * j + 2, :], x_low[:, 2 * j:2 * j + 2, :], HALF)
            gated_tiles(FT)
            layer_norm(1)
            skip(4)

            skip(8 + 4)
            hand_over()
            mask2 = earlier[:].unsqueeze(1).to_broadcast([P, 2, P])
            zs = {}

            def edge(t):
                return t.rearrange("p (i n) -> p i n", i=3)[:, 0:3:2, :]

            def sb_abs(h):
                zs[h] = bank = tiles[(first + h) % 4]
                vec.wait_ge(z_ready, h + 1)
                size = sb_size[:, h % 4, :]
                step(ts(size, bank[:, 0:384], 0.0, None, ALU.min))
                stt(size, bank[:, 0:384], 0.0, size, ALU.max, ALU.subtract).then_inc(abs_ready, 1)

            def sb_soft(h):
                keep = sb_keep[:, h % 4, :]
                vec.wait_ge(log_ready, n["log"].next())
                step(stt(keep, zs[h][:, 0:384], 0.0, sb_e[:, h % 4, :], ALU.max, ALU.add))
                tt(edge(keep), edge(keep), mask2, ALU.mult).then_inc(keep_ready, 1)

            def sb_bound(h):
                bank = arrived()
                ts(sb_w[:, h % 4, :], bank[:, 0:384], 0.0, None, ALU.min).then_inc(flow.tile_taken, 1)

            def sb_mask(h):
                vec.wait_ge(wexp_ready, n["wexp"].next())
                w = sb_w[:, h % 4, :]
                tt(edge(w), edge(w), mask2, ALU.mult).then_inc(w_ready, 1)

            first = n["tile"].index
            for s in range(SB_H + 4):
                if s < SB_H:
                    sb_abs(s)
                if 1 <= s <= SB_H:
                    sb_soft(s - 1)
                if 3 <= s <= SB_H + 2:
                    sb_bound(s - 3)
                if s >= 4:
                    sb_mask(s - 4)
            for _ in range(SB_H // 2):
                n["sum"].next()
            layer_norm(2)
            skip(4)

            hand_over()
            bank = arrived()
            nc.vector.tensor_copy(logits[:].rearrange("p b e -> p (b e)"), bank[:, 0:TB * EXPERTS]).then_inc(flow.tile_taken, 1)
            vec.wait_ge(flow.tile_taken, n["tile"].value)
            for e in range(EXPERTS):
                rival = logits[:, :, e:e + 1]
                tt(beaten[:, :, 0:e + 1, e], logits[:, :, 0:e + 1], rival.to_broadcast([P, TB, e + 1]), ALU.is_lt)
                if e < EXPERTS - 1:
                    tt(beaten[:, :, e + 1:, e], logits[:, :, e + 1:],
                       rival.to_broadcast([P, TB, EXPERTS - 1 - e]), ALU.is_le)
            step(nc.vector.tensor_reduce(top[:, :, 0], logits[:], AX.X, ALU.max))
            step(nc.vector.tensor_reduce(rank[:], beaten[:], AX.X, ALU.add))
            ts(rank[:], rank[:], float(2), None, ALU.is_lt).then_inc(chosen_ready, 1)
            tt(gate[:], logits[:], top[:, :, 0:1].to_broadcast([P, TB, EXPERTS]), ALU.subtract).then_inc(gexp_in, 1)
            nc.vector.memset(y_tok[:].rearrange("p b n -> p (b n)"), 0.0)
            vec.wait_ge(gexp_ready, n["gexp"].next())
            step(tt(gate[:], gate[:], rank[:], ALU.mult))
            step(nc.vector.tensor_reduce(top[:, :, 1], gate[:], AX.X, ALU.add))
            step(nc.vector.reciprocal(top[:, :, 1], top[:, :, 1]))
            step(tt(gate[:], gate[:], top[:, :, 1:2].to_broadcast([P, TB, EXPERTS]), ALU.mult))
            nc.vector.memset(route[:, :, :, PASSES * EXPERTS], 0.0)
            for again in range(PASSES):
                of = slice(again * EXPERTS, (again + 1) * EXPERTS)
                nc.vector.tensor_copy(route[:, 0, :, of], rank[:])
                nc.vector.tensor_copy(route[:, 2, :, of], gate[:])
            bank = arrived()
            nc.vector.tensor_copy(logits[:].rearrange("p b e -> p (b e)"), bank[:, 16:32])
            place = route[:, 1, :, 0:EXPERTS]
            nc.vector.tensor_copy(place, bank[:, 0:16].rearrange("p (b e) -> p b e", b=TB)).then_inc(flow.tile_taken, 1)
            vec.wait_ge(flow.tile_taken, n["tile"].value)
            tt(place[:, 1, :], place[:, 1, :], logits[:, 0, :], ALU.subtract)
            step(tt(logits[:, 0, :], logits[:, 0, :], logits[:, 1, :], ALU.add))
            for again in range(1, PASSES):
                ts(route[:, 1, :, again * EXPERTS:(again + 1) * EXPERTS], place, float(again * CAP), None, ALU.subtract)
            step(nc.vector.tensor_reduce(top[:, 0:1, 0], logits[:, 0, :], AX.X, ALU.min))
            ts(most[:], top[:, 0:1, 0], -1.0, None, ALU.mult).then_inc(most_ready, 1)

            def choose(v, i):
                step(nc.vector.tensor_copy(route_e[:, i, :], route[:, :, :, bass.ds(v, 1)].rearrange("p r b e -> p (r b e)")))
                for b in range(TB):
                    last = ts(choice[:, i, b, :], places[:], route_e[:, i, TB + b:TB + b + 1],
                              route_e[:, i, b:b + 1], ALU.is_equal, ALU.mult)
                last.then_inc(flow.choice_ready, 1)

            def gathered(i):
                for j in range(2):
                    low_tile(chosen_high[:, i, 4 * j:4 * j + 4, :], chosen_low[:, i, 4 * j:4 * j + 4, :], 4 * CAP)
                skip(1)

            def turned_over(g):
                low_tile(e_high[:, 4 * g:4 * g + 4, :], e_low[:, 4 * g:4 * g + 4, :], 4 * CAP)

            def expert(v, i):
                chunks = iter(range(EXPERT_CHUNKS))
                for _ in range(3):
                    low_part(next(chunks))
                for g in range(EG):
                    for _ in range(4):
                        low_part(next(chunks))
                    n["tile"].next()
                    vec.wait_ge(flow.tile_taken, n["tile"].value)
                    bank = arrived()
                    tt(h_tok[0:CAP, g % 2, :], acted[0:CAP, g % 2, :], bank[0:CAP, :], ALU.mult).then_inc(flow.tile_taken, 1)
                    if g:
                        turned_over(g - 1)
                    else:
                        choose(v + 1, 1 - i)
                for _ in range(EXPERT_CHUNKS - 4 * EG - 4):
                    low_part(next(chunks))
                turned_over(EG - 1)
                low_part(next(chunks))
                n["sum"].more(2)
                gathered(1 - i)
                for b in range(TB):
                    for h in range(2):
                        bank = arrived_sum()
                        ys = y_tok[:, b, h * HALF:(h + 1) * HALF]
                        stt(ys, bank[:], route_e[:, i, 2 * TB + b:2 * TB + b + 1], ys, ALU.mult, ALU.add)\
                            .then_inc(flow.sum_taken, 1)
                vec.wait_ge(flow.sum_taken, n["sum"].value)

            def experts(first, turns):
                choose(first, 0)
                gathered(0)
                with vec.Fori(0, turns) as turn:
                    n.enter(turn, split=PAIR_TURN["chunk"], part=2 * (EG + 2), step=2, **PAIR_TURN)
                    expert(2 * turn + first, 0)
                    expert(2 * turn + first + 1, 1)
                n.leave(turns)

            n["chunk"].more(FIRST_CHUNKS - FFN_CHUNK - FT)
            experts(0, EXPERTS // 2)
            with vec.If(vec.value_load(most[0:1, 0:1], min_val=0, max_val=S) > CAP):
                n_main, n, flow = n, Counts("tile", "sum", "step", "chunk", "split", "part"), crowd
                experts(EXPERTS, (PASSES - 1) * EXPERTS // 2)
                n, flow = n_main, main
            layer_norm(3, experts=True)

            with vec.Fori(0, LAYERS) as l:
                n.enter(l, std=2 * 4 + 1, square=4, acted=FT, split=FT, part=4,
                        flog=1, dexp=ML_H, lin=FT, rot=2, step=VEC_STEPS, **LAYER_TURN)
                nc.vector.memset(conv[:, :, 0:PAD], 0.0)
                nc.vector.memset(conv[:, :, PAD + S:], 0.0)
                nc.vector.memset(at_v[:, :, :, AT_D:VA], 1.0)
                nc.vector.memset(ml_v[:, :, :, ML_D:VM], 1.0)
                nc.vector.tensor_copy(parL[:], par[:, bass.ds(l, 1), :].rearrange("p l n -> p (l n)"))
                nc.vector.tensor_copy(gates_wL[:], gates_w[:, bass.ds(l, 1), :].rearrange("p l n -> p (l n)"))
                nc.vector.tensor_copy(gate_biasL[0:ML_H, :], gate_bias[0:ML_H, bass.ds(l, 1), :].rearrange("p l n -> p (l n)"))\
                    .then_inc(lay_ready, 1)

                def layer_gain(at, w):
                    return gain[:, bass.ds(l * GAINS + at, w)]

                def pre_norm():
                    for b in range(TB):
                        vec.wait_ge(std_ready, n["std"].next())
                        step(nc.vector.reciprocal(rstd[:, b:b + 1], std[:, b:b + 1]))
                        ts(y_tok[:, b, :], x_tok[:, b, :], rstd[:, b:b + 1], None, ALU.mult).then_inc(tok_ready, 1)

                def post_norm(at):
                    for b in range(TB):
                        got = [sums[(n["sum"].index + h) % 4] for h in range(2)]
                        n["sum"].more(2)
                        vec.wait_ge(flow.sum_ready, n["sum"].value)
                        vec.wait_ge(square_ready, n["square"].next())
                        nc.vector.tensor_reduce(sq_tot[:, b:b + 1], sq_sum[:, b, :], AX.X, ALU.add).then_inc(var_ready, 1)
                        vec.wait_ge(std_ready, n["std"].next())
                        step(nc.vector.reciprocal(rstd[:, b:b + 1], std[:, b:b + 1]))
                        for h in range(2):
                            stt(y_tok[:, b, h * HALF:(h + 1) * HALF], got[h][:], rstd[:, b:b + 1],
                                layer_gain(at + h * HALF, HALF), ALU.mult, ALU.mult).then_inc(flow.sum_taken, 1)
                        vec.wait_ge(flow.sum_taken, n["sum"].value)
                        tt(x_tok[:, b, :], x_tok[:, b, :], y_tok[:, b, :], ALU.add).then_inc(x_ready, 1)

                pre_norm()
                skip(4)
                hand_over()
                bank = arrived()
                nc.vector.tensor_copy(gate_tok[:].rearrange("p b g -> p (b g)"), bank[:, 0:TB * 16]).then_inc(flow.tile_taken, 1)
                for i in range(2):
                    for b in range(TB):
                        bank = arrived()[:].rearrange("p (h c n) -> p h c n", h=AT_H, c=2)
                        dst = rot[:, i, b, :].rearrange("p (h c n) -> p h c n", h=AT_H, c=2)
                        for t in range(2):
                            tr = rope[:, b, t, :].unsqueeze(1).to_broadcast([P, AT_H, AT_D // 2])
                            for c in range(2):
                                last = tt(rot_tmp[:, t, :, c, :], bank[:, :, c, :], tr, ALU.mult)
                        last.then_inc(flow.tile_taken, 1)
                        vec.wait_ge(flow.tile_taken, n["tile"].value)
                        tt(dst[:, :, 0, :], rot_tmp[:, 0, :, 0, :], rot_tmp[:, 1, :, 1, :], ALU.subtract)
                        last = tt(dst[:, :, 1, :], rot_tmp[:, 0, :, 1, :], rot_tmp[:, 1, :, 0, :], ALU.add)
                        if b == 0:
                            step(last)
                    last.then_inc(rot_ready, 1)
                    vec.wait_ge(rot_ready, n["rot"].next())
                skip(2)
                for j in range(4):
                    vec.wait_ge(flow.tile_taken, n["tile"].next())
                    for t in range(ML_TAPS):
                        for f in (2 * j, 2 * j + 1):
                            w = parL[:, PAR_TAP + f * ML_TAPS + t:PAR_TAP + f * ML_TAPS + t + 1]
                            if t == 0:
                                last = ts(ml_qk[:, f, :], conv[:, f, 0:S], w, None, ALU.mult)
                            else:
                                last = stt(ml_qk[:, f, :], conv[:, f, t:t + S], w, ml_qk[:, f, :], ALU.mult, ALU.add)
                            if t == ML_TAPS - 1:
                                last.then_inc(conv_ready, 1)
                        if t < ML_TAPS - 1:
                            step(last)
                skip(4 + 4)
                hand_over()
                li, lf, lw, mx, tmp = [row[0:ML_H, i, :, :] for i in range(5)]
                for kind, dst in ((0, li), (1, lf)):
                    bank = arrived()
                    for d in range(2):
                        last = ts(dst[:, d, :], bank[0:ML_H, d * S:(d + 1) * S],
                                  gate_biasL[0:ML_H, 2 * d + kind:2 * d + kind + 1], None, ALU.add)
                    last.then_inc(flow.tile_taken, 1)
                vec.wait_ge(flow.tile_taken, n["tile"].value)
                stt(tmp, lf, -1.0, lf, ALU.mult, ALU.min).then_inc(forget_in, 1)
                vec.wait_ge(forget_log, n["flog"].next())
                step(stt(lf, lf, 0.0, tmp, ALU.min, ALU.subtract))
                scan = nc.vector.tensor_tensor_scan
                one = ones_row[0:ML_H, :]
                scan(tmp[:, 0, :], one, lf[:, 0, :], 0.0, ALU.mult, ALU.add)
                step(scan(tmp[:, 1, ::-1], one, lf[:, 1, ::-1], 0.0, ALU.mult, ALU.add))
                step(tt(lw, li, tmp, ALU.subtract))
                scan(mx[:, 0, :], lw[:, 0, :], lw[:, 0, :], 0.0, ALU.max, ALU.max)
                step(scan(mx[:, 1, ::-1], lw[:, 1, ::-1], lw[:, 1, ::-1], 0.0, ALU.max, ALU.max))
                stt(tmp, tmp, -1.0, mx, ALU.mult, ALU.subtract).then_inc(rows_ready, 1)

                def at_mask(h):
                    bank = arrived()
                    p = at_p[h % 2]
                    stt(p.rearrange("p b s -> p (b s)"), bank[:], AT_D ** -0.5,
                        reach[:].rearrange("p b s -> p (b s)"), ALU.mult, ALU.add).then_inc(flow.tile_taken, 1)
                    vec.wait_ge(flow.tile_taken, n["tile"].value)
                    step(nc.vector.tensor_reduce(neg_max[:, h % 2, :], p, AX.X, ALU.max))
                    ts(neg_max[:, h % 2, :], neg_max[:, h % 2, :], -1.0, None, ALU.mult).then_inc(p_in, 1)

                def at_weight(h):
                    bank = arrived()
                    tt(at_pT[h % 2].rearrange("p b t -> p (b t)"), bank[:], windows[:].rearrange("p b t -> p (b t)"),
                       ALU.mult).then_inc(flow.tile_taken, 1)

                def at_norm(h):
                    got = arrived_sum()[:, 0:TB * VA].rearrange("p (b d) -> p b d", b=TB)
                    step(nc.vector.reciprocal(den[:, 2 + h % 2, :], got[:, :, AT_D]))
                    for b in range(TB):
                        last = ts(o_tok[:, b, h * AT_D:(h + 1) * AT_D], got[:, b, 0:AT_D], den[:, 2 + h % 2, b:b + 1], None, ALU.mult)
                    last.then_inc(flow.sum_taken, 1)

                for s in range(AT_H + 2):
                    if s < AT_H:
                        at_mask(s)
                    if 1 <= s <= AT_H:
                        at_weight(s - 1)
                    if s >= 2:
                        at_norm(s - 2)

                bank = arrived()
                nc.vector.tensor_copy(ml_col[:].rearrange("p k d b h -> p (k d b h)"), bank[:, 0:8 * ML_H])\
                    .then_inc(flow.tile_taken, 1)
                vec.wait_ge(flow.tile_taken, n["tile"].value)

                def ml_decay(h):
                    bank = arrived()
                    e = ml_e[h % 3]
                    for d in range(2):
                        for kb in range(TB):
                            last = ts(e[:, d, kb, :], bank[:, d * S:(d + 1) * S], ml_col[:, 0, d, kb, h:h + 1], 0.0,
                                      ALU.add, ALU.min)
                    last.then_inc(flow.tile_taken, 1)

                def ml_weigh(h):
                    e = ml_e[h % 3]
                    vec.wait_ge(d_exp, n["dexp"].next())
                    flat = e.rearrange("p d s t -> p (d s t)")
                    step(tt(flat, flat, ml_mask[:].rearrange("p d s t -> p (d s t)"), ALU.mult))
                    bank = arrived()
                    both = e.rearrange("p d s t -> p d (s t)")
                    tt(both, both, bank[:].unsqueeze(1).to_broadcast([P, 2, HALF]), ALU.mult).then_inc(flow.tile_taken, 1)

                def ml_norm(h):
                    for d in range(2):
                        got = arrived_sum()[:, 0:TB * VM].rearrange("p (b d) -> p b d", b=TB)
                        step(nc.vector.tensor_copy(den[:, d, :], got[:, :, ML_D]))
                        step(stt(den[:, d, :], den[:, d, :], -1.0, den[:, d, :], ALU.mult, ALU.max))
                        step(tt(den[:, d, :], den[:, d, :], ml_col[:, 1, d, :, h], ALU.max))
                        step(nc.vector.reciprocal(den[:, d, :], den[:, d, :]))
                        for b in range(TB):
                            o = o_tok[:, b, AT_W + h * ML_D:AT_W + (h + 1) * ML_D]
                            if d == 0:
                                last = ts(o, got[:, b, 0:ML_D], den[:, d, b:b + 1], None, ALU.mult)
                            else:
                                last = stt(o, got[:, b, 0:ML_D], den[:, d, b:b + 1], o, ALU.mult, ALU.add)
                        last.then_inc(flow.sum_taken, 1)
                        vec.wait_ge(flow.sum_taken, n["sum"].value)

                ml_decay(0)
                for s in range(ML_H + 1):
                    if s + 1 < ML_H:
                        ml_decay(s + 1)
                    if s < ML_H:
                        ml_weigh(s)
                    if s >= 1:
                        ml_norm(s - 1)
                hm = o_tok[:, :, AT_W:]
                sq = y_tok[:, :, 0:ML_W]
                step(tt(sq, hm, hm, ALU.mult))
                nc.vector.tensor_reduce(sq_tot[:].rearrange("p (b h) -> p b h", b=TB),
                                        sq.rearrange("p b (h d) -> p b h d", h=ML_H), AX.X, ALU.add).then_inc(var_ready, 1)
                vec.wait_ge(gains_in, 16 * 3 * LAYERS)
                for b in range(TB):
                    last = tt(ml_o[:, b, :], ml_o[:, b, :], layer_gain(2 * D, ML_W), ALU.mult)
                vec.wait_ge(std_ready, n["std"].next())
                step(nc.vector.reciprocal(rstd[:], std[:]))
                for b in range(TB):
                    last = tt(hm[:, b, :].rearrange("p (h d) -> p h d", h=ML_H),
                              hm[:, b, :].rearrange("p (h d) -> p h d", h=ML_H),
                              rstd[:, b * ML_H:(b + 1) * ML_H].unsqueeze(2).to_broadcast([P, ML_H, ML_D]), ALU.mult)
                step(last)
                tt(hm, hm, ml_o, ALU.mult).then_inc(mixed_ready, 1)
                skip(4)
                post_norm(0)
                pre_norm()
                n["chunk"].more(LAYER_FFN_CHUNK - FIRST_CHUNKS - EXPERTS * EXPERT_CHUNKS)
                low_part(0), low_part(1)
                for j in range(4):
                    bank = arrived()
                    vec.wait_ge(flow.part_ready, n["part"].next())
                    for i in range(2):
                        f = 2 * j + i
                        last = stt(x_low[:, f, :], bank[:, i * S:(i + 1) * S], parL[:, PAR_FFN_G + f:PAR_FFN_G + f + 1],
                                   x_high[:, f, :].bitcast(F32), ALU.mult, ALU.subtract)
                    last.then_inc(flow.tile_taken, 1)

                def ffn_taps(j):
                    bank = arrived()
                    vec.wait_ge(lin_ready, n["lin"].next())
                    c = fconv[:, j % 2, :, :]
                    for i in range(2):
                        w = PAR_FTAP + FF_TAPS * (i * FT + j)
                        last = stt(c[:, i, 1:S], bank[:, i * S:i * S + S - 1], parL[:, w:w + 1], c[:, i, 1:S],
                                   ALU.mult, ALU.add)
                    step(last)
                    for i in range(2):
                        w = PAR_FTAP + FF_TAPS * (i * FT + j) + 2
                        last = stt(c[:, i, 0:S - 1], bank[:, i * S + 1:(i + 1) * S], parL[:, w:w + 1], c[:, i, 0:S - 1],
                                   ALU.mult, ALU.add)
                        last.then_inc(gtap_ready if i == 0 else flow.tile_taken, 1)
                    taken[j] = n["tile"].value

                def ffn_mul(j):
                    vec.wait_ge(flow.acted_ready, n["acted"].next())
                    vec.wait_ge(flow.tile_taken, taken[j])
                    tt(hT[:, j, :], acted[:, j % 2, 0:S], fconv[:, j % 2, 1, :], ALU.mult).then_inc(h_ready, 1)

                taken = {}
                for s in range(FT + 1):
                    if s + 2 < FT:
                        low_part(s + 2)
                    if s < FT:
                        ffn_taps(s)
                    if s >= 1:
                        ffn_mul(s - 1)
                n["chunk"].more(len(LAYER_ROWS))
                post_norm(D)
            n.leave(LAYERS)


def constants():
    f32 = np.float32
    c = {}
    r = np.arange(P)
    c["c_ident"] = np.eye(P, dtype=f32)
    c["c_suffix"] = -np.stack([r[:, None] >= r[None, :], np.ones((P, P), bool)], 1).astype(f32).reshape(P, -1)
    c["c_earlier"] = (r[:, None] < r[None, :]).astype(f32)
    t = np.arange(S, dtype=f32)

    def angles(d, base):
        inv = (1.0 / (base ** (np.arange(0, d, 2, dtype=f32) / f32(d)))).astype(f32)
        return (t[:, None] * inv[None, :]).astype(f32).astype(np.float64)

    ang = angles(AT_D, 10000.0)
    c["c_rope"] = np.stack([np.cos(ang), np.sin(ang)], 1).reshape(TB, P, -1).transpose(1, 0, 2).reshape(P, -1).astype(f32)
    ang = angles(D // RET_H, 10000.0).T
    c["c_ret_rope"] = np.concatenate([np.cos(ang), np.sin(ang)], 1).astype(f32)
    ti, si = np.arange(S)[:, None], np.arange(S)[None, :]
    held = [(np.abs(ti - si) <= w // (2 * d) * d) & ((ti - si) % d == 0) for w, d in ((128, 1), (512, 4), (2048, 16))]
    count = sum(h.astype(f32) for h in held)
    c["c_windows"] = count.reshape(TB, P, S).transpose(1, 0, 2).reshape(P, -1)
    c["c_reach"] = np.where(c["c_windows"] > 0, 0.0, NEG).astype(f32)
    seen = np.stack([si.T <= ti.T, si.T >= ti.T]) * ML_D ** -0.5
    c["c_ml_mask"] = seen.reshape(2, TB, P, S).transpose(2, 0, 1, 3).reshape(P, -1).astype(f32)
    c["c_places"] = np.tile(np.arange(CAP, dtype=f32), (P, 1))
    c["c_neg_row"] = -np.repeat(np.eye(ML_H, dtype=f32), P, axis=1)
    gamma = 1.0 - 2.0 ** (-5.0 - np.arange(RET_H))
    full = np.where(si.T // CHUNK <= ti.T // CHUNK, gamma[:, None, None] ** np.abs(ti.T - si.T), 0.0)
    full = full * (D // RET_H) ** -0.5
    dec = np.concatenate([full[:, :P, :], full[:, P:, P:]], axis=2)
    c["c_decay"] = dec.transpose(1, 0, 2).reshape(P, -1).astype(f32)
    return {k: np.ascontiguousarray(v) for k, v in c.items()}


def feature_chunks(w):
    return w.reshape(KT, P, -1, 256).transpose(2, 1, 0, 3).reshape(-1, P, SLOT)


def paired_chunks(w):
    lead = w.shape[:-2]
    w = w.reshape(*lead, KT, P, 2, -1, P)
    k = len(lead)
    w = w.transpose(*range(k), k + 3, k + 1, k, k + 2, k + 4)
    return w.reshape(*lead, -1, P, SLOT)


def token_chunks(w):
    return w.reshape(2, KT // 2, P, -1, HALF).transpose(3, 0, 2, 1, 4).reshape(-1, 2, P, SLOT)


def by_partition(w, *lead):
    w = w.reshape(w.shape[0], -1, w.shape[-1] // P, P)
    return w.transpose(3, 0, 2, 1).reshape(P, w.shape[0], -1)


def layout(i):
    o = {name: i[name] for name in ("x", "ret_w_out", "ffn_w_out", "sb_w_out", "moe_w_out", "ln_mix_g", "ln_mix_b",
                                    "ln_ffn_g", "ln_ffn_b", "w_out_2", "w_down_2", "mix_post_g_2", "ffn_post_g_2",
                                    "mlstm_head_g_2")}
    o["ret_qk"] = feature_chunks(i["ret_w_in"][0][:, :2 * D])
    o["ret_vg"] = token_chunks(i["ret_w_in"][0][:, 2 * D:])
    o["ffn_up"] = paired_chunks(i["ffn_w_in"][0])
    o["sb_k"] = feature_chunks(i["sb_w_kv"][:, :D])
    o["sb_v"] = token_chunks(i["sb_w_kv"][:, D:])
    o["sb_q"] = feature_chunks(i["sb_w_q"][0])
    o["moe_up"] = i["moe_w_in"][0].reshape(EXPERTS, 2, KT // 2, P, 2, EG, HALF)\
        .transpose(0, 5, 4, 1, 3, 2, 6).reshape(EXPERTS, -1, P, SLOT)
    o["router_w"] = i["moe_w_router"][0].reshape(KT, P, EXPERTS).transpose(1, 0, 2).reshape(P, -1)
    w = i["w_in_2"]
    a3, m2, m4 = 3 * AT_W, 3 * AT_W + 2 * ML_W, 3 * AT_W + 4 * ML_W
    o["w2_attn"] = np.stack([token_chunks(w[l][:, :a3]) for l in range(LAYERS)])
    o["w2_mqk"] = np.stack([feature_chunks(w[l][:, a3:m2]) for l in range(LAYERS)])
    o["w2_mvo"] = np.stack([token_chunks(w[l][:, m2:m4]) for l in range(LAYERS)])
    o["gates_w"] = w[:, :, m4:].reshape(LAYERS, KT, P, 16).transpose(2, 0, 1, 3).reshape(P, -1)
    o["gate_bias"] = i["mlstm_gate_b_2"].reshape(LAYERS, 4, ML_H).transpose(2, 0, 1).reshape(ML_H, -1)
    o["w2_up"] = paired_chunks(i["w_up_2"])
    o["mix_pre_g"] = by_partition(i["mix_pre_g_2"])
    o["ffn_pre_g"] = by_partition(i["ffn_pre_g_2"])
    o["taps"] = by_partition(i["mlstm_conv_w_2"])
    o["taps_b"] = by_partition(i["mlstm_conv_b_2"])
    o["ffn_taps"] = by_partition(i["ffn_conv_w_2"])
    o["ffn_taps_b"] = by_partition(i["ffn_conv_b_2"])
    return {k: np.ascontiguousarray(v) for k, v in o.items()}


def kernel(**inputs):
    import concourse.bacc as bacc
    from concourse.bass_utils import run_bass_kernel_spmd

    nc = bacc.Bacc("TRN2", target_bir_lowering=False, num_devices=1)
    arrays = layout({k: np.asarray(v) for k, v in inputs.items()}) | constants()
    arrays = {f"in_{k}": v for k, v in arrays.items()}
    aps = {k[3:]: nc.dram_tensor(k, v.shape, mybir.dt.from_np(v.dtype), kind="ExternalInput").ap()
           for k, v in arrays.items()}
    out = nc.dram_tensor("out", (1, S, D), F32, kind="ExternalOutput").ap()
    program(nc, aps, out)
    return run_bass_kernel_spmd(nc, [arrays], core_ids=[0]).results[0]["out"]
```
